# Optimizing a Trainium2 kernel written in Bass

```python
import jax, jax.numpy as jnp
from jax import lax
import numpy as np

D_MODEL = 1024
BATCH = 1
SEQ = 256
DEPTH = 1
DEC_BATCH = 1
DEC_SEQ = 512
PAST_LEN = 128

N_META = 16
EPS = 1e-6
D_FF = 2816
SSD_D_INNER = D_MODEL
SSD_HEADDIM = 64
SSD_HEADS = SSD_D_INNER // SSD_HEADDIM
SSD_GROUPS = 4
SSD_STATE = 128
SSD_CONV = 5
SSD_CHUNK = 128
SSD_GN = SSD_GROUPS * SSD_STATE
SSD_CONV_DIM = SSD_D_INNER + 2 * SSD_GN
HG_WIDTH = D_MODEL
HG_HEADDIM = 128
HG_HEADS = HG_WIDTH // HG_HEADDIM
HG_CHUNK = 64
IN_WIDTHS = (SSD_D_INNER, SSD_CONV_DIM, 2 * SSD_HEADS, HG_WIDTH, 2 * HG_WIDTH, HG_WIDTH, HG_WIDTH, 2 * D_MODEL)
IN_COLS = sum(IN_WIDTHS)

kernel_name = 'hybrid_ssd_hgrn2_bidir_encoder'

def _split_points(widths):
    pts, acc = [], 0
    for w in widths[:-1]:
        acc += w
        pts.append(acc)
    return pts

def rmsnorm(x, w):
    xf = x.astype(jnp.float32)
    y = xf * lax.rsqrt(jnp.mean(xf * xf, axis=-1, keepdims=True) + EPS)
    return (y * w.astype(jnp.float32)).astype(x.dtype)

def swiglu(h, w_gate_up, w_down):
    g, u = jnp.split(h @ w_gate_up, 2, axis=-1)
    return (jax.nn.silu(g) * u) @ w_down

def _pad_front(u, n):
    return jnp.pad(u, [(0, 0), (n, 0)] + [(0, 0)] * (u.ndim - 2))

def _flip(u):
    return jnp.flip(u, axis=1)

def depthwise_conv_centred(u, w, bias):
    c = u.shape[-1]
    y = lax.conv_general_dilated(u, w.reshape(SSD_CONV, 1, c), window_strides=(1,),
                                 padding=[(SSD_CONV // 2, SSD_CONV // 2)],
                                 dimension_numbers=('NWC', 'WIO', 'NWC'), feature_group_count=c)
    return y + bias

def ssd_chunked(x, dt, A, Bm, Cm):
    b, T, H, P = x.shape
    G, N = Bm.shape[2], Bm.shape[3]
    Hg = H // G
    Q = SSD_CHUNK
    c = T // Q
    acs = jnp.cumsum((dt * A).reshape(b, c, Q, G, Hg), axis=2)
    xdt = (x * dt[..., None]).reshape(b, c, Q, G, Hg, P)
    Bc = Bm.reshape(b, c, Q, G, N)
    Cc = Cm.reshape(b, c, Q, G, N)
    mask = jnp.tril(jnp.ones((Q, Q), dtype=bool))[:, :, None, None]
    seg = acs[:, :, :, None] - acs[:, :, None, :]
    Lm = jnp.exp(jnp.where(mask, seg, -jnp.inf))
    CB = jnp.einsum('bctgn,bcsgn->bctsg', Cc, Bc)
    y_diag = jnp.einsum('bctsg,bctsgh,bcsghp->bctghp', CB, Lm, xdt)
    decay_to_end = jnp.exp(acs[:, :, -1:] - acs)
    states = jnp.einsum('bcsgn,bcsgh,bcsghp->bcghpn', Bc, decay_to_end, xdt)
    chunk_decay = jnp.exp(acs[:, :, -1])

    def step(h, inp):
        st, dec = inp
        return dec[..., None, None] * h + st, h

    h0 = jnp.zeros((b, G, Hg, P, N), x.dtype)
    _, prev = lax.scan(step, h0, (jnp.moveaxis(states, 1, 0), jnp.moveaxis(chunk_decay, 1, 0)))
    prev = jnp.moveaxis(prev, 0, 1)
    y_off = jnp.einsum('bctgn,bcghpn,bctgh->bctghp', Cc, prev, jnp.exp(acs))
    return (y_diag + y_off).reshape(b, T, H, P)

def hgrn2_chunked(q, k, v, logf):
    b, T, H, K = q.shape
    V = v.shape[-1]
    Q = HG_CHUNK
    c = T // Q
    q = q.reshape(b, c, Q, H, K)
    k = k.reshape(b, c, Q, H, K)
    v = v.reshape(b, c, Q, H, V)
    bcs = jnp.cumsum(logf.reshape(b, c, Q, H, K), axis=2)
    ref = bcs[:, :, Q // 2:Q // 2 + 1]
    qe = q * jnp.exp(bcs - ref)
    ke = k * jnp.exp(ref - bcs)
    mask = jnp.tril(jnp.ones((Q, Q), dtype=bool))
    A = jnp.where(mask, jnp.einsum('bcthk,bcshk->bchts', qe, ke), 0.0)
    o_intra = jnp.einsum('bchts,bcshv->bcthv', A, v)
    kv = jnp.einsum('bcshk,bcshv->bchkv', k * jnp.exp(bcs[:, :, -1:] - bcs), v)
    chunk_decay = jnp.exp(bcs[:, :, -1])

    def step(S, inp):
        upd, dec = inp
        return dec[..., None] * S + upd, S

    S0 = jnp.zeros((b, H, K, V), q.dtype)
    _, prev = lax.scan(step, S0, (jnp.moveaxis(kv, 1, 0), jnp.moveaxis(chunk_decay, 1, 0)))
    prev = jnp.moveaxis(prev, 0, 1)
    o_inter = jnp.einsum('bcthk,bchkv->bcthv', q * jnp.exp(bcs), prev)
    return (o_intra + o_inter).reshape(b, T, H, V)

def ssd_branch(z, xbc, dt_raw, conv_w, conv_b, dt_bias, a_log, d_skip, norm_w):
    f32 = jnp.float32
    b, L, _ = xbc.shape
    xbc = jax.nn.silu(depthwise_conv_centred(xbc.astype(f32), conv_w.astype(f32), conv_b.astype(f32)))
    xs = xbc[..., :SSD_D_INNER].reshape(b, L, SSD_HEADS, SSD_HEADDIM)
    Bm = xbc[..., SSD_D_INNER:SSD_D_INNER + SSD_GN].reshape(b, L, SSD_GROUPS, SSD_STATE)
    Cm = xbc[..., SSD_D_INNER + SSD_GN:].reshape(b, L, SSD_GROUPS, SSD_STATE)
    dt = jax.nn.softplus(dt_raw.astype(f32).reshape(b, L, 2, SSD_HEADS) + dt_bias.astype(f32))
    A = -jnp.exp(a_log.astype(f32))
    npad = SSD_CHUNK - N_META
    xp, Bp, Cp, dtp = (_pad_front(u, npad) for u in (xs, Bm, Cm, dt))
    y_fwd = ssd_chunked(xp, dtp[:, :, 0], A[0], Bp, Cp)
    y_bwd = _flip(ssd_chunked(_flip(xp), _flip(dtp[:, :, 1]), A[1], _flip(Bp), _flip(Cp)))
    y = (y_fwd + y_bwd)[:, npad:] + d_skip.astype(f32)[:, None] * xs
    y = y.reshape(b, L, SSD_D_INNER) * jax.nn.silu(z.astype(f32))
    return rmsnorm(y, norm_w)

def hgrn2_branch(hq, hf, hi, hg, lb, norm_w):
    f32 = jnp.float32
    b, L, _ = hq.shape
    q = jax.nn.silu(hq.astype(f32)).reshape(b, L, HG_HEADS, HG_HEADDIM)
    v = hi.astype(f32).reshape(b, L, HG_HEADS, HG_HEADDIM)
    lbf = lb.astype(f32).reshape(2, HG_HEADS, HG_HEADDIM)
    f = lbf + (1.0 - lbf) * jax.nn.sigmoid(hf.astype(f32).reshape(b, L, 2, HG_HEADS, HG_HEADDIM))
    k = 1.0 - f
    logf = jnp.log(f)
    npad = HG_CHUNK - N_META
    qp, vp, kp, lfp = (_pad_front(u, npad) for u in (q, v, k, logf))
    o_fwd = hgrn2_chunked(qp, kp[:, :, 0], vp, lfp[:, :, 0])
    o_bwd = _flip(hgrn2_chunked(_flip(qp), _flip(kp[:, :, 1]), _flip(vp), _flip(lfp[:, :, 1])))
    o = (o_fwd + o_bwd)[:, npad:]
    o = o * lax.rsqrt(jnp.mean(o * o, axis=-1, keepdims=True) + EPS) * norm_w.astype(f32).reshape(HG_HEADS, HG_HEADDIM)
    return o.reshape(b, L, HG_WIDTH) * jax.nn.silu(hg.astype(f32))

def hybrid_mixer(h, w_in, conv_w, conv_b, dt_bias, a_log, d_skip, ssd_norm, ssd_w_proj,
                 lb, hg_norm, hg_w_proj, w_out):
    proj = h @ w_in
    z, xbc, dt_raw, hq, hf, hi, hg, gates = jnp.split(proj, _split_points(IN_WIDTHS), axis=-1)
    branch_a = ssd_branch(z, xbc, dt_raw, conv_w, conv_b, dt_bias, a_log, d_skip, ssd_norm) @ ssd_w_proj
    branch_b = hgrn2_branch(hq, hf, hi, hg, lb, hg_norm) @ hg_w_proj
    ga, gb = jnp.split(jax.nn.sigmoid(gates.astype(jnp.float32)), 2, axis=-1)
    merged = ga * branch_a + gb * branch_b
    return (merged @ w_out).astype(h.dtype)

def encoder_trunk(x, meta_tokens, ffn1_norm, ffn1_w_gate_up, ffn1_w_down, mix_norm, w_in,
                  ssd_conv_w, ssd_conv_b, ssd_dt_bias, ssd_a_log, ssd_d, ssd_norm, ssd_w_proj,
                  hg_lb_table, hg_norm, hg_w_proj, w_out, ffn2_norm, ffn2_w_gate_up, ffn2_w_down,
                  final_norm):
    b = x.shape[0]
    meta = jnp.broadcast_to(meta_tokens[None].astype(x.dtype), (b, N_META, x.shape[-1]))
    h = jnp.concatenate([meta, x], axis=1)
    lb_all = jnp.cumsum(jax.nn.softmax(hg_lb_table.astype(jnp.float32), axis=1), axis=1)
    for l in range(DEPTH):
        h = h + 0.5 * swiglu(rmsnorm(h, ffn1_norm[l]), ffn1_w_gate_up[l], ffn1_w_down[l])
        h = h + hybrid_mixer(rmsnorm(h, mix_norm[l]), w_in[l], ssd_conv_w[l], ssd_conv_b[l],
                             ssd_dt_bias[l], ssd_a_log[l], ssd_d[l], ssd_norm[l], ssd_w_proj[l],
                             lb_all[:, l], hg_norm[l], hg_w_proj[l], w_out[l])
        h = h + 0.5 * swiglu(rmsnorm(h, ffn2_norm[l]), ffn2_w_gate_up[l], ffn2_w_down[l])
    return rmsnorm(h, final_norm)[:, N_META:]

def setup_inputs(seed: int = 0) -> dict:
    key = jax.random.key(seed)
    ks = jax.random.split(key, 26)
    nrm = lambda k, shape, scale: jax.random.normal(k, shape, jnp.float32) * scale
    gain = lambda k, shape: 1.0 + 0.05 * jax.random.normal(k, shape, jnp.float32)
    dt0 = jnp.exp(jax.random.uniform(ks[0], (DEPTH, 2, SSD_HEADS), jnp.float32, np.log(1e-3), np.log(1e-1)))
    return {
        'x_prompt': nrm(ks[1], (BATCH, SEQ, D_MODEL), 1.0),
        'x_sample': nrm(ks[2], (DEC_BATCH, DEC_SEQ, D_MODEL), 1.0),
        'meta_tokens': nrm(ks[3], (N_META, D_MODEL), 1.0),
        'ffn1_norm': gain(ks[4], (DEPTH, D_MODEL)),
        'ffn1_w_gate_up': nrm(ks[5], (DEPTH, D_MODEL, 2 * D_FF), D_MODEL ** -0.5),
        'ffn1_w_down': nrm(ks[6], (DEPTH, D_FF, D_MODEL), D_FF ** -0.5),
        'mix_norm': gain(ks[7], (DEPTH, D_MODEL)),
        'w_in': nrm(ks[8], (DEPTH, D_MODEL, IN_COLS), D_MODEL ** -0.5),
        'ssd_conv_w': nrm(ks[9], (DEPTH, SSD_CONV, SSD_CONV_DIM), SSD_CONV ** -0.5),
        'ssd_conv_b': nrm(ks[10], (DEPTH, SSD_CONV_DIM), 0.02),
        'ssd_dt_bias': dt0 + jnp.log(-jnp.expm1(-dt0)),
        'ssd_a_log': jnp.log(jax.random.uniform(ks[11], (DEPTH, 2, SSD_HEADS), jnp.float32, 1.0, 16.0)),
        'ssd_d': gain(ks[12], (DEPTH, SSD_HEADS)),
        'ssd_norm': gain(ks[13], (DEPTH, SSD_D_INNER)),
        'ssd_w_proj': nrm(ks[14], (DEPTH, SSD_D_INNER, D_MODEL), SSD_D_INNER ** -0.5),
        'hg_lb_table': nrm(ks[15], (2, DEPTH + 1, HG_WIDTH), 0.1),
        'hg_norm': gain(ks[16], (DEPTH, HG_WIDTH)),
        'hg_w_proj': nrm(ks[17], (DEPTH, HG_WIDTH, D_MODEL), HG_WIDTH ** -0.5),
        'w_out': nrm(ks[18], (DEPTH, D_MODEL, D_MODEL), D_MODEL ** -0.5),
        'ffn2_norm': gain(ks[19], (DEPTH, D_MODEL)),
        'ffn2_w_gate_up': nrm(ks[20], (DEPTH, D_MODEL, 2 * D_FF), D_MODEL ** -0.5),
        'ffn2_w_down': nrm(ks[21], (DEPTH, D_FF, D_MODEL), D_FF ** -0.5),
        'final_norm': gain(ks[22], (D_MODEL,)),
    }

def reference(x_prompt, x_sample, meta_tokens, ffn1_norm, ffn1_w_gate_up, ffn1_w_down, mix_norm, w_in,
              ssd_conv_w, ssd_conv_b, ssd_dt_bias, ssd_a_log, ssd_d, ssd_norm, ssd_w_proj,
              hg_lb_table, hg_norm, hg_w_proj, w_out, ffn2_norm, ffn2_w_gate_up, ffn2_w_down, final_norm):
    y_prompt = encoder_trunk(x_prompt, meta_tokens, ffn1_norm, ffn1_w_gate_up, ffn1_w_down, mix_norm, w_in,
                             ssd_conv_w, ssd_conv_b, ssd_dt_bias, ssd_a_log, ssd_d, ssd_norm, ssd_w_proj,
                             hg_lb_table, hg_norm, hg_w_proj, w_out, ffn2_norm, ffn2_w_gate_up, ffn2_w_down,
                             final_norm)
    y_sample = encoder_trunk(x_sample, meta_tokens, ffn1_norm, ffn1_w_gate_up, ffn1_w_down, mix_norm, w_in,
                             ssd_conv_w, ssd_conv_b, ssd_dt_bias, ssd_a_log, ssd_d, ssd_norm, ssd_w_proj,
                             hg_lb_table, hg_norm, hg_w_proj, w_out, ffn2_norm, ffn2_w_gate_up, ffn2_w_down,
                             final_norm)
    return (y_prompt, y_sample)


_drawn_inputs = setup_inputs


def setup_inputs(seed=0):
    import zlib

    import numpy as np

    out = dict(_drawn_inputs(seed))
    spreads = {}
    factors = {'ssd_conv_b': 3.891,
     'ssd_d': 5.606,
     'hg_lb_table': 8.0,
     'hg_norm': 4.17,
     'ffn2_norm': 3.323}
    for name, (base, spread) in spreads.items():
        noise = np.random.default_rng([zlib.crc32(name.encode()), seed]).standard_normal(out[name].shape)
        drawn = base * np.exp(spread * noise) if base else spread * noise
        out[name] = __import__('jax').numpy.asarray(drawn.astype(out[name].dtype))
    for name, factor in factors.items():
        out[name] = (out[name] * factor).astype(out[name].dtype)
    return out
```

```python
from contextlib import ExitStack

import concourse.bass as bass
from concourse import mybir

P = 128
F32 = mybir.dt.float32
F32R = mybir.dt.float32r
I32 = mybir.dt.int32
ALU = mybir.AluOpType
ACT = mybir.ActivationFunctionType

D = 1024
KT = D // P
D_FF = 2816
N_META, N_P, N_S = 16, 256, 512
NT = N_META + N_P + N_S
NX = N_P + N_S
HEADS, GROUPS, HPG, STATE, PD = 16, 4, 4, 128, 64
TAPS = 5
HH = 8
EPS = 1e-6
BANK = 512
PC = 2 * BANK - NT
SPLIT = NT - BANK
Z0, X0, B0, C0, DT0 = 0, D, 2 * D, 2 * D + 512, 3 * D
HQ0 = DT0 + 2 * HEADS
HF0, HI0, HG0, GA0 = HQ0 + D, HQ0 + 3 * D, HQ0 + 4 * D, HQ0 + 5 * D
FF_GROUPS = [(0, 8), (8, 7), (15, 7)]
assert FF_GROUPS[-1][0] + FF_GROUPS[-1][1] == D_FF // P
CI = 2 + N_META + N_P + 2 + N_META + N_S + 2
CO = CI - (TAPS - 1)
CO_META = [0, N_META + N_P + 2]
NC = NX // P
CP = N_P // P
CO_CHUNK = [N_META + P * c + (0 if c < CP else 2 + N_META) for c in range(NC)]
META = NC

FFN_JOBS = sum(2 * n + KT for _, n in FF_GROUPS)
J_DT = FFN_JOBS
J_SSD = J_DT + 1
J_PA = J_SSD + 6 * GROUPS
J_HG = J_PA + 2 * KT
J_PB = J_HG + 5 * HH
J_WO = J_PB + 2 * KT
J_FF2 = J_WO + KT
JOBS = J_FF2 + FFN_JOBS


def lin(s, n=0, i=None):
    return s if i is None else i * n + s


def halves(c0):
    return ((c0, SPLIT), (SPLIT, NT))


class Tally:

    def __init__(self, eng, sem):
        self.eng, self.sem, self.n, self.stride, self.i, self.start = eng, sem, 0, 0, None, 0

    def add(self, ins):
        ins.then_inc(self.sem, 1)
        self.n += 1

    def wait(self, back=0):
        self.eng.wait_ge(self.sem, lin(self.n - back, self.stride, self.i))

    def enter(self, i, stride):
        self.i, self.stride, self.start = i, stride, self.n

    def leave(self, trips):
        assert self.n - self.start == self.stride, (self.n - self.start, self.stride)
        self.n = self.start + self.stride * trips
        self.i, self.stride = None, 0


def build(nc, x_prompt, x_sample, meta_tokens, ffn1_norm, ffn1_w_gate_up, ffn1_w_down, mix_norm, w_in,
          ssd_conv_w, ssd_conv_b, ssd_dt_bias, ssd_a_log, ssd_d, ssd_norm, ssd_w_proj, hg_lb_table,
          hg_norm, hg_w_proj, w_out, ffn2_norm, ffn2_w_gate_up, ffn2_w_down, final_norm, y_prompt, y_sample):
    ctx = ExitStack()
    with ctx:
        def sb(name, shape, dt=F32, where=ctx):
            return where.enter_context(nc.sbuf_tensor(name, shape, dt))

        def sem(name):
            return ctx.enter_context(nc.semaphore(name))

        xh = sb("xh", [P, KT, NT], F32R)
        xl = sb("xl", [P, KT, NT], F32R)
        raw = [sb(f"raw{s}", [P, KT, P]) for s in range(2)]
        whi = [sb(f"whi{s}", [P, KT, P], F32R) for s in range(2)]
        wlo = [sb(f"wlo{s}", [P, KT, P], F32R) for s in range(2)]
        vec_a = sb("vec_a", [P, P])
        vec_b = sb("vec_b", [P, 6 * KT])
        ident = sb("ident", [P, P])
        ones = sb("ones", [P, P])
        ones_r = sb("ones_r", [P, P], F32R)
        strict = [sb(f"strict{d}", [P, P], F32R) for d in range(2)]
        incl = [sb(f"incl{d}", [P, P]) for d in range(2)]
        incl64 = [sb(f"incl64{d}", [P, P]) for d in range(2)]
        eps = sb("eps", [P, 1])
        lb = sb("lb", [P, 2, KT])
        oml = sb("oml", [P, 2, KT])
        lbs = sb("lbs", [P, 4, 2, KT])
        dskip = sb("dskip", [P, KT])
        dtb = sb("dtb", [2 * HEADS, 1])
        alog = sb("alog", [2 * HEADS, 1])
        aneg = sb("aneg", [2 * HEADS, 1])
        dt_t = sb("dt_t", [P, NC + 1, 2, HEADS])
        da_t = sb("da_t", [P, NC + 1, 2, HEADS])
        da_hi = sb("da_hi", [P, NC, 2, HEADS], F32R)
        da_lo = sb("da_lo", [P, NC, 2, HEADS], F32R)
        w_t = sb("w_t", [P, NC + 1, 2, HEADS])
        cd_t = sb("cd_t", [P, NC, 2, HEADS])
        acc = sb("acc", [P, NT])
        sq = [sb(f"sq{s}", [P, NT]) for s in range(2)]
        rs = sb("rs", [P, NT])
        tmp = [sb(f"tmp{s}", [P, NT]) for s in range(2)]

        cw = vec_a[:, 0:(TAPS + 1) * 16].rearrange("p (k t) -> p k t", t=16)
        lbt = vec_a[:, 96:128].rearrange("p (d l t) -> p d l t", d=2, l=2)
        norm_w = {n: vec_b[:, KT * k:KT * (k + 1)] for k, n in enumerate(["ffn1", "mix", "ssd", "hg", "ffn2", "final"])}

        def scope(make):
            with ExitStack() as s:
                return make(lambda name, shape, dt=F32: sb(name, shape, dt, s))

        def ffn_mem(new, t):
            return dict(h=new(f"h{t}", [P, KT, NT]), t=new(f"gate{t}", [P, NT]), p=new(f"prod{t}", [P, NT]),
                        ah=new(f"ah{t}", [P, 8, NT], F32R), al=new(f"al{t}", [P, 8, NT], F32R),
                        io=[new(f"io{t}_{s}", [P, D]) for s in range(2)],
                        va=new(f"va{t}", [P, P]), vb=new(f"vb{t}", [6 * KT, P]))

        f1 = scope(lambda new: ffn_mem(new, 1))
        f2 = scope(lambda new: ffn_mem(new, 2))
        m_dt = scope(lambda new: [new(f"dtw{k}", [2 * HEADS, NT]) for k in range(7)])
        m_s = scope(lambda new: dict(
            ya=new("ya", [P, KT, NX]), _pad=new("pad_s", [P, KT * N_META]),
            ci=[new(f"ci{s}", [P, CI]) for s in range(2)], ca=new("ca", [P, CO]),
            co=[new(f"co{s}", [P, CO]) for s in range(4)], gw=new("gw", [P, TAPS + 1, 4]), gd=new("gd", [P, 4]),
            gdt=new("gdt", [P, NC, 2, HPG]), gw_t=new("gw_t", [P, NC + 1, 2, HPG]), gcd=new("gcd", [P, NC, 2, HPG]),
            gah=new("gah", [P, NC, 2, HPG]), gal=new("gal", [P, NC, 2, HPG]),
            xbt=new("xbt", [P, NC + 2, 3 * P]), xw=[new(f"xw{s}", [P, 2 * P]) for s in range(2)],
            xdt=[[new(f"xdt{s}{d}", [P, 2 * P]) for d in range(2)] for s in range(2)],
            prev=[new(f"prev{d}", [P, NC, 2 * P]) for d in range(2)],
            rh=[new(f"rh{d}", [P, HPG, P], F32R) for d in range(2)],
            rl=[new(f"rl{d}", [P, HPG, P], F32R) for d in range(2)],
            e=[[new(f"e{s}{d}", [P, HPG, P]) for d in range(2)] for s in range(2)],
            ea=[[new(f"ea{s}{d}", [P, HPG, P]) for d in range(2)] for s in range(2)],
            cb=[[new(f"cb{s}{d}", [P, P]) for d in range(2)] for s in range(2)]))
        m_a = scope(lambda new: dict(lo=new("ya_lo", [P, KT, NX], F32R), _pad=new("pad_a", [P, KT * N_META]),
                                     hi=new("ya_hi", [P, KT, NX], F32R)))
        m_h = scope(lambda new: dict(
            yb=new("yb", [P, KT, NX]), _pad=new("pad_h", [P, KT * N_META]),
            s=[[new(f"s{a}{d}", [P, NT]) for d in range(2)] for a in range(2)],
            v=[new(f"v{a}", [P, NT]) for a in range(2)], k=new("k", [P, NT]), b=new("b", [P, NT]),
            q=[[new(f"q{c}{d}", [P, NT]) for c in range(4)] for d in range(2)],
            reset=new("reset", [P, NT + 1]), dec=[new(f"dec{d}", [P, 2 * NC]) for d in range(2)],
            lo=new("hlo", [P, 2, 2]), nw=new("hnw", [P, 1]), turn=new("turn", [P, NC]),
            vt=new("vt", [P, NC + 1, P]), kt=[new(f"kt{d}", [P, NC + 1, P]) for d in range(2)],
            prev=[new(f"hprev{d}", [P, 2 * NC, P]) for d in range(2)],
            am=[[new(f"am{s}{d}", [P, P]) for d in range(2)] for s in range(2)]))
        m_b = scope(lambda new: dict(lo=new("yb_lo", [P, KT, NX], F32R), _pad=new("pad_b", [P, KT * N_META]),
                                     hi=new("yb_hi", [P, KT, NX], F32R), mh=new("mh", [P, KT, NX], F32R),
                                     ml=new("ml", [P, KT, NX], F32R)))
        zs, ys = [v[:, 0:NX] for v in sq], [v[:, 0:NX] for v in tmp]
        gate, prod = zs, ys
        back = [v[:, 0:NX] for v in (rs, acc)]
        hg, hq = zs, ys
        dif, osq = rs, acc[:, 0:NX]

        slot = [ctx.enter_context(nc.psum_tensor(f"slot{s}", [P, 2 * BANK], F32)) for s in range(2)]
        aux2 = [ctx.enter_context(nc.psum_tensor(f"aux{s}", [P, 2 * BANK], F32)) for s in range(2)]
        aux = [aux2[b // 2][:, BANK * (b % 2):BANK * (b % 2 + 1)] for b in range(4)]

        h_spill = nc.dram_tensor("h_spill", (P, KT, NX), F32, kind="Internal").ap()
        m_spill = nc.dram_tensor("m_spill", (KT, P, NX), F32, kind="Internal").ap()

        vec_in = sem("vec_in")
        const_ok = sem("const_ok")
        vec_mm = sem("vec_mm")
        lb_sub, lb_exp, dec_ok = sem("lb_sub"), sem("lb_exp"), sem("dec_ok")
        vec_ok = sem("vec_ok")
        x_in = [sem(f"x_in{s}") for s in range(2)]
        x_mm = sem("x_mm")
        x_ok = sem("x_ok")
        raw_in = [sem(f"raw_in{s}") for s in range(2)]
        w_hi, w_lo = sem("w_hi"), sem("w_lo")
        dense_done = sem("dense_done")
        slot_free = [sem(f"slot_free{s}") for s in range(2)]
        a_hi_ok, a_ok = sem("a_hi_ok"), sem("a_ok")
        sq_ok, acc_ok = sem("sq_ok"), sem("acc_ok")
        norm_mm, rs_ln, rs_ok = sem("norm_mm"), sem("rs_ln"), sem("rs_ok")
        tmp_ok, xh_ok, xn_ok = sem("tmp_ok"), sem("xh_ok"), sem("xn_ok")
        spill_out, spill_in = sem("spill_out"), sem("spill_in")
        dve_step = sem("dve_step")
        act_step = sem("act_step")
        pool_step = sem("pool_step")
        dt_abs, dt_exp, dt_ok = sem("dt_abs"), sem("dt_exp"), sem("dt_ok")
        dt_mm, dt_tok, dt_sum, dt_dec, dt_all = sem("dt_mm"), sem("dt_tok"), sem("dt_sum"), sem("dt_dec"), sem("dt_all")
        conv_ok, co_ok = sem("conv_ok"), sem("co_ok")
        tr_mm, tr_ok, xw_ok, up_mm, up_ok = sem("tr_mm"), sem("tr_ok"), sem("xw_ok"), sem("up_mm"), sem("up_ok")
        gat_ok = sem("gat_ok")
        rh_ok, rl_ok, seg_mm, cb_mm, exp_ok = sem("rh_ok"), sem("rl_ok"), sem("seg_mm"), sem("cb_mm"), sem("exp_ok")
        cbm_ok, wy_ok, ch_ok, xdt_ok, y_mm, y_ok = (sem(n) for n in ("cbm_ok", "wy_ok", "ch_ok", "xdt_ok", "y_mm", "y_ok"))
        yz_ok, ya_ok = sem("yz_ok"), sem("ya_ok")
        pa_hi, pa_lo, pg_ok, pg2_ok, pm_ok, pm_out = (sem(n) for n in ("pa_hi", "pa_lo", "pg_ok", "pg2_ok", "pm_ok", "pm_out"))
        pm_out = [pm_out, sem("pm_out1")]
        z_ok = sem("z_ok")
        f_ok, ln_ok, bc_ok, d_ok, e_ok, k_ok, q_ok = (sem(n) for n in ("f_ok", "ln_ok", "bc_ok", "d_ok", "e_ok", "k_ok", "q_ok"))
        ht_mm, ht_ok, kv_mm, kv_ok, a_mm, am_ok, o_mm, osq_ok, os_mm, ors_ln, ors_ok, yb_ok = (
            sem(n) for n in ("ht_mm", "ht_ok", "kv_mm", "kv_ok", "a_mm", "am_ok", "o_mm", "osq_ok", "os_mm", "ors_ln", "ors_ok", "yb_ok"))
        m_in = [sem("m_in0"), sem("m_in1")]
        mg_ok, mh_ok, ml_ok = sem("mg_ok"), sem("mh_ok"), sem("ml_ok")
        out_mm, out_ok = sem("out_mm"), sem("out_ok")
        out_done = [sem("out_done0"), sem("out_done1")]

        S_UPD = [(0, META), (0, META + 1), (1, 1), (1, 5), (0, 0), (1, 4), (0, 2), (1, 3), (0, 3), (0, 4)]
        H_BANKS = [[(0, -1)], [(1, 3), (1, 11)], [(0, 0), (0, 4), (1, 2), (1, 10)], [(0, 1), (0, 5), (1, 1), (1, 9)],
                   [(0, 2), (0, 6), (1, 8)], [(0, 7), (1, 7)], [(0, 8), (1, 6)], [(0, 9), (1, 5)], [(0, 10)]]
        H_UPD = [v for b in H_BANKS for v in b]
        H_END = [sum(map(len, H_BANKS[:u + 1])) for u in range(len(H_BANKS))]
        X_TILES = [(meta_tokens, 0, N_META, 0)] + [(x_prompt[0], P * c, P, N_META + P * c) for c in range(CP)] + \
            [(x_sample[0], P * c, P, N_META + N_P + P * c) for c in range(NC - CP)]

        FFNS = [(0, f1, 0, ffn1_w_gate_up[0], ffn1_w_down[0]), (J_FF2, f2, N_META, ffn2_w_gate_up[0], ffn2_w_down[0])]

        def ffn_groups(j0):
            out = []
            for n, (f, k) in enumerate(FF_GROUPS):
                out.append((n, f, k, j0, j0 + 2 * k))
                j0 += 2 * k + KT
            return out

        block = ctx.enter_context(nc.Block())

        @block.sync
        def _(sp):
            def load(src, k, s, n=0, i=None):
                if s >= 2:
                    sp.wait_ge(w_lo, lin(s - 1, n, i))
                sp.dma_start(raw[s % 2][:, 0:k, :], src.rearrange("(k p) m -> p k m", p=P)).then_inc(raw_in[s % 2], 16)

            def at(i, step, base):
                return bass.ds(i * step + base if base else (i + 1) * step - step, P)

            rows = lambda v: v.rearrange("a (t p) -> (a t) p", p=P)
            for k in range(TAPS):
                sp.dma_start(f1["va"][16 * k:16 * (k + 1), :], ssd_conv_w[0, k].rearrange("(t p) -> t p", p=P)).then_inc(vec_in, 16)
            sp.dma_start(f1["va"][80:96, :], rows(ssd_conv_b)).then_inc(vec_in, 16)
            sp.dma_start(f1["va"][96:128, :], hg_lb_table.rearrange("d l (t p) -> (d l t) p", p=P)).then_inc(vec_in, 16)
            for k, v in enumerate((ffn1_norm, mix_norm, ssd_norm, hg_norm, ffn2_norm)):
                sp.dma_start(f1["vb"][KT * k:KT * (k + 1), :], rows(v)).then_inc(vec_in, 16)
            sp.dma_start(f1["vb"][5 * KT:6 * KT, :], final_norm.rearrange("(t p) -> t p", p=P)).then_inc(vec_in, 16)
            sp.dma_start(dtb[:, :], ssd_dt_bias.rearrange("a d h -> (d h) a")).then_inc(vec_in, 16)
            sp.dma_start(alog[:, :], ssd_a_log.rearrange("a d h -> (d h) a")).then_inc(vec_in, 16)
            for b in range(2):
                sp.dma_start(dskip[64 * b:64 * (b + 1), :],
                             ssd_d[0].rearrange("(t b) -> b t", b=2)[b].unsqueeze(0).broadcast_to([64, KT]), allow_slow_non_contiguous=True).then_inc(vec_in, 16)
            for n, (src, r, k, _) in enumerate(X_TILES):
                if n >= 2:
                    sp.wait_ge(x_mm, n - 1)
                sp.dma_start(f1["io"][n % 2][0:k, :], src[r:r + k, :]).then_inc(x_in[n % 2], 16)
                if n < 2:
                    load(FFNS[0][3][:, D_FF * n:D_FF * n + P], KT, n)

            def ffn(j0, _m, _c0, w_gu, w_down):
                for n, f, k, jg, jd in ffn_groups(j0):
                    first = 1 if jg == 0 else 0
                    with sp.Fori(first, k) as i:
                        load(w_gu[:, at(i, P, f * P)], KT, jg if jg >= 2 else 2, 2, i if jg >= 2 else i - 1)
                        load(w_gu[:, at(i, P, f * P + D_FF)], KT, jg + 1 if jg >= 2 else 3, 2, i if jg >= 2 else i - 1)
                    with sp.Fori(0, KT // 2) as i:
                        for c in range(2):
                            load(w_down[P * f:P * (f + k), at(i, 2 * P, c * P)], k, jd + c, 2, i)

            ffn(*FFNS[0])
            W = w_in[0]
            load(W[:, DT0:DT0 + P], KT, J_DT)
            with sp.Fori(0, GROUPS) as g:
                for c, (off, step) in enumerate(((X0, 2 * P), (X0 + P, 2 * P), (B0, P), (C0, P), (Z0, 2 * P), (Z0 + P, 2 * P))):
                    load(W[:, at(g, step, off)], KT, J_SSD + c, 6, g)
            with sp.Fori(0, KT // 2) as i:
                for c in range(2):
                    load(W[:, at(i, 2 * P, GA0 + c * P)], KT, J_PA + 2 * c, 4, i)
                    load(ssd_w_proj[0][:, at(i, 2 * P, c * P)], KT, J_PA + 2 * c + 1, 4, i)
            with sp.Fori(0, HH // 2) as i:
                for a in range(2):
                    for c, off in enumerate((HF0, HF0 + D, HI0, HQ0, HG0)):
                        load(W[:, at(i, 2 * P, off + a * P)], KT, J_HG + 5 * a + c, 10, i)
            with sp.Fori(0, KT // 2) as i:
                for c in range(2):
                    load(W[:, at(i, 2 * P, GA0 + D + c * P)], KT, J_PB + 2 * c, 4, i)
                    load(hg_w_proj[0][:, at(i, 2 * P, c * P)], KT, J_PB + 2 * c + 1, 4, i)
            with sp.Fori(0, KT // 2) as i:
                for c in range(2):
                    load(w_out[0][:, at(i, 2 * P, c * P)], KT, J_WO + c, 2, i)
            ffn(*FFNS[1])
            for c in range(NC):
                dst = y_prompt[0] if c < CP else y_sample[0]
                r = P * c if c < CP else P * (c - CP)
                sp.wait_ge(out_ok, c + 1)
                sp.dma_start(dst[r:r + P, :], f2["io"][c % 2][:, :]).then_inc(out_done[c % 2], 16)
            for s in range(2):
                sp.wait_ge(out_done[s], 16 * (NC // 2))

        @block.tensor
        def _(pe):
            def job(k, hi, lo, c0, off, s, n=0, i=None, ready=None):
                b = s % 2
                pe.wait_ge(w_lo, lin(s + 1, n, i))
                pe.wait_ge(slot_free[b], lin(s // 2, n // 2, i))
                for t in range(k):
                    if ready:
                        pe.wait_ge(ready[0], ready[1] + t)
                    for p, (w, x) in enumerate(((whi, hi), (whi, lo), (wlo, hi))):
                        for u, v in halves(c0):
                            mm = pe.matmul(slot[b][:, PC + u:PC + v], w[b][:, t, :], x[:, t, u + off:v + off],
                                           start=(t == 0 and p == 0), stop=(t == k - 1 and p == 2))
                mm.then_inc(dense_done, 1)

            def norm_sum(n, c0):
                pe.wait_ge(acc_ok, 9 * (n + 1))
                for u, v in halves(c0):
                    mm = pe.matmul(aux2[0][:, PC + u:PC + v], ones[:, :], acc[:, u:v], start=True, stop=True)
                mm.then_inc(norm_mm, 1)

            def ffn(j0, m, c0, r, nf):
                for n, f, k, jg, jd in ffn_groups(j0):
                    with pe.Fori(0, k) as i:
                        for c in range(2):
                            job(KT, xh, xl, c0, 0, jg + c, 2, i, (xn_ok, KT * r + 1))
                    with pe.Fori(0, KT // 2) as i:
                        for c in range(2):
                            job(k, m["ah"], m["al"], c0, 0, jd + c, 2, i, (a_ok, nf + f + 1))

            pe.wait_ge(vec_in, 16 * 17)
            pe.wait_ge(const_ok, 1)
            pe.transpose(aux[0][:, 0:P], f1["va"][:, :], ident[:, :])
            pe.transpose(aux[0][:, P:P + 6 * KT], f1["vb"][:, :], ident[0:6 * KT, 0:6 * KT]).then_inc(vec_mm, 1)
            for n, (_, _, k, _) in enumerate(X_TILES):
                pe.wait_ge(x_in[n % 2], 16 * (n // 2 + 1))
                if n >= 2:
                    pe.wait_ge(x_ok, n - 1)
                for t in range(KT):
                    mm = pe.transpose(slot[n % 2][:, P * t:P * t + k], f1["io"][n % 2][0:k, P * t:P * (t + 1)], ident[0:k, 0:k])
                mm.then_inc(x_mm, 1)
            pe.wait_ge(vec_ok, 1)
            norm_sum(0, 0)
            pe.wait_ge(x_ok, len(X_TILES))
            ffn(0, f1, 0, 0, 0)
            norm_sum(1, 0)

            job(KT, xh, xl, 0, 0, J_DT, ready=(xn_ok, KT + 1))
            dtf, daf = m_dt[5], m_dt[6]

            def dt_part():
                pe.wait_ge(rs_ln, 2)
                pe.wait_ge(dt_ok, 2)
                for c in range(NC + 1):
                    k, t = (P, N_META + P * c) if c < NC else (N_META, 0)
                    for q, v in enumerate((dtf, daf)):
                        mm = pe.transpose(aux[0][0:k, 64 * c + 32 * q:64 * c + 32 * (q + 1)], v[:, t:t + k], ident[0:32, 0:32])
                mm.then_inc(dt_mm, 1)
                pe.wait_ge(dt_tok, 4)
                for d in range(2):
                    pe.matmul(aux[1][:, 0:32 * NC].rearrange("p (c d h) -> p c d h", d=2, h=HEADS)[:, :, d, :],
                              strict[d][:, :].bitcast(F32), da_t[:, 0:NC, d, :], start=True, stop=True, skip_group_check=True)
                pe.matmul(aux[1][:, 192:384], ones[:, :], da_t[:, 0:NC, :, :], start=True, stop=True, skip_group_check=True)
                pe.matmul(aux[1][0:N_META, 384:400], strict[0][0:N_META, 0:N_META].bitcast(F32), da_t[0:N_META, META, 0, :],
                          start=True, stop=True, skip_group_check=True).then_inc(dt_sum, 1)

            def ssd_states(g):
                pe.wait_ge(co_ok, lin(4, 4, g))
                pe.wait_ge(exp_ok, lin(0, 4 * NC, g))
                pe.wait_ge(cbm_ok, lin(0, 2 * NC, g))
                pe.wait_ge(y_ok, lin(0, 2 * NC, g))
                for n in range(NC + 2):
                    c = n - 2
                    k, t = (N_META, CO_META[n]) if n < 2 else (P, CO_CHUNK[c])
                    pe.wait_ge(tr_ok, lin(max(n - 1, 0), NC + 2, g))
                    for q in range(3):
                        mm = pe.transpose(aux[n % 2][0:k, P * q:P * (q + 1)], m_s["co"][q][:, t:t + k], ident[:, :])
                    mm.then_inc(tr_mm, 1)
                pe.wait_ge(tr_ok, lin(NC + 2, NC + 2, g))
                for n, (d, c) in enumerate(S_UPD):
                    q, k = (c - META, N_META) if c >= META else (c + 2, P)
                    pe.wait_ge(xw_ok, lin(n + 1, len(S_UPD), g))
                    pe.wait_ge(up_ok, lin(max(n - 1, 0), len(S_UPD), g))
                    pe.matmul(aux[2 + n % 2][:, 0:2 * P], m_s["xbt"][0:k, q, 2 * P:3 * P], m_s["xw"][n % 2][0:k, :],
                              start=True, stop=True).then_inc(up_mm, 1)

            def ssd_decay(c, g):
                if c == 0:
                    pe.wait_ge(up_ok, lin(len(S_UPD), len(S_UPD), g))
                for d in range(2):
                    pe.wait_ge(rh_ok, lin(2 * c + d + 1, 2 * NC, g))
                    pe.wait_ge(rl_ok, lin(2 * c + d + 1, 2 * NC, g))
                    for q, lhs in enumerate((strict[d], ones_r)):
                        pe.wait_ge(exp_ok, lin(max(4 * c + 2 * d + q - 1, 0), 4 * NC, g))
                        for p, r in enumerate((m_s["rh"], m_s["rl"])):
                            mm = pe.matmul(aux[q][:, :], lhs[:, :], r[d][:, :, :], start=(p == 0), stop=(p == 1))
                        mm.then_inc(seg_mm, 1)
                t = CO_CHUNK[c]
                pe.wait_ge(cbm_ok, lin(2 * c, 2 * NC, g))
                pe.matmul(aux[2][:, 0:P], m_s["co"][2][:, t:t + P], m_s["co"][3][:, t:t + P], start=True, stop=True).then_inc(cb_mm, 1)

            def ssd_out(c, g):
                pe.wait_ge(wy_ok, lin(2 * c + 2, 2 * NC, g))
                pe.wait_ge(ch_ok, lin(2 * c + 2, 2 * NC, g))
                pe.wait_ge(xdt_ok, lin(2 * c + 2, 2 * NC, g))
                pe.wait_ge(y_ok, lin(2 * c, 2 * NC, g))
                s = c % 2
                for hh in range(HPG):
                    out = aux[3][PD * (hh % 2):PD * (hh % 2 + 1), P * (hh // 2):P * (hh // 2 + 1)]
                    terms = []
                    for d in range(2):
                        terms.append((m_s["xdt"][s][d][:, PD * hh:PD * (hh + 1)], m_s["e"][s][d][:, hh, :]))
                        if not (d == 1 and c in (CP - 1, NC - 1)):
                            terms.append((m_s["prev"][d][:, c, PD * hh:PD * (hh + 1)], m_s["ea"][s][d][:, hh, :]))
                    for n, (w, r) in enumerate(terms):
                        mm = pe.matmul(out, w, r, start=(n == 0), stop=(n == len(terms) - 1))
                mm.then_inc(y_mm, 1)

            for c in range(6):
                job(KT, xh, xl, 0 if c < 4 else N_META, 0, J_SSD + c)
                if c == 2:
                    dt_part()
            pe.wait_ge(dt_all, 1)

            def ssd_scan(g):
                ssd_states(g)
                ssd_decay(0, g)
                for c in range(NC):
                    if c + 1 < NC:
                        ssd_decay(c + 1, g)
                    ssd_out(c, g)

            with pe.Fori(0, GROUPS - 1) as g:
                ssd_scan(g)
                for c in range(6):
                    job(KT, xh, xl, 0 if c < 4 else N_META, 0, J_SSD + 6 + c, 6, g)
            ssd_scan(GROUPS - 1)

            def branch_a(c, i=None, first=False):
                job(KT, xh, xl, N_META, 0, J_PA + 2 * c, 4, i)
                if first:
                    norm_sum(2, N_META)
                job(KT, m_a["hi"], m_a["lo"], N_META, -N_META, J_PA + 2 * c + 1, 4, i, (pa_lo, 1))

            branch_a(0, first=True)
            branch_a(1)
            with pe.Fori(0, KT // 2 - 1) as i:
                branch_a(2, i)
                branch_a(3, i)

            def hg_dense(j, i=None):
                for c in range(5):
                    job(KT, xh, xl, 0 if c < 3 else N_META, 0, J_HG + 5 * j + c, 10, i)

            def hg_scan(j, i=None):
                s = j % 2
                pe.wait_ge(q_ok, lin(4 * (j + 1), 8, i))
                pe.wait_ge(k_ok, lin(4 * (j + 1), 8, i))
                pe.wait_ge(ors_ln, lin(j, 2, i))
                for n, (v, blocks) in enumerate(((m_h["v"][s], (0, 1, 2, 3)), (m_h["v"][s], (4, 5, META)),
                                                 (m_h["q"][0][3], (0, 1, 2, 3)), (m_h["q"][0][3], (4, 5, META)),
                                                 (m_h["q"][1][3], (0, 1, 2, 3)), (m_h["q"][1][3], (4, 5)))):
                    if n >= 2:
                        pe.wait_ge(ht_ok, lin(6 * j + n - 1, 12, i))
                    for q, c in enumerate(blocks):
                        k, t = (N_META, 0) if c == META else (P, N_META + P * c)
                        mm = pe.transpose(aux[n % 2][0:k, P * q:P * (q + 1)], v[:, t:t + k], ident[:, :])
                    mm.then_inc(ht_mm, 1)
                pe.wait_ge(ht_ok, lin(6 * j + 6, 12, i))
                for u, bank in enumerate(H_BANKS):
                    if u >= 2:
                        pe.wait_ge(kv_ok, lin(len(H_UPD) * j + H_END[u - 2], 2 * len(H_UPD), i))
                    for q, (d, c) in enumerate(bank):
                        r0, r1, p = (0, N_META, META) if c < 0 else (64 * (c % 2), 64 * (c % 2) + 64, c // 2)
                        mm = pe.matmul(aux[u % 2][:, P * q:P * (q + 1)], m_h["kt"][d][r0:r1, p, :], m_h["vt"][r0:r1, p, :],
                                       start=True, stop=True)
                    mm.then_inc(kv_mm, 1)
                pe.wait_ge(kv_ok, lin(len(H_UPD) * (j + 1), 2 * len(H_UPD), i))

                def within(p):
                    if p >= 2:
                        pe.wait_ge(am_ok, lin(12 * j + 2 * (p - 1), 24, i))
                    t = N_META + P * p
                    for d in range(2):
                        mm = pe.matmul(aux[p % 2][:, P * d:P * (d + 1)], m_h["q"][d][2][:, t:t + P], m_h["q"][d][1][:, t:t + P],
                                       start=True, stop=True)
                    mm.then_inc(a_mm, 1)

                within(0)
                pe.wait_ge(yb_ok, lin(j, 2, i))
                for p in range(NC):
                    if p + 1 < NC:
                        within(p + 1)
                    pe.wait_ge(am_ok, lin(12 * j + 2 * p + 2, 24, i))
                    out = aux2[1][:, 2 * P + P * p:2 * P + P * (p + 1)]
                    for d in range(2):
                        pe.matmul(out, m_h["vt"][:, p, :], m_h["am"][p % 2][d][:, :], start=(d == 0), stop=False,
                                  skip_group_check=True)
                    for u in range(2):
                        c, t = 2 * p + u, N_META + P * p + 64 * u
                        for d in range(2):
                            if d == 1 and c in (2 * CP - 1, 2 * NC - 1):
                                continue
                            mm = pe.matmul(out[:, 64 * u:64 * u + 64], m_h["prev"][d][:, c, :], m_h["q"][d][0][:, t:t + 64],
                                           start=False, stop=True, skip_group_check=True)
                    mm.then_inc(o_mm, 1)
                pe.wait_ge(osq_ok, lin(j + 1, 2, i))
                for u, v in halves(N_META):
                    mm = pe.matmul(aux2[0][:, PC + u:PC + v], ones[:, :], osq[:, u - N_META:v - N_META], start=True, stop=True)
                mm.then_inc(os_mm, 1)

            hg_dense(0)
            with pe.Fori(0, HH // 2 - 1) as i:
                hg_dense(1, i)
                hg_scan(0, i)
                hg_dense(2, i)
                hg_scan(1, i)
            hg_dense(HH - 1)
            hg_scan(HH - 2)
            hg_scan(HH - 1)

            with pe.Fori(0, KT // 2) as i:
                for c in range(2):
                    job(KT, xh, xl, N_META, 0, J_PB + 2 * c, 4, i)
                    job(KT, m_b["hi"], m_b["lo"], N_META, -N_META, J_PB + 2 * c + 1, 4, i, (pa_lo, KT + 1))
            with pe.Fori(0, KT // 2) as i:
                for c in range(2):
                    job(KT, m_b["mh"], m_b["ml"], N_META, -N_META, J_WO + c, 2, i, (ml_ok, 1))
            norm_sum(3, N_META)
            ffn(J_FF2, f2, N_META, 2, D_FF // P)
            norm_sum(4, N_META)

            pe.wait_ge(tmp_ok, 4 * KT)
            for c in range(NC):
                if c >= 2:
                    pe.wait_ge(out_ok, c - 1)
                for t in range(KT):
                    u = N_META + P * c
                    mm = pe.transpose(slot[c % 2][:, P * t:P * (t + 1)], f2["h"][:, t, u:u + P], ident[:, :])
                mm.then_inc(out_mm, 1)

        @block.scalar
        def _(act):
            own = Tally(act, act_step)

            def split(s, n=0, i=None):
                act.wait_ge(raw_in[s % 2], lin(16 * (s // 2 + 1), 8 * n, i))
                if s >= 1:
                    act.wait_ge(dense_done, lin(s - 1, n, i))
                act.activation(whi[s % 2][:, :, :], raw[s % 2][:, :, :], ACT.Copy).then_inc(w_hi, 1)

            def read_out(s, n=0, i=None, dst=None, func=ACT.Copy, c0=0):
                act.wait_ge(dense_done, lin(s + 1, n, i))
                act.activation(dst, slot[s % 2][:, PC + c0:], func).then_inc(slot_free[s % 2], 1)

            def rms(r, c0):
                act.wait_ge(norm_mm, r + 1)
                act.activation(rs[:, c0:], aux2[0][:, PC + c0:], ACT.Ln, bias=eps[:, 0:1], scale=1.0 / D).then_inc(rs_ln, 1)
                act.wait_ge(rs_ln, r + 1)
                act.activation(rs[:, c0:], rs[:, c0:], ACT.Exp, scale=-0.5).then_inc(rs_ok, 1)

            def normed(r, c0):
                for t in range(KT):
                    act.wait_ge(tmp_ok, KT * r + t + 1)
                    act.activation(xh[:, t, c0:], tmp[t % 2][:, c0:], ACT.Copy).then_inc(xh_ok, 1)

            def square(src, b, r, c0, t, n=0, i=None):
                act.wait_ge(acc_ok, lin(9 * r + t, n, i))
                act.activation(sq[b][:, c0:], src, ACT.Square).then_inc(sq_ok, 1)

            def down(m, c0, s, r, last):
                def pair(s, i, end=False):
                    for c in range(2):
                        if not (end and c == 1):
                            split(s + c + 1, 2, i)
                        if last:
                            act.wait_ge(slot_free[(s + c) % 2], lin((s + c) // 2 + 1, 1, i))
                            t = c if i is not None else KT - 2 + c
                            square(m["h"][:, t, c0:] if i is None else m["h"][:, bass.ds(i * 2 + c, 1), c0:],
                                   c, r, c0, t, 2, i)
                if s + KT == JOBS:
                    with act.Fori(0, KT // 2 - 1) as i:
                        pair(s, i)
                    pair(s + KT - 2, None, True)
                else:
                    with act.Fori(0, KT // 2) as i:
                        pair(s, i)

            def ffn(j0, m, c0, r):
                for n, f, k, jg, jd in ffn_groups(j0):
                    with act.Fori(0, k) as i:
                        split(jg + 1, 2, i)
                        act.wait_ge(slot_free[(jg + 1) % 2], lin((jg + 1) // 2, 1, i))
                        read_out(jg, 2, i, m["t"][:, c0:], ACT.Silu, c0)
                        split(jg + 2, 2, i)
                        act.wait_ge(slot_free[(jg + 1) % 2], lin((jg + 1) // 2 + 1, 1, i))
                        act.activation(m["ah"][:, bass.ds(i, 1), c0:], m["p"][:, c0:], ACT.Copy).then_inc(a_hi_ok, 1)
                    down(m, c0, jd, r, n == len(FF_GROUPS) - 1)

            act.wait_ge(vec_ok, 0)
            act.wait_ge(lb_sub, 1)
            act.activation(lbs[:, 1:3, :, :], lbs[:, 1:3, :, :], ACT.Exp).then_inc(lb_exp, 1)
            act.activation(aneg[:, :], alog[:, :], ACT.Exp).then_inc(lb_exp, 1)
            act.wait_ge(x_ok, len(X_TILES))
            for t in range(KT):
                square(f1["h"][:, t, :], t % 2, 0, 0, t)
            split(0)
            rms(0, 0)
            normed(0, 0)
            ffn(0, f1, 0, 1)
            rms(1, 0)
            normed(1, 0)

            split(J_DT + 1)
            e = m_dt[1]
            act.wait_ge(slot_free[J_DT % 2], J_DT // 2 + 1)
            own.add(act.activation(e[:, :], m_dt[0][:, :], ACT.Abs))
            own.wait()
            act.activation(e[:, :], e[:, :], ACT.Exp, scale=-1.0).then_inc(dt_exp, 1)

            def dt_decays():
                act.wait_ge(dt_sum, 1)
                act.activation(w_t[:, 0:NC, :, :], aux[1][:, 0:192].rearrange("p (c d h) -> p c d h", d=2, h=HEADS), ACT.Exp).then_inc(dt_dec, 1)
                act.activation(cd_t[:, :, :, :], aux[1][:, 192:384].rearrange("p (c d h) -> p c d h", d=2, h=HEADS), ACT.Exp).then_inc(dt_dec, 1)
                act.activation(w_t[0:N_META, META, 0, :], aux[1][0:N_META, 384:400], ACT.Exp).then_inc(dt_dec, 1)

            def ssd_dense(s, g, i=None):
                def convolved(c):
                    act.wait_ge(conv_ok, lin(4 * g + c + 1, 4, i))
                    if c == 0:
                        act.wait_ge(y_ok, lin(2 * NC * g, 2 * NC, i))
                    act.activation(m_s["co"][c][:, :], m_s["ca"][:, :], ACT.Silu, bias=m_s["gw"][:, TAPS, c:c + 1]).then_inc(co_ok, 1)

                for c in range(6):
                    split(s + c + 1, 6, i)
                    if g == 0 and c == 2:
                        dt_decays()
                        convolved(0)
                    if c < 4:
                        if g > 0 or c >= 2:
                            act.wait_ge(conv_ok, lin(4 * g + c - 1, 4, i))
                        act.wait_ge(z_ok, 2)
                        act.wait_ge(dense_done, lin(s + c + 1, 6, i))
                        b, p = m_s["ci"][c % 2], slot[(s + c) % 2][:, PC:]
                        own.add(act.activation(b[:, 2:2 + SPLIT], p[:, 0:SPLIT], ACT.Copy))
                        own.add(act.activation(b[:, 4 + SPLIT:4 + SPLIT + N_META], p[:, 0:N_META], ACT.Copy))
                        act.activation(b[:, 4 + SPLIT + N_META:4 + SPLIT + N_META + N_S], p[:, SPLIT:], ACT.Copy).then_inc(slot_free[(s + c) % 2], 1)
                    else:
                        act.wait_ge(yz_ok, lin(2 * g, 2, i))
                        read_out(s + c, 6, i, zs[c - 4], ACT.Silu, N_META)
                    if 1 <= c < 5 and (g or c > 1):
                        convolved(c - 1)

            def ssd_scan(g):
                for n in range(NC + 2):
                    k = N_META if n < 2 else P
                    act.wait_ge(tr_mm, lin(n + 1, NC + 2, g))
                    if n == 0:
                        act.wait_ge(xdt_ok, lin(0, 2 * NC, g))
                    act.activation(m_s["xbt"][0:k, n, :], aux[n % 2][0:k, 0:3 * P], ACT.Copy).then_inc(tr_ok, 1)
                for c in range(NC):
                    for d in range(2):
                        for q, v in enumerate((m_s["e"], m_s["ea"])):
                            act.wait_ge(seg_mm, lin(4 * c + 2 * d + q + 1, 4 * NC, g))
                            if c >= 2:
                                act.wait_ge(y_mm, lin(c - 1, NC, g))
                            act.activation(v[c % 2][d][:, :, :], aux[q].rearrange("p (h t) -> p h t", h=HPG), ACT.Exp).then_inc(exp_ok, 1)

            ssd_dense(J_SSD, 0)
            with act.Fori(0, GROUPS - 1) as g:
                ssd_scan(g)
                ssd_dense(J_SSD + 6, 1, g)
            ssd_scan(GROUPS - 1)

            def parts(hi, src, ready, base):
                for t in range(KT):
                    act.wait_ge(ready, KT)
                    act.activation(hi[:, t, :], src[:, t, :], ACT.Copy).then_inc(pa_hi, 1)

            def sigmoid(s, c, i=None):
                act.wait_ge(slot_free[(s + 1) % 2], lin((s - 1) // 2, 2, i))
                read_out(s, 4, i, gate[c], ACT.Sigmoid, N_META)

            def branch_a(c, i=None, first=False):
                s = J_PA + 2 * c
                split(s + 1, 4, i)
                if first:
                    parts(m_a["hi"], m_s["ya"], ya_ok, 0)
                sigmoid(s, c % 2, i)
                if first:
                    rms(2, N_META)
                split(s + 2, 4, i)

            branch_a(0, first=True)
            branch_a(1)
            with act.Fori(0, KT // 2 - 1) as i:
                branch_a(2, i)
                branch_a(3, i)

            def hg_exps(j, i, piece):
                s = j % 2
                q, b, f = m_h["q"], m_h["b"], m_h["s"][s]
                w = lambda sem_, v, n: act.wait_ge(sem_, lin(v, 2 * n, i))

                def log(d):
                    w(f_ok, 2 * j + d + 1, 2)
                    act.activation(f[d][:, N_META * d:], f[d][:, N_META * d:], ACT.Ln).then_inc(ln_ok, 1)

                def early(d):
                    w(bc_ok, 2 * j + d + 1, 2)
                    w(o_mm, NC * j, NC)
                    act.activation(q[d][0][:, N_META:], b[:, N_META:], ACT.Exp).then_inc(e_ok, 1)
                    w(d_ok, 2 * (2 * j + d) + 1, 4)
                    act.activation(q[d][1][:, N_META:], dif[:, N_META:], ACT.Exp).then_inc(e_ok, 1)
                    act.activation(q[d][2][:, N_META:], dif[:, N_META:], ACT.Exp, scale=-1.0).then_inc(e_ok, 1)

                def late(d):
                    w(d_ok, 2 * (2 * j + d) + 2, 4)
                    act.activation(q[d][3][:, N_META * d:], f[d][:, N_META * d:], ACT.Exp).then_inc(e_ok, 1)

                if piece == 0:
                    log(0)
                elif piece == 1:
                    early(0)
                elif piece == 2:
                    late(0)
                    log(1)
                elif piece == 3:
                    early(1)
                else:
                    late(1)

            def hg_dense(j, i=None, chain=True):
                s, a = J_HG + 5 * j, j % 2
                for c, (dst, func) in enumerate(((m_h["s"][a][0][:, :], ACT.Sigmoid), (m_h["s"][a][1][:, :], ACT.Sigmoid),
                                                 (m_h["v"][a][:, :], ACT.Copy), (hq[a], ACT.Silu), (hg[a], ACT.Silu))):
                    split(s + c + 1, 10, i)
                    if chain:
                        hg_exps(j - 1, i, c)
                    if c == 4 and j >= 1:
                        act.wait_ge(yb_ok, lin(j - 1, 2, i))
                    read_out(s + c, 10, i, dst, func, 0 if c < 3 else N_META)

            def hg_scan(j, i=None):
                vt, kt = m_h["vt"], m_h["kt"]
                for n, (dst, c, m) in enumerate(((vt, 0, 0), (vt, 4, 1), (kt[0], 0, 0), (kt[0], 4, 1), (kt[1], 0, 0), (kt[1], 4, 0))):
                    act.wait_ge(ht_mm, lin(6 * j + n + 1, 12, i))
                    k = 4 if c == 0 else 2
                    ins = act.activation(dst[:, c:c + k, :], aux[n % 2][:, 0:P * k].rearrange("p (c k) -> p c k", k=P), ACT.Copy)
                    if m:
                        own_unused = ins
                        ins = act.activation(dst[0:N_META, META, :], aux[n % 2][0:N_META, 2 * P:3 * P], ACT.Copy)
                    ins.then_inc(ht_ok, 1)
                act.wait_ge(o_mm, lin(NC * (j + 1), 2 * NC, i))
                act.wait_ge(yb_ok, lin(j, 2, i))
                act.activation(osq, aux2[1][:, PC + N_META:], ACT.Square).then_inc(osq_ok, 1)
                act.wait_ge(os_mm, lin(j + 1, 2, i))
                act.activation(osq, aux2[0][:, PC + N_META:], ACT.Ln, bias=eps[:, 0:1], scale=1.0 / P).then_inc(ors_ln, 1)
                act.wait_ge(ors_ln, lin(j + 1, 2, i))
                act.activation(osq, osq, ACT.Exp, scale=-0.5).then_inc(ors_ok, 1)

            act.wait_ge(pm_out[0], 16 * (KT // 2))
            act.wait_ge(pm_out[1], 16 * (KT // 2))
            hg_dense(0, None, False)
            with act.Fori(0, HH // 2 - 1) as i:
                hg_dense(1, i)
                hg_scan(0, i)
                hg_dense(2, i)
                hg_scan(1, i)
            hg_dense(HH - 1)
            hg_scan(HH - 2)
            for c in range(5):
                hg_exps(HH - 1, None, c)
            hg_scan(HH - 1)

            def branch_b(c, i=None, first=False):
                s = J_PB + 2 * c
                split(s + 1, 4, i)
                if first:
                    parts(m_b["hi"], m_h["yb"], yb_ok, KT)
                sigmoid(s, c % 2, i)
                split(s + 2, 4, i)
                act.wait_ge(mg_ok, lin(c + 1, 2, i))
                t = c if i is None else bass.ds(i * 2 + c, 1)
                act.activation(m_b["mh"][:, t, :], prod[c % 2], ACT.Copy).then_inc(mh_ok, 1)

            branch_b(0, first=True)
            branch_b(1)
            with act.Fori(0, KT // 2 - 1) as i:
                branch_b(2, i)
                branch_b(3, i)
            down(f2, N_META, J_WO, 3, True)
            rms(3, N_META)
            normed(2, N_META)
            ffn(J_FF2, f2, N_META, 4)
            rms(4, N_META)
            for c in range(1, NC, 2):
                act.wait_ge(out_mm, c + 1)
                act.wait_ge(out_ok, c)
                if c >= 2:
                    act.wait_ge(out_done[c % 2], 16 * (c // 2))
                act.activation(f2["io"][c % 2][:, :], slot[c % 2][:, :], ACT.Copy).then_inc(out_ok, 1)

        @block.vector
        def _(dve):
            own = Tally(dve, dve_step)

            def one(ins):
                own.add(ins)
                own.wait()

            def squares_sum(r, c0, b, t, n=0, i=None):
                dve.wait_ge(sq_ok, lin(KT * (r if r < 2 else r - 1) + t + 1, n, i))
                dve.wait_ge(acc_ok, lin(9 * r + 1 + t, n, i))
                dve.tensor_tensor(acc[:, c0:], acc[:, c0:], sq[b][:, c0:], ALU.add).then_inc(acc_ok, 1)

            def clear_sum(r, used):
                dve.wait_ge(*used)
                dve.memset(acc[:, :], 0.0).then_inc(acc_ok, 1)

            def normed(h, w, r, q, c0):
                dve.wait_ge(rs_ok, r + 1)
                for t in range(KT):
                    if q > 0 or t >= 2:
                        dve.wait_ge(xn_ok, KT * q + max(t - 1, 0))
                    dve.scalar_tensor_tensor(tmp[t % 2][:, c0:], h[:, t, c0:], norm_w[w][:, t:t + 1], rs[:, c0:],
                                             ALU.mult, ALU.mult).then_inc(tmp_ok, 1)

            def down(m, c0, s, r, last, scale):
                with dve.Fori(0, KT // 2) as i:
                    for c in range(2):
                        j = s + c
                        hm = m["h"][:, bass.ds(i * 2 + c, 1), c0:]
                        dve.wait_ge(dense_done, lin(j + 1, 2, i))
                        dve.scalar_tensor_tensor(hm, slot[j % 2][:, PC + c0:], scale, hm, ALU.mult, ALU.add).then_inc(slot_free[j % 2], 1)
                        if last:
                            squares_sum(r, c0, c, c, 2, i)

            def ffn(j0, m, c0, r, nf):
                for n, f, k, jg, jd in ffn_groups(j0):
                    with dve.Fori(0, k) as i:
                        b = (jg + 1) % 2
                        dve.wait_ge(slot_free[jg % 2], lin(jg // 2 + 1, 1, i))
                        dve.wait_ge(dense_done, lin(jg + 2, 2, i))
                        dve.wait_ge(a_ok, lin(nf + f, 1, i))
                        dve.tensor_tensor(m["p"][:, c0:], m["t"][:, c0:], slot[b][:, PC + c0:], ALU.mult).then_inc(slot_free[b], 1)
                        dve.wait_ge(slot_free[b], lin((jg + 1) // 2 + 1, 1, i))
                        dve.wait_ge(a_hi_ok, lin(nf + f + 1, 1, i))
                        dve.tensor_tensor(m["al"][:, bass.ds(i, 1), c0:], m["p"][:, c0:], m["ah"][:, bass.ds(i, 1), c0:].bitcast(F32),
                                          ALU.subtract).then_inc(a_ok, 1)
                    last = n == len(FF_GROUPS) - 1
                    if last:
                        clear_sum(r, (norm_mm, r))
                    down(m, c0, jd, r, last, 0.5)

            dve.memset(acc[:, :], 0.0).then_inc(acc_ok, 1)
            dve.wait_ge(vec_mm, 1)
            own.add(dve.tensor_copy(vec_a[:, :], aux[0][:, 0:P]))
            one(dve.tensor_copy(vec_b[:, :], aux[0][:, P:P + 6 * KT]))
            one(dve.tensor_tensor(lbs[:, 0], lbt[:, :, 0, :], lbt[:, :, 1, :], ALU.max))
            for q in range(2):
                ins = dve.tensor_tensor(lbs[:, 1 + q], lbt[:, :, q, :], lbs[:, 0], ALU.subtract)
                if q == 0:
                    own.add(ins)
            ins.then_inc(lb_sub, 1)
            dve.wait_ge(lb_exp, 2)
            own.add(dve.tensor_scalar(aneg[:, :], aneg[:, :], -1.0, None, ALU.mult))
            one(dve.tensor_tensor(lbs[:, 3], lbs[:, 1], lbs[:, 2], ALU.add))
            one(dve.reciprocal(lbs[:, 3], lbs[:, 3]))
            one(dve.tensor_tensor(lb[:, :, :], lbs[:, 1], lbs[:, 3], ALU.mult))
            dve.tensor_scalar(oml[:, :, :], lb[:, :, :], -1.0, 1.0, ALU.mult, ALU.add).then_inc(vec_ok, 1)
            dve.wait_ge(vec_ok, 1)
            for n, (_, _, k, t) in enumerate(X_TILES):
                dve.wait_ge(x_mm, n + 1)
                dve.tensor_copy(f1["h"][:, :, t:t + k], slot[n % 2][:, :].rearrange("p (t k) -> p t k", k=P)[:, :, 0:k]).then_inc(x_ok, 1)
            dve.wait_ge(x_ok, len(X_TILES))
            for t in range(KT):
                squares_sum(0, 0, t % 2, t)
            normed(f1["h"], "ffn1", 0, 0, 0)
            ffn(0, f1, 0, 1, 0)
            normed(f1["h"], "mix", 1, 1, 0)

            dx, e, s, s2, poly, dtf, daf = m_dt
            dve.wait_ge(spill_out, 16)
            dve.wait_ge(tmp_ok, 2 * KT)
            dve.wait_ge(dense_done, J_DT + 1)
            dve.tensor_scalar(dx[:, :], slot[J_DT % 2][0:32, PC:], dtb[:, 0:1], None, ALU.add).then_inc(slot_free[J_DT % 2], 1)
            clear_sum(2, (norm_mm, 2))
            for b in range(2):
                dve.memset(m_s["ci"][b][:, :], 0.0).then_inc(z_ok, 1)
            dve.wait_ge(dt_exp, 1)
            one(dve.tensor_scalar(s2[:, :], e[:, :], 2.0, None, ALU.add))
            one(dve.reciprocal(s[:, :], s2[:, :]))
            one(dve.tensor_tensor(s[:, :], e[:, :], s[:, :], ALU.mult))
            one(dve.tensor_tensor(s2[:, :], s[:, :], s[:, :], ALU.mult))
            one(dve.tensor_scalar(poly[:, :], s2[:, :], 1.0 / 15, None, ALU.mult))
            for k in range(13, 1, -2):
                one(dve.scalar_tensor_tensor(poly[:, :], poly[:, :], 1.0 / k, s2[:, :], ALU.add, ALU.mult))
            one(dve.scalar_tensor_tensor(poly[:, :], poly[:, :], 1.0, s[:, :], ALU.add, ALU.mult))
            one(dve.tensor_scalar(dx[:, :], dx[:, :], 0.0, None, ALU.max))
            dve.scalar_tensor_tensor(dtf[:, :], poly[:, :], 2.0, dx[:, :], ALU.mult, ALU.add).then_inc(dt_ok, 1)
            dve.wait_ge(dt_ok, 1)
            dve.tensor_scalar(daf[:, :], dtf[:, :], aneg[:, 0:1], None, ALU.mult).then_inc(dt_ok, 1)
            dve.wait_ge(dt_mm, 1)
            both = aux[0][:, 0:64 * NC].rearrange("p (c q h) -> p c q h", q=2, h=2 * HEADS)
            flat = lambda v: v.rearrange("p c d h -> p c (d h)")
            dve.tensor_copy(flat(da_t[:, 0:NC]), both[:, :, 1, :]).then_inc(dt_tok, 1)
            dve.tensor_copy(flat(da_t[0:N_META, NC:NC + 1]), aux[0][0:N_META, 64 * NC + 32:64 * NC + 64]).then_inc(dt_tok, 1)
            dve.tensor_copy(flat(dt_t[:, 0:NC]), both[:, :, 0, :]).then_inc(dt_tok, 1)
            dve.tensor_copy(flat(dt_t[0:N_META, NC:NC + 1]), aux[0][0:N_META, 64 * NC:64 * NC + 32]).then_inc(dt_tok, 1)
            dve.wait_ge(dt_tok, 4)
            one(dve.tensor_copy(da_hi[:, :, :, :], da_t[:, 0:NC]))
            own.add(dve.tensor_tensor(da_lo[:, :, :, :], da_t[:, 0:NC], da_hi[:, :, :, :].bitcast(F32), ALU.subtract))
            dve.wait_ge(dt_dec, 3)
            own.add(dve.tensor_tensor(w_t[0:N_META, META, 0, :], w_t[0:N_META, META, 0, :], dt_t[0:N_META, META, 0, :], ALU.mult))
            own.wait()
            dve.tensor_tensor(w_t[:, 0:NC], w_t[:, 0:NC], dt_t[:, 0:NC], ALU.mult).then_inc(dt_all, 1)
            dve.wait_ge(dt_all, 1)

            def wide(v):
                return v.unsqueeze(2).broadcast_to([P, HPG, PD])

            heads4 = lambda v: v.rearrange("p (h q) -> p h q", h=HPG)
            U = len(S_UPD)
            with dve.Fori(0, GROUPS) as g:
                own.enter(g, 9 + 4 * (TAPS - 1) + sum(1 for d, c in S_UPD if c < META and not (d == 1 and c in (1, 5))) + 2)
                s = J_SSD
                dve.wait_ge(ya_ok, lin(0, 2, g))
                dve.wait_ge(co_ok, lin(0, 4, g))
                dve.wait_ge(rl_ok, lin(0, 2 * NC, g))
                dve.wait_ge(xw_ok, lin(0, U, g))
                own.add(dve.tensor_copy(m_s["gw"][:, :, 0:2], cw[:, :, bass.ds(g * 2, 2)]))
                own.add(dve.tensor_copy(m_s["gw"][:, :, 2:3], cw[:, :, bass.ds(g + 8, 1)]))
                own.add(dve.tensor_copy(m_s["gw"][:, :, 3:4], cw[:, :, bass.ds(g + 12, 1)]))
                own.add(dve.tensor_copy(m_s["gd"][:, 0:2], dskip[:, bass.ds(g * 2, 2)]))
                own.add(dve.tensor_copy(m_s["gd"][:, 2:4], norm_w["ssd"][:, bass.ds(g * 2, 2)]))
                own.add(dve.tensor_copy(m_s["gdt"][:, :, :, :], dt_t[:, 0:NC, :, bass.ds(g * HPG, HPG)]))
                own.add(dve.tensor_copy(m_s["gcd"][:, :, :, :], cd_t[:, :, :, bass.ds(g * HPG, HPG)]))
                own.add(dve.tensor_copy(m_s["gah"][:, :, :, :], da_hi[:, :, :, bass.ds(g * HPG, HPG)].bitcast(F32)))
                own.add(dve.tensor_copy(m_s["gal"][:, :, :, :], da_lo[:, :, :, bass.ds(g * HPG, HPG)].bitcast(F32)))
                dve.tensor_copy(m_s["gw_t"][:, 0:NC, :, :], w_t[:, 0:NC, :, bass.ds(g * HPG, HPG)]).then_inc(gat_ok, 1)
                dve.tensor_copy(m_s["gw_t"][0:N_META, META, 0, :], w_t[0:N_META, META, 0, bass.ds(g * HPG, HPG)]).then_inc(gat_ok, 1)
                own.wait()
                ca = m_s["ca"]
                for c in range(4):
                    dve.wait_ge(slot_free[(s + c) % 2], lin((s + c) // 2 + 1, 3, g))
                    dve.wait_ge(co_ok, lin(c, 4, g))
                    ci = m_s["ci"][c % 2]
                    one(dve.tensor_scalar(ca[:, :], ci[:, 0:CO], m_s["gw"][:, 0, c:c + 1], None, ALU.mult))
                    for k in range(1, TAPS):
                        ins = dve.scalar_tensor_tensor(ca[:, :], ci[:, k:k + CO], m_s["gw"][:, k, c:c + 1], ca[:, :], ALU.mult, ALU.add)
                        if k < TAPS - 1:
                            one(ins)
                    ins.then_inc(conv_ok, 1)
                prev = m_s["prev"]
                for n, (d, c) in enumerate(S_UPD):
                    up = aux[2 + n % 2][:, 0:2 * P]
                    if c >= META or (d == 1 and c in (CP - 1, NC - 1)):
                        dst = prev[d][:, 0 if c == META else CP if c > META else c - 1, :]
                        dve.wait_ge(up_mm, lin(n + 1, U, g))
                        dve.tensor_copy(dst, up).then_inc(up_ok, 1)
                    else:
                        dst = prev[d][:, c + 1 if d == 0 else c - 1, :]
                        dve.wait_ge(up_ok, lin(n, U, g))
                        dve.wait_ge(up_mm, lin(n, U, g))
                        one(dve.tensor_tensor(heads4(dst), heads4(prev[d][:, c, :]), wide(m_s["gcd"][:, c, d, :]), ALU.mult))
                        dve.wait_ge(up_mm, lin(n + 1, U, g))
                        dve.tensor_tensor(dst, dst, up, ALU.add).then_inc(up_ok, 1)

                def decays(c):
                    for d in range(2):
                        if c >= 1:
                            dve.wait_ge(seg_mm, lin(4 * (c - 1) + 2 * d + 2, 4 * NC, g))
                        dve.tensor_tensor(m_s["rh"][d][:, :, :], incl[d][:, :].unsqueeze(1).broadcast_to([P, HPG, P]),
                                          m_s["gah"][:, c, d, :].unsqueeze(2).broadcast_to([P, HPG, P]), ALU.mult).then_inc(rh_ok, 1)

                def y_out(c):
                    dve.wait_ge(y_mm, lin(c + 1, NC, g))
                    for q in range(2):
                        dve.scalar_tensor_tensor(ys[q][:, P * c:P * (c + 1)], m_s["co"][q][:, CO_CHUNK[c]:CO_CHUNK[c] + P],
                                                 m_s["gd"][:, q:q + 1], aux[3][:, P * q:P * (q + 1)], ALU.mult, ALU.add).then_inc(y_ok, 1)

                decays(0)
                for c in range(NC):
                    b = c % 2
                    if c + 1 < NC:
                        decays(c + 1)
                    if c >= 2:
                        dve.wait_ge(y_mm, lin(c - 1, NC, g))
                    for d in range(2):
                        dve.tensor_tensor(heads4(m_s["xdt"][b][d][:, :]), heads4(m_s["xbt"][:, c + 2, 0:2 * P]), wide(m_s["gdt"][:, c, d, :]),
                                          ALU.mult).then_inc(xdt_ok, 1)
                    dve.wait_ge(cb_mm, lin(c + 1, NC, g))
                    for d in range(2):
                        dve.tensor_tensor(m_s["cb"][b][d][:, :], aux[2][:, 0:P], incl[d][:, :], ALU.mult).then_inc(cbm_ok, 1)
                    for d in range(2):
                        dve.wait_ge(exp_ok, lin(4 * c + 2 * d + 1, 4 * NC, g))
                        dve.wait_ge(cbm_ok, lin(2 * c + d + 1, 2 * NC, g))
                        v = m_s["e"][b][d][:, :, :]
                        dve.tensor_tensor(v, v, m_s["cb"][b][d][:, :].unsqueeze(1).broadcast_to([P, HPG, P]), ALU.mult).then_inc(wy_ok, 1)
                    if c >= 1:
                        y_out(c - 1)
                y_out(NC - 1)
                dve.wait_ge(y_ok, lin(2 * NC, 2 * NC, g))
                for q in range(2):
                    dve.wait_ge(slot_free[(s + 4 + q) % 2], lin((s + 4 + q) // 2 + 1, 3, g))
                    dve.tensor_tensor(ys[q], ys[q], zs[q], ALU.mult).then_inc(yz_ok, 1)
                for q in range(2):
                    dve.wait_ge(yz_ok, lin(q + 1, 2, g))
                    one(dve.tensor_tensor(ca[:, 0:NX], ys[q], ys[q], ALU.mult))
                    dve.wait_ge(acc_ok, lin(9 * 2 + 1 + q, 2, g))
                    dve.tensor_tensor(acc[:, N_META:], acc[:, N_META:], ca[:, 0:NX], ALU.add).then_inc(acc_ok, 1)
                    dve.wait_ge(acc_ok, lin(9 * 2 + 2 + q, 2, g))
                    dve.tensor_scalar(m_s["ya"][:, bass.ds(g * 2 + q, 1), :], ys[q], m_s["gd"][:, 2 + q:3 + q], None, ALU.mult).then_inc(ya_ok, 1)
                own.leave(GROUPS)

            def low_parts(m, src, base):
                for t in range(KT):
                    dve.wait_ge(pa_hi, base + t + 1)
                    dve.tensor_tensor(m["lo"][:, t, :], src[:, t, :], m["hi"][:, t, :].bitcast(F32), ALU.subtract).then_inc(pa_lo, 1)

            low_parts(m_a, m_s["ya"], 0)
            dve.wait_ge(rs_ok, 3)
            with dve.Fori(0, KT // 2) as i:
                own.enter(i, 2)
                for c in range(2):
                    j = J_PA + 2 * c
                    dve.wait_ge(slot_free[j % 2], lin(j // 2 + 1, 2, i))
                    one(dve.tensor_tensor(gate[c], gate[c], rs[:, N_META:], ALU.mult))
                    dve.wait_ge(dense_done, lin(j + 2, 4, i))
                    dve.wait_ge(pm_out[c], lin(0, 16, i))
                    dve.tensor_tensor(prod[c], gate[c], slot[(j + 1) % 2][:, PC + N_META:], ALU.mult).then_inc(slot_free[(j + 1) % 2], 1)
                own.leave(KT // 2)

            q_, k_, b_, s_ = m_h["q"], m_h["k"], m_h["b"], m_h["s"]
            main = lambda v: v[:, N_META:N_META + NX].rearrange("p (c t) -> p c t", t=64)
            dve.wait_ge(dense_done, J_HG)
            for v in (m_h["reset"][:, :],):
                one(dve.memset(v, 1.0))
            own.add(dve.memset(m_h["reset"][:, 0:1], 0.0))
            one(dve.memset(m_h["reset"][:, N_META::64], 0.0))
            for v in m_h["am"]:
                for d in range(2):
                    own.add(dve.memset(v[d][:, :], 0.0))
            own.wait()

            def hg_chain(j, i=None):
                a = j % 2
                w = lambda sem_, v, n: dve.wait_ge(sem_, lin(v, 2 * n, i))
                t = j if i is None else bass.ds(i * 2 + j, 1)
                t = slice(j, j + 1) if i is None else t
                if j:
                    w(k_ok, 4 * j, 4)
                for d in range(2):
                    own.add(dve.tensor_copy(m_h["lo"][:, d, 0:1], oml[:, d, t]))
                    own.add(dve.tensor_copy(m_h["lo"][:, d, 1:2], lb[:, d, t]))
                own.wait()
                for d in range(2):
                    jj = J_HG + 5 * j + d
                    f, c0 = s_[a][d], N_META * d
                    dve.wait_ge(slot_free[jj % 2], lin(jj // 2 + 1, 5, i))
                    one(dve.tensor_scalar(f[:, c0:], f[:, c0:], m_h["lo"][:, d, 0:1], m_h["lo"][:, d, 1:2], ALU.mult, ALU.add))
                    if j or d:
                        w(k_ok, 2 * (2 * j + d), 4)
                    dve.tensor_scalar(k_[:, c0:], f[:, c0:], -1.0, 1.0, ALU.mult, ALU.add).then_inc(f_ok, 1)
                    w(ln_ok, 2 * j + d + 1, 2)
                    if d == 0:
                        o, r, l = b_[:, :], m_h["reset"][:, 0:NT], f[:, :]
                    else:
                        o, r, l = b_[:, N_META:][:, ::-1], m_h["reset"][:, N_META + 1:][:, ::-1], f[:, N_META:][:, ::-1]
                    dve.tensor_tensor_scan(o, r, l, 0.0, ALU.mult, ALU.add).then_inc(bc_ok, 1)
                    w(bc_ok, 2 * j + d + 1, 2)
                    if j or d:
                        w(e_ok, 4 * (2 * j + d) - 1, 8)
                    mid, end = (32, 63) if d == 0 else (31, 0)
                    dve.tensor_tensor(main(dif), main(b_), main(b_)[:, :, mid:mid + 1].broadcast_to([P, 2 * NC, 64]),
                                      ALU.subtract).then_inc(d_ok, 1)
                    if d == 0:
                        own.add(dve.tensor_tensor(f[:, 0:N_META], b_[:, N_META - 1:N_META].broadcast_to([P, N_META]), b_[:, 0:N_META],
                                                  ALU.subtract))
                    dve.tensor_tensor(main(f), main(b_)[:, :, end:end + 1].broadcast_to([P, 2 * NC, 64]), main(b_),
                                      ALU.subtract).then_inc(d_ok, 1)
                    w(e_ok, 4 * (2 * j + d) + 1, 8)
                    dve.tensor_copy(m_h["dec"][d][:, :], main(q_[d][0])[:, :, end]).then_inc(dec_ok, 1)
                    w(e_ok, 4 * (2 * j + d) + 3, 8)
                    w(f_ok, 2 * j + d + 1, 2)
                    dve.tensor_tensor(q_[d][2][:, N_META:], q_[d][2][:, N_META:], k_[:, N_META:], ALU.mult).then_inc(k_ok, 1)
                    w(e_ok, 4 * (2 * j + d) + 4, 8)
                    dve.tensor_tensor(q_[d][3][:, c0:], q_[d][3][:, c0:], k_[:, c0:], ALU.mult).then_inc(k_ok, 1)

            def hg_scan(j, i=None):
                a = j % 2
                w = lambda sem_, v, n: dve.wait_ge(sem_, lin(v, 2 * n, i))
                U, prev, dec = len(H_UPD), m_h["prev"], m_h["dec"]
                t = slice(j, j + 1) if i is None else bass.ds(i * 2 + j, 1)
                w(yb_ok, j, 1)
                own.add(dve.tensor_copy(m_h["nw"][:, :], norm_w["hg"][:, t]))
                w(dec_ok, 2 * (j + 1), 2)
                for u, q, (d, c) in ((u, q, v) for u, bank in enumerate(H_BANKS) for q, v in enumerate(bank)):
                    up = aux[u % 2][:, P * q:P * (q + 1)]
                    w(kv_mm, len(H_BANKS) * j + u + 1, len(H_BANKS))
                    if c < 0:
                        own.add(dve.tensor_copy(prev[0][:, 0, :], up))
                        ins = dve.tensor_copy(prev[0][:, 2 * CP, :], up)
                    elif d == 1 and c in (2 * CP - 1, 2 * NC - 1):
                        ins = dve.tensor_copy(prev[1][:, c - 1, :], up)
                    else:
                        before = (0, -1) if d == 0 and c in (0, 2 * CP) else (d, c - 1 if d == 0 else c + 1)
                        w(kv_ok, U * j + H_UPD.index(before) + 1, U)
                        ins = dve.scalar_tensor_tensor(prev[d][:, c + 1 if d == 0 else c - 1, :], prev[d][:, c, :], dec[d][:, c:c + 1], up,
                                                       ALU.mult, ALU.add)
                    ins.then_inc(kv_ok, 1)
                for p in range(NC):
                    dve.wait_ge(const_ok, 1)
                    w(a_mm, NC * j + p + 1, NC)
                    if p >= 2:
                        w(o_mm, NC * j + p - 1, NC)
                    own.add(dve.tensor_copy(m_h["turn"][:, p:p + 1], ones[:, 0:1]))
                    for d in range(2):
                        dve.copy_predicated(m_h["am"][p % 2][d][:, :], incl64[d][:, :].bitcast(I32), aux[p % 2][:, P * d:P * (d + 1)]).then_inc(am_ok, 1)
                own.wait()
                w(ors_ok, j + 1, 1)
                yj = m_h["yb"][:, j, :] if i is None else m_h["yb"][:, bass.ds(i * 2 + j, 1), :]
                one(dve.scalar_tensor_tensor(yj, aux2[1][:, PC + N_META:], m_h["nw"][:, 0:1], osq, ALU.mult, ALU.mult))
                jj = J_HG + 5 * j + 4
                dve.wait_ge(slot_free[jj % 2], lin(jj // 2 + 1, 5, i))
                dve.tensor_tensor(yj, yj, hg[a], ALU.mult).then_inc(yb_ok, 1)

            hg_chain(0)
            with dve.Fori(0, HH // 2 - 1) as i:
                own.enter(i, 2 * (4 + 2 + 1 + 3 + NC))
                hg_scan(0, i)
                hg_chain(1, i)
                hg_scan(1, i)
                hg_chain(2, i)
                own.leave(HH // 2 - 1)
            hg_scan(HH - 2)
            hg_chain(HH - 1)
            hg_scan(HH - 1)

            low_parts(m_b, m_h["yb"], KT)
            with dve.Fori(0, KT // 2) as i:
                for c in range(2):
                    j = J_PB + 2 * c
                    dve.wait_ge(slot_free[j % 2], lin(j // 2 + 1, 2, i))
                    dve.wait_ge(dense_done, lin(j + 2, 4, i))
                    dve.wait_ge(ml_ok, lin(c, 2, i))
                    dve.tensor_tensor(prod[c], gate[c], slot[(j + 1) % 2][:, PC + N_META:], ALU.mult).then_inc(slot_free[(j + 1) % 2], 1)
                    dve.wait_ge(slot_free[(j + 1) % 2], lin((j + 1) // 2 + 1, 2, i))
                    dve.wait_ge(m_in[c], lin(16, 16, i))
                    dve.tensor_tensor(prod[c], prod[c], back[c], ALU.add).then_inc(mg_ok, 1)
                    dve.wait_ge(mg_ok, lin(c + 1, 2, i))
                    dve.wait_ge(mh_ok, lin(c + 1, 2, i))
                    t = bass.ds(i * 2 + c, 1)
                    dve.tensor_tensor(m_b["ml"][:, t, :], prod[c], m_b["mh"][:, t, :].bitcast(F32), ALU.subtract).then_inc(ml_ok, 1)
            clear_sum(3, (mg_ok, KT))
            dve.wait_ge(spill_in, 16)
            down(f2, N_META, J_WO, 3, True, 1.0)
            normed(f2["h"], "ffn2", 3, 2, N_META)
            ffn(J_FF2, f2, N_META, 4, D_FF // P)
            dve.wait_ge(rs_ok, 5)
            for t in range(KT):
                h = f2["h"][:, t, N_META:]
                dve.scalar_tensor_tensor(h, h, norm_w["final"][:, t:t + 1], rs[:, N_META:], ALU.mult, ALU.mult).then_inc(tmp_ok, 1)
            for c in range(0, NC, 2):
                dve.wait_ge(out_mm, c + 1)
                dve.wait_ge(out_ok, c)
                if c >= 2:
                    dve.wait_ge(out_done[c % 2], 16 * (c // 2))
                dve.tensor_copy(f2["io"][c % 2][:, :], slot[c % 2][:, :]).then_inc(out_ok, 1)

        @block.gpsimd
        def _(pool):
            own = Tally(pool, pool_step)

            def low(s, n=0, i=None):
                pool.wait_ge(w_hi, lin(s + 1, n, i))
                pool.tensor_tensor(wlo[s % 2][:, :, :], raw[s % 2][:, :, :], whi[s % 2][:, :, :].bitcast(F32), ALU.subtract).then_inc(w_lo, 1)

            pool.memset(ident[:, :], 0.0)
            pool.memset(ones[:, :], 1.0)
            pool.memset(ones_r[:, :].bitcast(F32), 1.0)
            pool.memset(eps[:, :], EPS)
            own.add(pool.memset(incl[0][:, :], 1.0))
            own.wait()
            sel = lambda out, fill, op, mult, step, base: own.add(pool.affine_select(
                out=out, in_=out, compare_op=op, fill=fill, base=base, pattern=[[step, P]], channel_multiplier=mult))
            own.wait()
            sel(ident[:, :], 1.0, ALU.not_equal, 1, -1, 0)
            for d in range(2):
                sg = 1 - 2 * d
                src = ones[:, :]
                own.add(pool.affine_select(out=strict[d][:, :], in_=src, compare_op=ALU.is_gt, fill=0.0, base=0,
                                           pattern=[[-sg, P]], channel_multiplier=sg))
                own.add(pool.affine_select(out=incl[d][:, :], in_=src, compare_op=ALU.is_ge, fill=0.0, base=0,
                                           pattern=[[sg, P]], channel_multiplier=-sg))
                own.add(pool.affine_select(out=incl64[d][:, :], in_=src, compare_op=ALU.is_ge, fill=0.0, base=0,
                                           pattern=[[sg, P]], channel_multiplier=-sg))
            own.wait()
            own.add(pool.memset(incl64[0][0:64, 64:P], 0.0))
            own.add(pool.memset(incl64[1][64:P, 0:64], 0.0))
            own.wait()
            pool.memset(eps[:, :], EPS).then_inc(const_ok, 1)

            def lows(s, count):
                with pool.Fori(0, count // 2) as i:
                    low(s, 2, i)
                    low(s + 1, 2, i)
                if count % 2:
                    low(s + count - 1)

            def normed(q, c0):
                for t in range(KT):
                    pool.wait_ge(xh_ok, KT * q + t + 1)
                    pool.tensor_tensor(xl[:, t, c0:], tmp[t % 2][:, c0:], xh[:, t, c0:].bitcast(F32), ALU.subtract).then_inc(xn_ok, 1)

            low(0)
            normed(0, 0)
            lows(1, J_DT)
            for b in range(2):
                pool.wait_ge(slot_free[(J_DT - 1 - b) % 2], (J_DT - 1 - b) // 2 + 1)
            pool.dma_start(h_spill, f1["h"][:, :, N_META:]).then_inc(spill_out, 16)
            normed(1, 0)
            low(J_DT + 1)

            U = len(S_UPD)

            def ssd_scan(g):
                pool.wait_ge(gat_ok, lin(2, 2, g))
                for n, (d, c) in enumerate(S_UPD):
                    q, k, m = (c - META, N_META, META) if c >= META else (c + 2, P, c)
                    pool.wait_ge(tr_ok, lin(NC + 2 if n else 2, NC + 2, g))
                    if n >= 2:
                        pool.wait_ge(up_mm, lin(n - 1, U, g))
                    h4 = lambda v: v.rearrange("p (h q) -> p h q", h=HPG)
                    pool.tensor_tensor(h4(m_s["xw"][n % 2][0:k, :]), h4(m_s["xbt"][0:k, q, 0:2 * P]),
                                       m_s["gw_t"][0:k, m, d, :].unsqueeze(2).broadcast_to([k, HPG, PD]), ALU.mult).then_inc(xw_ok, 1)

                def decays(c):
                    for d in range(2):
                        if c >= 1:
                            pool.wait_ge(seg_mm, lin(4 * (c - 1) + 2 * d + 2, 4 * NC, g))
                        pool.tensor_tensor(m_s["rl"][d][:, :, :], incl[d][:, :].unsqueeze(1).broadcast_to([P, HPG, P]),
                                           m_s["gal"][:, c, d, :].unsqueeze(2).broadcast_to([P, HPG, P]), ALU.mult).then_inc(rl_ok, 1)

                decays(0)
                for c in range(NC):
                    if c + 1 < NC:
                        decays(c + 1)
                    for d in range(2):
                        pool.wait_ge(exp_ok, lin(4 * c + 2 * d + 2, 4 * NC, g))
                        v = m_s["ea"][c % 2][d][:, :, :]
                        pool.tensor_tensor(v, v, m_s["co"][3][:, CO_CHUNK[c]:CO_CHUNK[c] + P].unsqueeze(1).broadcast_to([P, HPG, P]),
                                           ALU.mult).then_inc(ch_ok, 1)

            for c in range(6):
                low(J_SSD + c + 1)
            with pool.Fori(0, GROUPS - 1) as g:
                ssd_scan(g)
                for c in range(6):
                    low(J_SSD + 7 + c, 6, g)
            ssd_scan(GROUPS - 1)

            with pool.Fori(0, KT // 2) as i:
                for c in range(2):
                    j = J_PA + 2 * c
                    low(j + 1, 4, i)
                    low(j + 2, 4, i)
                    pool.wait_ge(slot_free[(j + 1) % 2], lin((j + 1) // 2 + 1, 2, i))
                    pool.dma_start(m_spill[bass.ds(i * 2 + c, 1)].rearrange("a p n -> p (a n)"), prod[c]).then_inc(pm_out[c], 16)

            def hg_queries(j, d, i=None):
                a = j % 2
                w = lambda sem_, v, n: pool.wait_ge(sem_, lin(v, 2 * n, i))
                w(dec_ok, 2 * j + d + 1, 2)
                w(e_ok, 4 * (2 * j + d) + 2, 8)
                for c in range(2):
                    v = m_h["q"][d][c][:, N_META:]
                    pool.tensor_tensor(v, v, hq[a], ALU.mult).then_inc(q_ok, 1)

            def hg_dense(j, i=None):
                s = J_HG + 5 * j
                for c in range(5):
                    low(s + c + 1, 10, i)
                    if c in (1, 3):
                        hg_queries(j - 1, c // 2, i)

            lows(J_HG + 1, 5)
            with pool.Fori(0, HH // 2 - 1) as i:
                hg_dense(1, i)
                hg_dense(2, i)
            hg_dense(HH - 1)
            hg_queries(HH - 1, 0)
            hg_queries(HH - 1, 1)

            pool.wait_ge(yb_ok, HH)
            with pool.Fori(0, KT // 2) as i:
                for c in range(2):
                    j = J_PB + 2 * c
                    if c == 0:
                        pool.wait_ge(mg_ok, lin(0, 2, i))
                        for b in range(2):
                            pool.dma_start(back[b], m_spill[bass.ds(i * 2 + b, 1)].rearrange("a p n -> p (a n)")).then_inc(m_in[b], 16)
                    low(j + 1, 4, i)
                    low(j + 2, 4, i)
            pool.wait_ge(dense_done, J_WO)
            pool.dma_start(f2["h"][:, :, N_META:], h_spill).then_inc(spill_in, 16)
            lows(J_WO + 1, KT)
            normed(2, N_META)
            lows(J_FF2 + 1, FFN_JOBS - 1)


_INS = ["x_prompt", "x_sample", "meta_tokens", "ffn1_norm", "ffn1_w_gate_up", "ffn1_w_down", "mix_norm", "w_in",
        "ssd_conv_w", "ssd_conv_b", "ssd_dt_bias", "ssd_a_log", "ssd_d", "ssd_norm", "ssd_w_proj", "hg_lb_table",
        "hg_norm", "hg_w_proj", "w_out", "ffn2_norm", "ffn2_w_gate_up", "ffn2_w_down", "final_norm"]
_OUTS = [(1, 256, 1024), (1, 512, 1024)]


def kernel(**inputs):
    import numpy as _np
    import concourse.bacc as _bacc
    from concourse import mybir as _mybir
    from concourse.bass_utils import run_bass_kernel_spmd as _run

    nc = _bacc.Bacc("TRN2", target_bir_lowering=False, num_devices=1)
    arrays, args = {}, []
    for name in _INS:
        a = _np.ascontiguousarray(inputs[name])
        arrays[f"in_{name}"] = a
        args.append(nc.dram_tensor(f"in_{name}", a.shape, _mybir.dt.from_np(a.dtype), kind="ExternalInput").ap())
    for n, shape in enumerate(_OUTS):
        args.append(nc.dram_tensor(f"out_{n}", shape, _mybir.dt.float32, kind="ExternalOutput").ap())
    build(nc, *args)
    r = _run(nc, [arrays], core_ids=[0])
    return tuple(_np.asarray(r.results[0][f"out_{n}"]) for n in range(len(_OUTS)))
```

```python
from contextlib import ExitStack

import concourse.bass as bass
from concourse import mybir

P = 128
F32 = mybir.dt.float32
F32R = mybir.dt.float32r
I32 = mybir.dt.int32
ALU = mybir.AluOpType
ACT = mybir.ActivationFunctionType

D = 1024
KT = D // P
D_FF = 2816
N_META, N_P, N_S = 16, 256, 512
NT = N_META + N_P + N_S
NX = N_P + N_S
HEADS, GROUPS, HPG, STATE, PD = 16, 4, 4, 128, 64
TAPS = 5
HH = 8
EPS = 1e-6
BANK = 512
PC = 2 * BANK - NT
SPLIT = NT - BANK
Z0, X0, B0, C0, DT0 = 0, D, 2 * D, 2 * D + 512, 3 * D
HQ0 = DT0 + 2 * HEADS
HF0, HI0, HG0, GA0 = HQ0 + D, HQ0 + 3 * D, HQ0 + 4 * D, HQ0 + 5 * D
FF_GROUPS = [(0, 8), (8, 7), (15, 7)]
assert FF_GROUPS[-1][0] + FF_GROUPS[-1][1] == D_FF // P
CI = 2 + N_META + N_P + 2 + N_META + N_S + 2
CO = CI - (TAPS - 1)
CO_META = [0, N_META + N_P + 2]
NC = NX // P
CP = N_P // P
CO_CHUNK = [N_META + P * c + (0 if c < CP else 2 + N_META) for c in range(NC)]
META = NC

FFN_JOBS = sum(2 * n + KT for _, n in FF_GROUPS)
J_DT = FFN_JOBS
J_SSD = J_DT + 1
J_PA = J_SSD + 6 * GROUPS
J_HG = J_PA + 2 * KT
J_PB = J_HG + 5 * HH
J_WO = J_PB + 2 * KT
J_FF2 = J_WO + KT
JOBS = J_FF2 + FFN_JOBS


def lin(s, n=0, i=None):
    return s if i is None else i * n + s


def halves(c0):
    return ((c0, SPLIT), (SPLIT, NT))


class Tally:

    def __init__(self, eng, sem):
        self.eng, self.sem, self.n, self.stride, self.i, self.start = eng, sem, 0, 0, None, 0

    def add(self, ins):
        ins.then_inc(self.sem, 1)
        self.n += 1

    def wait(self, back=0):
        self.eng.wait_ge(self.sem, lin(self.n - back, self.stride, self.i))

    def enter(self, i, stride):
        self.i, self.stride, self.start = i, stride, self.n

    def leave(self, trips):
        assert self.n - self.start == self.stride, (self.n - self.start, self.stride)
        self.n = self.start + self.stride * trips
        self.i, self.stride = None, 0


def build(nc, x_prompt, x_sample, meta_tokens, ffn1_norm, ffn1_w_gate_up, ffn1_w_down, mix_norm, w_in,
          ssd_conv_w, ssd_conv_b, ssd_dt_bias, ssd_a_log, ssd_d, ssd_norm, ssd_w_proj, hg_lb_table,
          hg_norm, hg_w_proj, w_out, ffn2_norm, ffn2_w_gate_up, ffn2_w_down, final_norm, y_prompt, y_sample):
    ctx = ExitStack()
    with ctx:
        def sb(name, shape, dt=F32, where=ctx):
            return where.enter_context(nc.sbuf_tensor(name, shape, dt))

        def sem(name):
            return ctx.enter_context(nc.semaphore(name))

        xh = sb("xh", [P, KT, NT], F32R)
        xl = sb("xl", [P, KT, NT], F32R)
        raw = [sb(f"raw{s}", [P, KT, P]) for s in range(2)]
        whi = [sb(f"whi{s}", [P, KT, P], F32R) for s in range(2)]
        wlo = [sb(f"wlo{s}", [P, KT, P], F32R) for s in range(2)]
        vec_a = sb("vec_a", [P, P])
        vec_b = sb("vec_b", [P, 6 * KT])
        ident = sb("ident", [P, P])
        ones = sb("ones", [P, P])
        ones_r = sb("ones_r", [P, P], F32R)
        strict = [sb(f"strict{d}", [P, P], F32R) for d in range(2)]
        incl = [sb(f"incl{d}", [P, P]) for d in range(2)]
        incl64 = [sb(f"incl64{d}", [P, P]) for d in range(2)]
        eps = sb("eps", [P, 1])
        lb = sb("lb", [P, 2, KT])
        oml = sb("oml", [P, 2, KT])
        lbs = sb("lbs", [P, 4, 2, KT])
        dskip = sb("dskip", [P, KT])
        dtb = sb("dtb", [2 * HEADS, 1])
        alog = sb("alog", [2 * HEADS, 1])
        aneg = sb("aneg", [2 * HEADS, 1])
        dt_t = sb("dt_t", [P, NC + 1, 2, HEADS])
        da_t = sb("da_t", [P, NC + 1, 2, HEADS])
        da_hi = sb("da_hi", [P, NC, 2, HEADS], F32R)
        da_lo = sb("da_lo", [P, NC, 2, HEADS], F32R)
        w_t = sb("w_t", [P, NC + 1, 2, HEADS])
        cd_t = sb("cd_t", [P, NC, 2, HEADS])
        acc = sb("acc", [P, NT])
        sq = [sb(f"sq{s}", [P, NT]) for s in range(2)]
        rs = sb("rs", [P, NT])
        tmp = [sb(f"tmp{s}", [P, NT]) for s in range(2)]

        cw = vec_a[:, 0:(TAPS + 1) * 16].rearrange("p (k t) -> p k t", t=16)
        lbt = vec_a[:, 96:128].rearrange("p (d l t) -> p d l t", d=2, l=2)
        norm_w = {n: vec_b[:, KT * k:KT * (k + 1)] for k, n in enumerate(["ffn1", "mix", "ssd", "hg", "ffn2", "final"])}

        def scope(make):
            with ExitStack() as s:
                return make(lambda name, shape, dt=F32: sb(name, shape, dt, s))

        def ffn_mem(new, t):
            return dict(h=new(f"h{t}", [P, KT, NT]), t=new(f"gate{t}", [P, NT]), p=new(f"prod{t}", [P, NT]),
                        ah=new(f"ah{t}", [P, 8, NT], F32R), al=new(f"al{t}", [P, 8, NT], F32R),
                        io=[new(f"io{t}_{s}", [P, D]) for s in range(2)],
                        va=new(f"va{t}", [P, P]), vb=new(f"vb{t}", [6 * KT, P]))

        f1 = scope(lambda new: ffn_mem(new, 1))
        f2 = scope(lambda new: ffn_mem(new, 2))
        m_dt = scope(lambda new: [new(f"dtw{k}", [2 * HEADS, NT]) for k in range(7)])
        m_s = scope(lambda new: dict(
            ya=new("ya", [P, KT, NX]), _pad=new("pad_s", [P, KT * N_META]),
            ci=[new(f"ci{s}", [P, CI]) for s in range(2)], ca=new("ca", [P, CO]),
            co=[new(f"co{s}", [P, CO]) for s in range(4)], gw=new("gw", [P, TAPS + 1, 4]), gd=new("gd", [P, 4]),
            gdt=new("gdt", [P, NC, 2, HPG]), gw_t=new("gw_t", [P, NC + 1, 2, HPG]), gcd=new("gcd", [P, NC, 2, HPG]),
            gah=new("gah", [P, NC, 2, HPG]), gal=new("gal", [P, NC, 2, HPG]),
            xbt=new("xbt", [P, NC + 2, 3 * P]), xw=[new(f"xw{s}", [P, 2 * P]) for s in range(2)],
            xdt=[[new(f"xdt{s}{d}", [P, 2 * P]) for d in range(2)] for s in range(2)],
            prev=[new(f"prev{d}", [P, NC, 2 * P]) for d in range(2)],
            rh=[new(f"rh{d}", [P, HPG, P], F32R) for d in range(2)],
            rl=[new(f"rl{d}", [P, HPG, P], F32R) for d in range(2)],
            e=[[new(f"e{s}{d}", [P, HPG, P]) for d in range(2)] for s in range(2)],
            ea=[[new(f"ea{s}{d}", [P, HPG, P]) for d in range(2)] for s in range(2)],
            cb=[[new(f"cb{s}{d}", [P, P]) for d in range(2)] for s in range(2)]))
        m_a = scope(lambda new: dict(lo=new("ya_lo", [P, KT, NX], F32R), _pad=new("pad_a", [P, KT * N_META]),
                                     hi=new("ya_hi", [P, KT, NX], F32R)))
        m_h = scope(lambda new: dict(
            yb=new("yb", [P, KT, NX]), _pad=new("pad_h", [P, KT * N_META]),
            s=[[new(f"s{a}{d}", [P, NT]) for d in range(2)] for a in range(2)],
            v=[new(f"v{a}", [P, NT]) for a in range(2)], k=new("k", [P, NT]), b=new("b", [P, NT]),
            q=[[new(f"q{c}{d}", [P, NT]) for c in range(4)] for d in range(2)],
            reset=new("reset", [P, NT + 1]), dec=[new(f"dec{d}", [P, 2 * NC]) for d in range(2)],
            lo=new("hlo", [P, 2, 2]), nw=new("hnw", [P, 1]), turn=new("turn", [P, NC]),
            vt=new("vt", [P, NC + 1, P]), kt=[new(f"kt{d}", [P, NC + 1, P]) for d in range(2)],
            prev=[new(f"hprev{d}", [P, 2 * NC, P]) for d in range(2)],
            am=[[new(f"am{s}{d}", [P, P]) for d in range(2)] for s in range(2)]))
        m_b = scope(lambda new: dict(lo=new("yb_lo", [P, KT, NX], F32R), _pad=new("pad_b", [P, KT * N_META]),
                                     hi=new("yb_hi", [P, KT, NX], F32R), mh=new("mh", [P, KT, NX], F32R),
                                     ml=new("ml", [P, KT, NX], F32R)))
        zs, ys = [v[:, 0:NX] for v in sq], [v[:, 0:NX] for v in tmp]
        gate, prod = zs, ys
        back = [v[:, 0:NX] for v in (rs, acc)]
        hg, hq = zs, ys
        dif, osq = rs, acc[:, 0:NX]

        slot = [ctx.enter_context(nc.psum_tensor(f"slot{s}", [P, 2 * BANK], F32)) for s in range(2)]
        aux2 = [ctx.enter_context(nc.psum_tensor(f"aux{s}", [P, 2 * BANK], F32)) for s in range(2)]
        aux = [aux2[b // 2][:, BANK * (b % 2):BANK * (b % 2 + 1)] for b in range(4)]

        h_spill = nc.dram_tensor("h_spill", (P, KT, NX), F32, kind="Internal").ap()
        m_spill = nc.dram_tensor("m_spill", (KT, P, NX), F32, kind="Internal").ap()

        vec_in = sem("vec_in")
        const_ok = sem("const_ok")
        vec_mm = sem("vec_mm")
        lb_sub, lb_exp, dec_ok = sem("lb_sub"), sem("lb_exp"), sem("dec_ok")
        vec_ok = sem("vec_ok")
        x_in = [sem(f"x_in{s}") for s in range(2)]
        x_mm = sem("x_mm")
        x_ok = sem("x_ok")
        raw_in = [sem(f"raw_in{s}") for s in range(2)]
        w_hi, w_lo = sem("w_hi"), sem("w_lo")
        dense_done = sem("dense_done")
        slot_free = [sem(f"slot_free{s}") for s in range(2)]
        a_hi_ok, a_ok = sem("a_hi_ok"), sem("a_ok")
        sq_ok, acc_ok = sem("sq_ok"), sem("acc_ok")
        norm_mm, rs_ln, rs_ok = sem("norm_mm"), sem("rs_ln"), sem("rs_ok")
        tmp_ok, xh_ok, xn_ok = sem("tmp_ok"), sem("xh_ok"), sem("xn_ok")
        spill_out, spill_in = sem("spill_out"), sem("spill_in")
        dve_step = sem("dve_step")
        act_step = sem("act_step")
        pool_step = sem("pool_step")
        dt_abs, dt_exp, dt_ok = sem("dt_abs"), sem("dt_exp"), sem("dt_ok")
        dt_mm, dt_tok, dt_sum, dt_dec, dt_all = sem("dt_mm"), sem("dt_tok"), sem("dt_sum"), sem("dt_dec"), sem("dt_all")
        conv_ok, co_ok = sem("conv_ok"), sem("co_ok")
        tr_mm, tr_ok, xw_ok, up_mm, up_ok = sem("tr_mm"), sem("tr_ok"), sem("xw_ok"), sem("up_mm"), sem("up_ok")
        gat_ok = sem("gat_ok")
        rh_ok, rl_ok, seg_mm, cb_mm, exp_ok = sem("rh_ok"), sem("rl_ok"), sem("seg_mm"), sem("cb_mm"), sem("exp_ok")
        cbm_ok, wy_ok, ch_ok, xdt_ok, y_mm, y_ok = (sem(n) for n in ("cbm_ok", "wy_ok", "ch_ok", "xdt_ok", "y_mm", "y_ok"))
        yz_ok, ya_ok = sem("yz_ok"), sem("ya_ok")
        pa_hi, pa_lo, pg_ok, pg2_ok, pm_ok, pm_out = (sem(n) for n in ("pa_hi", "pa_lo", "pg_ok", "pg2_ok", "pm_ok", "pm_out"))
        pm_out = [pm_out, sem("pm_out1")]
        z_ok = sem("z_ok")
        f_ok, ln_ok, bc_ok, d_ok, e_ok, k_ok, q_ok = (sem(n) for n in ("f_ok", "ln_ok", "bc_ok", "d_ok", "e_ok", "k_ok", "q_ok"))
        ht_mm, ht_ok, kv_mm, kv_ok, a_mm, am_ok, o_mm, osq_ok, os_mm, ors_ln, ors_ok, yb_ok = (
            sem(n) for n in ("ht_mm", "ht_ok", "kv_mm", "kv_ok", "a_mm", "am_ok", "o_mm", "osq_ok", "os_mm", "ors_ln", "ors_ok", "yb_ok"))
        m_in = [sem("m_in0"), sem("m_in1")]
        mg_ok, mh_ok, ml_ok = sem("mg_ok"), sem("mh_ok"), sem("ml_ok")
        out_mm, out_ok = sem("out_mm"), sem("out_ok")
        out_done = [sem("out_done0"), sem("out_done1")]

        S_UPD = [(0, META), (0, META + 1), (1, 1), (1, 5), (0, 0), (1, 4), (0, 2), (1, 3), (0, 3), (0, 4)]
        H_BANKS = [[(0, -1)], [(1, 3), (1, 11)], [(0, 0), (0, 4), (1, 2), (1, 10)], [(0, 1), (0, 5), (1, 1), (1, 9)],
                   [(0, 2), (0, 6), (1, 8)], [(0, 7), (1, 7)], [(0, 8), (1, 6)], [(0, 9), (1, 5)], [(0, 10)]]
        H_UPD = [v for b in H_BANKS for v in b]
        H_END = [sum(map(len, H_BANKS[:u + 1])) for u in range(len(H_BANKS))]
        X_TILES = [(meta_tokens, 0, N_META, 0)] + [(x_prompt[0], P * c, P, N_META + P * c) for c in range(CP)] + \
            [(x_sample[0], P * c, P, N_META + N_P + P * c) for c in range(NC - CP)]

        FFNS = [(0, f1, 0, ffn1_w_gate_up[0], ffn1_w_down[0]), (J_FF2, f2, N_META, ffn2_w_gate_up[0], ffn2_w_down[0])]

        def ffn_groups(j0):
            out = []
            for n, (f, k) in enumerate(FF_GROUPS):
                out.append((n, f, k, j0, j0 + 2 * k))
                j0 += 2 * k + KT
            return out

        block = ctx.enter_context(nc.Block())

        @block.sync
        def _(sp):
            def load(src, k, s, n=0, i=None):
                if s >= 2:
                    sp.wait_ge(w_lo, lin(s - 1, n, i))
                sp.dma_start(raw[s % 2][:, 0:k, :], src.rearrange("(k p) m -> p k m", p=P)).then_inc(raw_in[s % 2], 16)

            def at(i, step, base):
                return bass.ds(i * step + base if base else (i + 1) * step - step, P)

            rows = lambda v: v.rearrange("a (t p) -> (a t) p", p=P)
            for k in range(TAPS):
                sp.dma_start(f1["va"][16 * k:16 * (k + 1), :], ssd_conv_w[0, k].rearrange("(t p) -> t p", p=P)).then_inc(vec_in, 16)
            sp.dma_start(f1["va"][80:96, :], rows(ssd_conv_b)).then_inc(vec_in, 16)
            sp.dma_start(f1["va"][96:128, :], hg_lb_table.rearrange("d l (t p) -> (d l t) p", p=P)).then_inc(vec_in, 16)
            for k, v in enumerate((ffn1_norm, mix_norm, ssd_norm, hg_norm, ffn2_norm)):
                sp.dma_start(f1["vb"][KT * k:KT * (k + 1), :], rows(v)).then_inc(vec_in, 16)
            sp.dma_start(f1["vb"][5 * KT:6 * KT, :], final_norm.rearrange("(t p) -> t p", p=P)).then_inc(vec_in, 16)
            sp.dma_start(dtb[:, :], ssd_dt_bias.rearrange("a d h -> (d h) a")).then_inc(vec_in, 16)
            sp.dma_start(alog[:, :], ssd_a_log.rearrange("a d h -> (d h) a")).then_inc(vec_in, 16)
            for b in range(2):
                sp.dma_start(dskip[64 * b:64 * (b + 1), :],
                             ssd_d[0].rearrange("(t b) -> b t", b=2)[b].unsqueeze(0).broadcast_to([64, KT]), allow_slow_non_contiguous=True).then_inc(vec_in, 16)
            for n, (src, r, k, _) in enumerate(X_TILES):
                if n >= 2:
                    sp.wait_ge(x_mm, n - 1)
                sp.dma_start(f1["io"][n % 2][0:k, :], src[r:r + k, :]).then_inc(x_in[n % 2], 16)
                if n < 2:
                    load(FFNS[0][3][:, D_FF * n:D_FF * n + P], KT, n)

            def ffn(j0, _m, _c0, w_gu, w_down):
                for n, f, k, jg, jd in ffn_groups(j0):
                    first = 1 if jg == 0 else 0
                    with sp.Fori(first, k) as i:
                        load(w_gu[:, at(i, P, f * P)], KT, jg if jg >= 2 else 2, 2, i if jg >= 2 else i - 1)
                        load(w_gu[:, at(i, P, f * P + D_FF)], KT, jg + 1 if jg >= 2 else 3, 2, i if jg >= 2 else i - 1)
                    with sp.Fori(0, KT // 2) as i:
                        for c in range(2):
                            load(w_down[P * f:P * (f + k), at(i, 2 * P, c * P)], k, jd + c, 2, i)

            ffn(*FFNS[0])
            W = w_in[0]
            load(W[:, DT0:DT0 + P], KT, J_DT)
            with sp.Fori(0, GROUPS) as g:
                for c, (off, step) in enumerate(((X0, 2 * P), (X0 + P, 2 * P), (B0, P), (C0, P), (Z0, 2 * P), (Z0 + P, 2 * P))):
                    load(W[:, at(g, step, off)], KT, J_SSD + c, 6, g)
            with sp.Fori(0, KT // 2) as i:
                for c in range(2):
                    load(W[:, at(i, 2 * P, GA0 + c * P)], KT, J_PA + 2 * c, 4, i)
                    load(ssd_w_proj[0][:, at(i, 2 * P, c * P)], KT, J_PA + 2 * c + 1, 4, i)
            with sp.Fori(0, HH // 2) as i:
                for a in range(2):
                    for c, off in enumerate((HF0, HF0 + D, HI0, HQ0, HG0)):
                        load(W[:, at(i, 2 * P, off + a * P)], KT, J_HG + 5 * a + c, 10, i)
            with sp.Fori(0, KT // 2) as i:
                for c in range(2):
                    load(W[:, at(i, 2 * P, GA0 + D + c * P)], KT, J_PB + 2 * c, 4, i)
                    load(hg_w_proj[0][:, at(i, 2 * P, c * P)], KT, J_PB + 2 * c + 1, 4, i)
            with sp.Fori(0, KT // 2) as i:
                for c in range(2):
                    load(w_out[0][:, at(i, 2 * P, c * P)], KT, J_WO + c, 2, i)
            ffn(*FFNS[1])
            for c in range(NC):
                dst = y_prompt[0] if c < CP else y_sample[0]
                r = P * c if c < CP else P * (c - CP)
                sp.wait_ge(out_ok, c + 1)
                sp.dma_start(dst[r:r + P, :], f2["io"][c % 2][:, :]).then_inc(out_done[c % 2], 16)
            for s in range(2):
                sp.wait_ge(out_done[s], 16 * (NC // 2))

        @block.tensor
        def _(pe):
            def job(k, hi, lo, c0, off, s, n=0, i=None, ready=None):
                b = s % 2
                pe.wait_ge(w_lo, lin(s + 1, n, i))
                pe.wait_ge(slot_free[b], lin(s // 2, n // 2, i))
                for t in range(k):
                    if ready:
                        pe.wait_ge(ready[0], ready[1] + t)
                    for p, (w, x) in enumerate(((whi, hi), (whi, lo), (wlo, hi))):
                        for u, v in halves(c0):
                            mm = pe.matmul(slot[b][:, PC + u:PC + v], w[b][:, t, :], x[:, t, u + off:v + off],
                                           start=(t == 0 and p == 0), stop=(t == k - 1 and p == 2))
                mm.then_inc(dense_done, 1)

            def norm_sum(n, c0):
                pe.wait_ge(acc_ok, 9 * (n + 1))
                for u, v in halves(c0):
                    mm = pe.matmul(aux2[0][:, PC + u:PC + v], ones[:, :], acc[:, u:v], start=True, stop=True)
                mm.then_inc(norm_mm, 1)

            def ffn(j0, m, c0, r, nf):
                for n, f, k, jg, jd in ffn_groups(j0):
                    with pe.Fori(0, k) as i:
                        for c in range(2):
                            job(KT, xh, xl, c0, 0, jg + c, 2, i, (xn_ok, KT * r + 1))
                    with pe.Fori(0, KT // 2) as i:
                        for c in range(2):
                            job(k, m["ah"], m["al"], c0, 0, jd + c, 2, i, (a_ok, nf + f + 1))

            pe.wait_ge(vec_in, 16 * 17)
            pe.wait_ge(const_ok, 1)
            pe.transpose(aux[0][:, 0:P], f1["va"][:, :], ident[:, :])
            pe.transpose(aux[0][:, P:P + 6 * KT], f1["vb"][:, :], ident[0:6 * KT, 0:6 * KT]).then_inc(vec_mm, 1)
            for n, (_, _, k, _) in enumerate(X_TILES):
                pe.wait_ge(x_in[n % 2], 16 * (n // 2 + 1))
                if n >= 2:
                    pe.wait_ge(x_ok, n - 1)
                for t in range(KT):
                    mm = pe.transpose(slot[n % 2][:, P * t:P * t + k], f1["io"][n % 2][0:k, P * t:P * (t + 1)], ident[0:k, 0:k])
                mm.then_inc(x_mm, 1)
            pe.wait_ge(vec_ok, 1)
            norm_sum(0, 0)
            pe.wait_ge(x_ok, len(X_TILES))
            ffn(0, f1, 0, 0, 0)
            norm_sum(1, 0)

            job(KT, xh, xl, 0, 0, J_DT, ready=(xn_ok, KT + 1))
            dtf, daf = m_dt[5], m_dt[6]

            def dt_part():
                pe.wait_ge(rs_ln, 2)
                pe.wait_ge(dt_ok, 2)
                for c in range(NC + 1):
                    k, t = (P, N_META + P * c) if c < NC else (N_META, 0)
                    for q, v in enumerate((dtf, daf)):
                        mm = pe.transpose(aux[0][0:k, 64 * c + 32 * q:64 * c + 32 * (q + 1)], v[:, t:t + k], ident[0:32, 0:32])
                mm.then_inc(dt_mm, 1)
                pe.wait_ge(dt_tok, 4)
                for d in range(2):
                    pe.matmul(aux[1][:, 0:32 * NC].rearrange("p (c d h) -> p c d h", d=2, h=HEADS)[:, :, d, :],
                              strict[d][:, :].bitcast(F32), da_t[:, 0:NC, d, :], start=True, stop=True, skip_group_check=True)
                pe.matmul(aux[1][:, 192:384], ones[:, :], da_t[:, 0:NC, :, :], start=True, stop=True, skip_group_check=True)
                pe.matmul(aux[1][0:N_META, 384:400], strict[0][0:N_META, 0:N_META].bitcast(F32), da_t[0:N_META, META, 0, :],
                          start=True, stop=True, skip_group_check=True).then_inc(dt_sum, 1)

            def ssd_states(g):
                pe.wait_ge(co_ok, lin(4, 4, g))
                pe.wait_ge(exp_ok, lin(0, 4 * NC, g))
                pe.wait_ge(cbm_ok, lin(0, 2 * NC, g))
                pe.wait_ge(y_ok, lin(0, 2 * NC, g))
                for n in range(NC + 2):
                    c = n - 2
                    k, t = (N_META, CO_META[n]) if n < 2 else (P, CO_CHUNK[c])
                    pe.wait_ge(tr_ok, lin(max(n - 1, 0), NC + 2, g))
                    for q in range(3):
                        mm = pe.transpose(aux[n % 2][0:k, P * q:P * (q + 1)], m_s["co"][q][:, t:t + k], ident[:, :])
                    mm.then_inc(tr_mm, 1)
                pe.wait_ge(tr_ok, lin(NC + 2, NC + 2, g))
                for n, (d, c) in enumerate(S_UPD):
                    q, k = (c - META, N_META) if c >= META else (c + 2, P)
                    pe.wait_ge(xw_ok, lin(n + 1, len(S_UPD), g))
                    pe.wait_ge(up_ok, lin(max(n - 1, 0), len(S_UPD), g))
                    pe.matmul(aux[2 + n % 2][:, 0:2 * P], m_s["xbt"][0:k, q, 2 * P:3 * P], m_s["xw"][n % 2][0:k, :],
                              start=True, stop=True).then_inc(up_mm, 1)

            def ssd_decay(c, g):
                if c == 0:
                    pe.wait_ge(up_ok, lin(len(S_UPD), len(S_UPD), g))
                for d in range(2):
                    pe.wait_ge(rh_ok, lin(2 * c + d + 1, 2 * NC, g))
                    pe.wait_ge(rl_ok, lin(2 * c + d + 1, 2 * NC, g))
                    for q, lhs in enumerate((strict[d], ones_r)):
                        pe.wait_ge(exp_ok, lin(max(4 * c + 2 * d + q - 1, 0), 4 * NC, g))
                        for p, r in enumerate((m_s["rh"], m_s["rl"])):
                            mm = pe.matmul(aux[q][:, :], lhs[:, :], r[d][:, :, :], start=(p == 0), stop=(p == 1))
                        mm.then_inc(seg_mm, 1)
                t = CO_CHUNK[c]
                pe.wait_ge(cbm_ok, lin(2 * c, 2 * NC, g))
                pe.matmul(aux[2][:, 0:P], m_s["co"][2][:, t:t + P], m_s["co"][3][:, t:t + P], start=True, stop=True).then_inc(cb_mm, 1)

            def ssd_out(c, g):
                pe.wait_ge(wy_ok, lin(2 * c + 2, 2 * NC, g))
                pe.wait_ge(ch_ok, lin(2 * c + 2, 2 * NC, g))
                pe.wait_ge(xdt_ok, lin(2 * c + 2, 2 * NC, g))
                pe.wait_ge(y_ok, lin(2 * c, 2 * NC, g))
                s = c % 2
                for hh in range(HPG):
                    out = aux[3][PD * (hh % 2):PD * (hh % 2 + 1), P * (hh // 2):P * (hh // 2 + 1)]
                    terms = []
                    for d in range(2):
                        terms.append((m_s["xdt"][s][d][:, PD * hh:PD * (hh + 1)], m_s["e"][s][d][:, hh, :]))
                        if not (d == 1 and c in (CP - 1, NC - 1)):
                            terms.append((m_s["prev"][d][:, c, PD * hh:PD * (hh + 1)], m_s["ea"][s][d][:, hh, :]))
                    for n, (w, r) in enumerate(terms):
                        mm = pe.matmul(out, w, r, start=(n == 0), stop=(n == len(terms) - 1))
                mm.then_inc(y_mm, 1)

            for c in range(6):
                job(KT, xh, xl, 0 if c < 4 else N_META, 0, J_SSD + c)
                if c == 2:
                    dt_part()
            pe.wait_ge(dt_all, 1)

            def ssd_scan(g):
                ssd_states(g)
                ssd_decay(0, g)
                for c in range(NC):
                    if c + 1 < NC:
                        ssd_decay(c + 1, g)
                    ssd_out(c, g)

            with pe.Fori(0, GROUPS - 1) as g:
                ssd_scan(g)
                for c in range(6):
                    job(KT, xh, xl, 0 if c < 4 else N_META, 0, J_SSD + 6 + c, 6, g)
            ssd_scan(GROUPS - 1)

            def branch_a(c, i=None, first=False):
                job(KT, xh, xl, N_META, 0, J_PA + 2 * c, 4, i)
                if first:
                    norm_sum(2, N_META)
                job(KT, m_a["hi"], m_a["lo"], N_META, -N_META, J_PA + 2 * c + 1, 4, i, (pa_lo, 1))

            branch_a(0, first=True)
            branch_a(1)
            with pe.Fori(0, KT // 2 - 1) as i:
                branch_a(2, i)
                branch_a(3, i)

            def hg_job(j, c, i=None):
                job(KT, xh, xl, 0 if c < 3 else N_META, 0, J_HG + 5 * j + c, 10, i)

            def hg_turn(j, i=None):
                s = j % 2
                pe.wait_ge(k_ok, lin(4 * (j + 1), 8, i))
                pe.wait_ge(ors_ln, lin(j, 2, i))
                pe.wait_ge(yb_ok, lin(j, 2, i))
                for n, (v, blocks) in enumerate(((m_h["v"][s], (0, 1, 2, 3)), (m_h["v"][s], (4, 5, META)),
                                                 (m_h["q"][0][3], (0, 1, 2, 3)), (m_h["q"][0][3], (4, 5, META)),
                                                 (m_h["q"][1][3], (0, 1, 2, 3)), (m_h["q"][1][3], (4, 5)))):
                    if n >= 4:
                        pe.wait_ge(ht_ok, lin(6 * j + n - 3, 12, i))
                    for q, c in enumerate(blocks):
                        k, t = (N_META, 0) if c == META else (P, N_META + P * c)
                        mm = pe.transpose(aux[n % 4][0:k, P * q:P * (q + 1)], v[:, t:t + k], ident[:, :])
                    mm.then_inc(ht_mm, 1)

            def hg_states(j, first, last, i=None):
                pe.wait_ge(ht_ok, lin(6 * j + 6, 12, i))
                for u in range(first, last):
                    if u >= 4:
                        pe.wait_ge(kv_ok, lin(len(H_UPD) * j + H_END[u - 4], 2 * len(H_UPD), i))
                    for q, (d, c) in enumerate(H_BANKS[u]):
                        r0, r1, p = (0, N_META, META) if c < 0 else (64 * (c % 2), 64 * (c % 2) + 64, c // 2)
                        mm = pe.matmul(aux[u % 4][:, P * q:P * (q + 1)], m_h["kt"][d][r0:r1, p, :], m_h["vt"][r0:r1, p, :],
                                       start=True, stop=True)
                    mm.then_inc(kv_mm, 1)

            def hg_outputs(j, i=None):
                def within(p):
                    if p < 2:
                        pe.wait_ge(kv_ok, lin(len(H_UPD) * j + H_END[(5, 8)[p]], 2 * len(H_UPD), i))
                    else:
                        pe.wait_ge(am_ok, lin(12 * j + 2 * (p - 1), 24, i))
                    t = N_META + P * p
                    for d in range(2):
                        mm = pe.matmul(aux[1 - p % 2][:, P * d:P * (d + 1)], m_h["q"][d][2][:, t:t + P], m_h["q"][d][1][:, t:t + P],
                                       start=True, stop=True)
                    mm.then_inc(a_mm, 1)

                pe.wait_ge(q_ok, lin(4 * (j + 1), 8, i))
                within(0)
                for p in range(NC):
                    if p + 1 < NC:
                        within(p + 1)
                    pe.wait_ge(am_ok, lin(12 * j + 2 * p + 2, 24, i))
                    out = aux2[1][:, 2 * P + P * p:2 * P + P * (p + 1)]
                    for d in range(2):
                        pe.matmul(out, m_h["vt"][:, p, :], m_h["am"][p % 2][d][:, :], start=(d == 0), stop=False,
                                  skip_group_check=True)
                    for u in range(2):
                        c, t = 2 * p + u, N_META + P * p + 64 * u
                        for d in range(2):
                            if d == 1 and c in (2 * CP - 1, 2 * NC - 1):
                                continue
                            mm = pe.matmul(out[:, 64 * u:64 * u + 64], m_h["prev"][d][:, c, :], m_h["q"][d][0][:, t:t + 64],
                                           start=False, stop=True, skip_group_check=True)
                    mm.then_inc(o_mm, 1)

            def hg_sums(j, i=None):
                pe.wait_ge(osq_ok, lin(j + 1, 2, i))
                for u, v in halves(N_META):
                    mm = pe.matmul(aux2[0][:, PC + u:PC + v], ones[:, :], osq[:, u - N_META:v - N_META], start=True, stop=True)
                mm.then_inc(os_mm, 1)

            def hg_step(j, i=None):
                hg_job(j + 1, 0, i)
                hg_turn(j, i)
                hg_job(j + 1, 1, i)
                hg_states(j, 0, 4, i)
                hg_job(j + 1, 2, i)
                hg_states(j, 4, len(H_BANKS), i)
                hg_outputs(j, i)
                hg_job(j + 1, 3, i)
                hg_sums(j, i)
                hg_job(j + 1, 4, i)

            for c in range(5):
                hg_job(0, c)
            with pe.Fori(0, HH // 2 - 1) as i:
                hg_step(0, i)
                hg_step(1, i)
            hg_step(HH - 2)
            hg_turn(HH - 1)
            hg_states(HH - 1, 0, len(H_BANKS))
            hg_outputs(HH - 1)
            hg_sums(HH - 1)

            with pe.Fori(0, KT // 2) as i:
                for c in range(2):
                    job(KT, xh, xl, N_META, 0, J_PB + 2 * c, 4, i)
                    job(KT, m_b["hi"], m_b["lo"], N_META, -N_META, J_PB + 2 * c + 1, 4, i, (pa_lo, KT + 1))
            with pe.Fori(0, KT // 2) as i:
                for c in range(2):
                    job(KT, m_b["mh"], m_b["ml"], N_META, -N_META, J_WO + c, 2, i, (ml_ok, 1))
            norm_sum(3, N_META)
            ffn(J_FF2, f2, N_META, 2, D_FF // P)
            norm_sum(4, N_META)

            pe.wait_ge(tmp_ok, 4 * KT)
            for c in range(NC):
                if c >= 2:
                    pe.wait_ge(out_ok, c - 1)
                for t in range(KT):
                    u = N_META + P * c
                    mm = pe.transpose(slot[c % 2][:, P * t:P * (t + 1)], f2["h"][:, t, u:u + P], ident[:, :])
                mm.then_inc(out_mm, 1)

        @block.scalar
        def _(act):
            own = Tally(act, act_step)

            def split(s, n=0, i=None):
                act.wait_ge(raw_in[s % 2], lin(16 * (s // 2 + 1), 8 * n, i))
                if s >= 1:
                    act.wait_ge(dense_done, lin(s - 1, n, i))
                act.activation(whi[s % 2][:, :, :], raw[s % 2][:, :, :], ACT.Copy).then_inc(w_hi, 1)

            def read_out(s, n=0, i=None, dst=None, func=ACT.Copy, c0=0):
                act.wait_ge(dense_done, lin(s + 1, n, i))
                act.activation(dst, slot[s % 2][:, PC + c0:], func).then_inc(slot_free[s % 2], 1)

            def rms(r, c0):
                act.wait_ge(norm_mm, r + 1)
                act.activation(rs[:, c0:], aux2[0][:, PC + c0:], ACT.Ln, bias=eps[:, 0:1], scale=1.0 / D).then_inc(rs_ln, 1)
                act.wait_ge(rs_ln, r + 1)
                act.activation(rs[:, c0:], rs[:, c0:], ACT.Exp, scale=-0.5).then_inc(rs_ok, 1)

            def normed(r, c0):
                for t in range(KT):
                    act.wait_ge(tmp_ok, KT * r + t + 1)
                    act.activation(xh[:, t, c0:], tmp[t % 2][:, c0:], ACT.Copy).then_inc(xh_ok, 1)

            def square(src, b, r, c0, t, n=0, i=None):
                act.wait_ge(acc_ok, lin(9 * r + t, n, i))
                act.activation(sq[b][:, c0:], src, ACT.Square).then_inc(sq_ok, 1)

            def down(m, c0, s, r, last):
                def pair(s, i, end=False):
                    for c in range(2):
                        if not (end and c == 1):
                            split(s + c + 1, 2, i)
                        if last:
                            act.wait_ge(slot_free[(s + c) % 2], lin((s + c) // 2 + 1, 1, i))
                            t = c if i is not None else KT - 2 + c
                            square(m["h"][:, t, c0:] if i is None else m["h"][:, bass.ds(i * 2 + c, 1), c0:],
                                   c, r, c0, t, 2, i)
                if s + KT == JOBS:
                    with act.Fori(0, KT // 2 - 1) as i:
                        pair(s, i)
                    pair(s + KT - 2, None, True)
                else:
                    with act.Fori(0, KT // 2) as i:
                        pair(s, i)

            def ffn(j0, m, c0, r):
                for n, f, k, jg, jd in ffn_groups(j0):
                    with act.Fori(0, k) as i:
                        split(jg + 1, 2, i)
                        act.wait_ge(slot_free[(jg + 1) % 2], lin((jg + 1) // 2, 1, i))
                        read_out(jg, 2, i, m["t"][:, c0:], ACT.Silu, c0)
                        split(jg + 2, 2, i)
                        act.wait_ge(slot_free[(jg + 1) % 2], lin((jg + 1) // 2 + 1, 1, i))
                        act.activation(m["ah"][:, bass.ds(i, 1), c0:], m["p"][:, c0:], ACT.Copy).then_inc(a_hi_ok, 1)
                    down(m, c0, jd, r, n == len(FF_GROUPS) - 1)

            act.wait_ge(vec_ok, 0)
            act.wait_ge(lb_sub, 1)
            act.activation(lbs[:, 1:3, :, :], lbs[:, 1:3, :, :], ACT.Exp).then_inc(lb_exp, 1)
            act.activation(aneg[:, :], alog[:, :], ACT.Exp).then_inc(lb_exp, 1)
            act.wait_ge(x_ok, len(X_TILES))
            for t in range(KT):
                square(f1["h"][:, t, :], t % 2, 0, 0, t)
            split(0)
            rms(0, 0)
            normed(0, 0)
            ffn(0, f1, 0, 1)
            rms(1, 0)
            normed(1, 0)

            split(J_DT + 1)
            e = m_dt[1]
            act.wait_ge(slot_free[J_DT % 2], J_DT // 2 + 1)
            own.add(act.activation(e[:, :], m_dt[0][:, :], ACT.Abs))
            own.wait()
            act.activation(e[:, :], e[:, :], ACT.Exp, scale=-1.0).then_inc(dt_exp, 1)

            def dt_decays():
                act.wait_ge(dt_sum, 1)
                act.activation(w_t[:, 0:NC, :, :], aux[1][:, 0:192].rearrange("p (c d h) -> p c d h", d=2, h=HEADS), ACT.Exp).then_inc(dt_dec, 1)
                act.activation(cd_t[:, :, :, :], aux[1][:, 192:384].rearrange("p (c d h) -> p c d h", d=2, h=HEADS), ACT.Exp).then_inc(dt_dec, 1)
                act.activation(w_t[0:N_META, META, 0, :], aux[1][0:N_META, 384:400], ACT.Exp).then_inc(dt_dec, 1)

            def ssd_dense(s, g, i=None):
                def convolved(c):
                    act.wait_ge(conv_ok, lin(4 * g + c + 1, 4, i))
                    if c == 0:
                        act.wait_ge(y_ok, lin(2 * NC * g, 2 * NC, i))
                    act.activation(m_s["co"][c][:, :], m_s["ca"][:, :], ACT.Silu, bias=m_s["gw"][:, TAPS, c:c + 1]).then_inc(co_ok, 1)

                for c in range(6):
                    split(s + c + 1, 6, i)
                    if g == 0 and c == 2:
                        dt_decays()
                        convolved(0)
                    if c < 4:
                        if g > 0 or c >= 2:
                            act.wait_ge(conv_ok, lin(4 * g + c - 1, 4, i))
                        act.wait_ge(z_ok, 2)
                        act.wait_ge(dense_done, lin(s + c + 1, 6, i))
                        b, p = m_s["ci"][c % 2], slot[(s + c) % 2][:, PC:]
                        own.add(act.activation(b[:, 2:2 + SPLIT], p[:, 0:SPLIT], ACT.Copy))
                        own.add(act.activation(b[:, 4 + SPLIT:4 + SPLIT + N_META], p[:, 0:N_META], ACT.Copy))
                        act.activation(b[:, 4 + SPLIT + N_META:4 + SPLIT + N_META + N_S], p[:, SPLIT:], ACT.Copy).then_inc(slot_free[(s + c) % 2], 1)
                    else:
                        act.wait_ge(yz_ok, lin(2 * g, 2, i))
                        read_out(s + c, 6, i, zs[c - 4], ACT.Silu, N_META)
                    if 1 <= c < 5 and (g or c > 1):
                        convolved(c - 1)

            def ssd_scan(g):
                for n in range(NC + 2):
                    k = N_META if n < 2 else P
                    act.wait_ge(tr_mm, lin(n + 1, NC + 2, g))
                    if n == 0:
                        act.wait_ge(xdt_ok, lin(0, 2 * NC, g))
                    act.activation(m_s["xbt"][0:k, n, :], aux[n % 2][0:k, 0:3 * P], ACT.Copy).then_inc(tr_ok, 1)
                for c in range(NC):
                    for d in range(2):
                        for q, v in enumerate((m_s["e"], m_s["ea"])):
                            act.wait_ge(seg_mm, lin(4 * c + 2 * d + q + 1, 4 * NC, g))
                            if c >= 2:
                                act.wait_ge(y_mm, lin(c - 1, NC, g))
                            act.activation(v[c % 2][d][:, :, :], aux[q].rearrange("p (h t) -> p h t", h=HPG), ACT.Exp).then_inc(exp_ok, 1)

            ssd_dense(J_SSD, 0)
            with act.Fori(0, GROUPS - 1) as g:
                ssd_scan(g)
                ssd_dense(J_SSD + 6, 1, g)
            ssd_scan(GROUPS - 1)

            def parts(hi, src, ready, base):
                for t in range(KT):
                    act.wait_ge(ready, KT)
                    act.activation(hi[:, t, :], src[:, t, :], ACT.Copy).then_inc(pa_hi, 1)

            def sigmoid(s, c, i=None):
                act.wait_ge(slot_free[(s + 1) % 2], lin((s - 1) // 2, 2, i))
                read_out(s, 4, i, gate[c], ACT.Sigmoid, N_META)

            def branch_a(c, i=None, first=False):
                s = J_PA + 2 * c
                split(s + 1, 4, i)
                if first:
                    parts(m_a["hi"], m_s["ya"], ya_ok, 0)
                sigmoid(s, c % 2, i)
                if first:
                    rms(2, N_META)
                split(s + 2, 4, i)

            branch_a(0, first=True)
            branch_a(1)
            with act.Fori(0, KT // 2 - 1) as i:
                branch_a(2, i)
                branch_a(3, i)

            def hg_log(j, d, i=None):
                f = m_h["s"][j % 2][d]
                act.wait_ge(f_ok, lin(2 * j + d + 1, 4, i))
                act.activation(f[:, N_META * d:], f[:, N_META * d:], ACT.Ln).then_inc(ln_ok, 1)

            def hg_exps(j, d, i=None):
                q, b = m_h["q"][d], m_h["b"]
                act.wait_ge(bc_ok, lin(2 * j + d + 1, 4, i))
                act.wait_ge(o_mm, lin(NC * j, 2 * NC, i))
                act.activation(q[0][:, N_META:], b[:, N_META:], ACT.Exp).then_inc(e_ok, 1)
                act.wait_ge(d_ok, lin(2 * (2 * j + d) + 1, 8, i))
                act.activation(q[1][:, N_META:], dif[:, N_META:], ACT.Exp).then_inc(e_ok, 1)
                act.activation(q[2][:, N_META:], dif[:, N_META:], ACT.Exp, scale=-1.0).then_inc(e_ok, 1)

            def hg_end_exp(j, d, i=None):
                f = m_h["s"][j % 2][d]
                act.wait_ge(d_ok, lin(2 * (2 * j + d) + 2, 8, i))
                act.activation(m_h["q"][d][3][:, N_META * d:], f[:, N_META * d:], ACT.Exp).then_inc(e_ok, 1)

            def hg_read(j, c, i=None):
                a = j % 2
                if c == 4 and j >= 1:
                    act.wait_ge(yb_ok, lin(j - 1, 2, i))
                if c == 3 and j >= 1:
                    act.wait_ge(q_ok, lin(4 * (j - 1), 8, i))
                dst, func = ((m_h["s"][a][0][:, :], ACT.Sigmoid), (m_h["s"][a][1][:, :], ACT.Sigmoid),
                             (m_h["v"][a][:, :], ACT.Copy), (hq[a], ACT.Silu), (hg[a], ACT.Silu))[c]
                read_out(J_HG + 5 * j + c, 10, i, dst, func, 0 if c < 3 else N_META)

            def hg_turn(j, i=None):
                vt, kt = m_h["vt"], m_h["kt"]
                for n, (dst, c, m) in enumerate(((vt, 0, 0), (vt, 4, 1), (kt[0], 0, 0), (kt[0], 4, 1), (kt[1], 0, 0), (kt[1], 4, 0))):
                    act.wait_ge(ht_mm, lin(6 * j + n + 1, 12, i))
                    k = 4 if c == 0 else 2
                    ins = act.activation(dst[:, c:c + k, :], aux[n % 4][:, 0:P * k].rearrange("p (c k) -> p c k", k=P), ACT.Copy)
                    if m:
                        ins = act.activation(dst[0:N_META, META, :], aux[n % 4][0:N_META, 2 * P:3 * P], ACT.Copy)
                    ins.then_inc(ht_ok, 1)

            def hg_squares(j, i=None):
                act.wait_ge(o_mm, lin(NC * (j + 1), 2 * NC, i))
                act.wait_ge(yb_ok, lin(j, 2, i))
                act.activation(osq, aux2[1][:, PC + N_META:], ACT.Square).then_inc(osq_ok, 1)

            def hg_rms(j, i=None):
                act.wait_ge(os_mm, lin(j + 1, 2, i))
                act.activation(osq, aux2[0][:, PC + N_META:], ACT.Ln, bias=eps[:, 0:1], scale=1.0 / P).then_inc(ors_ln, 1)
                act.wait_ge(ors_ln, lin(j + 1, 2, i))
                act.activation(osq, osq, ACT.Exp, scale=-0.5).then_inc(ors_ok, 1)

            def hg_step(j, i=None, scan=True):
                n, s = j + 1, J_HG + 5 * (j + 1)
                split(s + 1, 10, i)
                hg_read(n, 0, i)
                if scan:
                    hg_turn(j, i)
                hg_log(n, 0, i)
                split(s + 2, 10, i)
                hg_read(n, 1, i)
                split(s + 3, 10, i)
                hg_read(n, 2, i)
                if scan:
                    hg_squares(j, i)
                hg_exps(n, 0, i)
                hg_end_exp(n, 0, i)
                split(s + 4, 10, i)
                hg_read(n, 3, i)
                if scan:
                    hg_rms(j, i)
                hg_log(n, 1, i)
                split(s + 5, 10, i)
                hg_exps(n, 1, i)
                hg_read(n, 4, i)
                hg_end_exp(n, 1, i)

            act.wait_ge(pm_out[0], 16 * (KT // 2))
            act.wait_ge(pm_out[1], 16 * (KT // 2))
            hg_step(-1, scan=False)
            with act.Fori(0, HH // 2 - 1) as i:
                hg_step(0, i)
                hg_step(1, i)
            hg_step(HH - 2)
            hg_turn(HH - 1)
            hg_squares(HH - 1)
            hg_rms(HH - 1)

            def branch_b(c, i=None, first=False):
                s = J_PB + 2 * c
                split(s + 1, 4, i)
                if first:
                    parts(m_b["hi"], m_h["yb"], yb_ok, KT)
                sigmoid(s, c % 2, i)
                split(s + 2, 4, i)
                act.wait_ge(mg_ok, lin(c + 1, 2, i))
                t = c if i is None else bass.ds(i * 2 + c, 1)
                act.activation(m_b["mh"][:, t, :], prod[c % 2], ACT.Copy).then_inc(mh_ok, 1)

            branch_b(0, first=True)
            branch_b(1)
            with act.Fori(0, KT // 2 - 1) as i:
                branch_b(2, i)
                branch_b(3, i)
            down(f2, N_META, J_WO, 3, True)
            rms(3, N_META)
            normed(2, N_META)
            ffn(J_FF2, f2, N_META, 4)
            rms(4, N_META)
            for c in range(1, NC, 2):
                act.wait_ge(out_mm, c + 1)
                act.wait_ge(out_ok, c)
                if c >= 2:
                    act.wait_ge(out_done[c % 2], 16 * (c // 2))
                act.activation(f2["io"][c % 2][:, :], slot[c % 2][:, :], ACT.Copy).then_inc(out_ok, 1)

        @block.vector
        def _(dve):
            own = Tally(dve, dve_step)

            def one(ins):
                own.add(ins)
                own.wait()

            def squares_sum(r, c0, b, t, n=0, i=None):
                dve.wait_ge(sq_ok, lin(KT * (r if r < 2 else r - 1) + t + 1, n, i))
                dve.wait_ge(acc_ok, lin(9 * r + 1 + t, n, i))
                dve.tensor_tensor(acc[:, c0:], acc[:, c0:], sq[b][:, c0:], ALU.add).then_inc(acc_ok, 1)

            def clear_sum(r, used):
                dve.wait_ge(*used)
                dve.memset(acc[:, :], 0.0).then_inc(acc_ok, 1)

            def normed(h, w, r, q, c0):
                dve.wait_ge(rs_ok, r + 1)
                for t in range(KT):
                    if q > 0 or t >= 2:
                        dve.wait_ge(xn_ok, KT * q + max(t - 1, 0))
                    dve.scalar_tensor_tensor(tmp[t % 2][:, c0:], h[:, t, c0:], norm_w[w][:, t:t + 1], rs[:, c0:],
                                             ALU.mult, ALU.mult).then_inc(tmp_ok, 1)

            def down(m, c0, s, r, last, scale):
                with dve.Fori(0, KT // 2) as i:
                    for c in range(2):
                        j = s + c
                        hm = m["h"][:, bass.ds(i * 2 + c, 1), c0:]
                        dve.wait_ge(dense_done, lin(j + 1, 2, i))
                        dve.scalar_tensor_tensor(hm, slot[j % 2][:, PC + c0:], scale, hm, ALU.mult, ALU.add).then_inc(slot_free[j % 2], 1)
                        if last:
                            squares_sum(r, c0, c, c, 2, i)

            def ffn(j0, m, c0, r, nf):
                for n, f, k, jg, jd in ffn_groups(j0):
                    with dve.Fori(0, k) as i:
                        b = (jg + 1) % 2
                        dve.wait_ge(slot_free[jg % 2], lin(jg // 2 + 1, 1, i))
                        dve.wait_ge(dense_done, lin(jg + 2, 2, i))
                        dve.wait_ge(a_ok, lin(nf + f, 1, i))
                        dve.tensor_tensor(m["p"][:, c0:], m["t"][:, c0:], slot[b][:, PC + c0:], ALU.mult).then_inc(slot_free[b], 1)
                        dve.wait_ge(slot_free[b], lin((jg + 1) // 2 + 1, 1, i))
                        dve.wait_ge(a_hi_ok, lin(nf + f + 1, 1, i))
                        dve.tensor_tensor(m["al"][:, bass.ds(i, 1), c0:], m["p"][:, c0:], m["ah"][:, bass.ds(i, 1), c0:].bitcast(F32),
                                          ALU.subtract).then_inc(a_ok, 1)
                    last = n == len(FF_GROUPS) - 1
                    if last:
                        clear_sum(r, (norm_mm, r))
                    down(m, c0, jd, r, last, 0.5)

            dve.memset(acc[:, :], 0.0).then_inc(acc_ok, 1)
            dve.wait_ge(vec_mm, 1)
            own.add(dve.tensor_copy(vec_a[:, :], aux[0][:, 0:P]))
            one(dve.tensor_copy(vec_b[:, :], aux[0][:, P:P + 6 * KT]))
            one(dve.tensor_tensor(lbs[:, 0], lbt[:, :, 0, :], lbt[:, :, 1, :], ALU.max))
            for q in range(2):
                ins = dve.tensor_tensor(lbs[:, 1 + q], lbt[:, :, q, :], lbs[:, 0], ALU.subtract)
                if q == 0:
                    own.add(ins)
            ins.then_inc(lb_sub, 1)
            dve.wait_ge(lb_exp, 2)
            own.add(dve.tensor_scalar(aneg[:, :], aneg[:, :], -1.0, None, ALU.mult))
            one(dve.tensor_tensor(lbs[:, 3], lbs[:, 1], lbs[:, 2], ALU.add))
            one(dve.reciprocal(lbs[:, 3], lbs[:, 3]))
            one(dve.tensor_tensor(lb[:, :, :], lbs[:, 1], lbs[:, 3], ALU.mult))
            dve.tensor_scalar(oml[:, :, :], lb[:, :, :], -1.0, 1.0, ALU.mult, ALU.add).then_inc(vec_ok, 1)
            dve.wait_ge(vec_ok, 1)
            for n, (_, _, k, t) in enumerate(X_TILES):
                dve.wait_ge(x_mm, n + 1)
                dve.tensor_copy(f1["h"][:, :, t:t + k], slot[n % 2][:, :].rearrange("p (t k) -> p t k", k=P)[:, :, 0:k]).then_inc(x_ok, 1)
            dve.wait_ge(x_ok, len(X_TILES))
            for t in range(KT):
                squares_sum(0, 0, t % 2, t)
            normed(f1["h"], "ffn1", 0, 0, 0)
            ffn(0, f1, 0, 1, 0)
            normed(f1["h"], "mix", 1, 1, 0)

            dx, e, s, s2, poly, dtf, daf = m_dt
            dve.wait_ge(spill_out, 16)
            dve.wait_ge(tmp_ok, 2 * KT)
            dve.wait_ge(dense_done, J_DT + 1)
            dve.tensor_scalar(dx[:, :], slot[J_DT % 2][0:32, PC:], dtb[:, 0:1], None, ALU.add).then_inc(slot_free[J_DT % 2], 1)
            clear_sum(2, (norm_mm, 2))
            for b in range(2):
                dve.memset(m_s["ci"][b][:, :], 0.0).then_inc(z_ok, 1)
            dve.wait_ge(dt_exp, 1)
            one(dve.tensor_scalar(s2[:, :], e[:, :], 2.0, None, ALU.add))
            one(dve.reciprocal(s[:, :], s2[:, :]))
            one(dve.tensor_tensor(s[:, :], e[:, :], s[:, :], ALU.mult))
            one(dve.tensor_tensor(s2[:, :], s[:, :], s[:, :], ALU.mult))
            one(dve.tensor_scalar(poly[:, :], s2[:, :], 1.0 / 15, None, ALU.mult))
            for k in range(13, 1, -2):
                one(dve.scalar_tensor_tensor(poly[:, :], poly[:, :], 1.0 / k, s2[:, :], ALU.add, ALU.mult))
            one(dve.scalar_tensor_tensor(poly[:, :], poly[:, :], 1.0, s[:, :], ALU.add, ALU.mult))
            one(dve.tensor_scalar(dx[:, :], dx[:, :], 0.0, None, ALU.max))
            dve.scalar_tensor_tensor(dtf[:, :], poly[:, :], 2.0, dx[:, :], ALU.mult, ALU.add).then_inc(dt_ok, 1)
            dve.wait_ge(dt_ok, 1)
            dve.tensor_scalar(daf[:, :], dtf[:, :], aneg[:, 0:1], None, ALU.mult).then_inc(dt_ok, 1)
            dve.wait_ge(dt_mm, 1)
            both = aux[0][:, 0:64 * NC].rearrange("p (c q h) -> p c q h", q=2, h=2 * HEADS)
            flat = lambda v: v.rearrange("p c d h -> p c (d h)")
            dve.tensor_copy(flat(da_t[:, 0:NC]), both[:, :, 1, :]).then_inc(dt_tok, 1)
            dve.tensor_copy(flat(da_t[0:N_META, NC:NC + 1]), aux[0][0:N_META, 64 * NC + 32:64 * NC + 64]).then_inc(dt_tok, 1)
            dve.tensor_copy(flat(dt_t[:, 0:NC]), both[:, :, 0, :]).then_inc(dt_tok, 1)
            dve.tensor_copy(flat(dt_t[0:N_META, NC:NC + 1]), aux[0][0:N_META, 64 * NC:64 * NC + 32]).then_inc(dt_tok, 1)
            dve.wait_ge(dt_tok, 4)
            one(dve.tensor_copy(da_hi[:, :, :, :], da_t[:, 0:NC]))
            own.add(dve.tensor_tensor(da_lo[:, :, :, :], da_t[:, 0:NC], da_hi[:, :, :, :].bitcast(F32), ALU.subtract))
            dve.wait_ge(dt_dec, 3)
            own.add(dve.tensor_tensor(w_t[0:N_META, META, 0, :], w_t[0:N_META, META, 0, :], dt_t[0:N_META, META, 0, :], ALU.mult))
            own.wait()
            dve.tensor_tensor(w_t[:, 0:NC], w_t[:, 0:NC], dt_t[:, 0:NC], ALU.mult).then_inc(dt_all, 1)
            dve.wait_ge(dt_all, 1)

            def wide(v):
                return v.unsqueeze(2).broadcast_to([P, HPG, PD])

            heads4 = lambda v: v.rearrange("p (h q) -> p h q", h=HPG)
            U = len(S_UPD)
            with dve.Fori(0, GROUPS) as g:
                own.enter(g, 9 + 4 * (TAPS - 1) + sum(1 for d, c in S_UPD if c < META and not (d == 1 and c in (1, 5))) + 2)
                s = J_SSD
                dve.wait_ge(ya_ok, lin(0, 2, g))
                dve.wait_ge(co_ok, lin(0, 4, g))
                dve.wait_ge(rl_ok, lin(0, 2 * NC, g))
                dve.wait_ge(xw_ok, lin(0, U, g))
                own.add(dve.tensor_copy(m_s["gw"][:, :, 0:2], cw[:, :, bass.ds(g * 2, 2)]))
                own.add(dve.tensor_copy(m_s["gw"][:, :, 2:3], cw[:, :, bass.ds(g + 8, 1)]))
                own.add(dve.tensor_copy(m_s["gw"][:, :, 3:4], cw[:, :, bass.ds(g + 12, 1)]))
                own.add(dve.tensor_copy(m_s["gd"][:, 0:2], dskip[:, bass.ds(g * 2, 2)]))
                own.add(dve.tensor_copy(m_s["gd"][:, 2:4], norm_w["ssd"][:, bass.ds(g * 2, 2)]))
                own.add(dve.tensor_copy(m_s["gdt"][:, :, :, :], dt_t[:, 0:NC, :, bass.ds(g * HPG, HPG)]))
                own.add(dve.tensor_copy(m_s["gcd"][:, :, :, :], cd_t[:, :, :, bass.ds(g * HPG, HPG)]))
                own.add(dve.tensor_copy(m_s["gah"][:, :, :, :], da_hi[:, :, :, bass.ds(g * HPG, HPG)].bitcast(F32)))
                own.add(dve.tensor_copy(m_s["gal"][:, :, :, :], da_lo[:, :, :, bass.ds(g * HPG, HPG)].bitcast(F32)))
                dve.tensor_copy(m_s["gw_t"][:, 0:NC, :, :], w_t[:, 0:NC, :, bass.ds(g * HPG, HPG)]).then_inc(gat_ok, 1)
                dve.tensor_copy(m_s["gw_t"][0:N_META, META, 0, :], w_t[0:N_META, META, 0, bass.ds(g * HPG, HPG)]).then_inc(gat_ok, 1)
                own.wait()
                ca = m_s["ca"]
                for c in range(4):
                    dve.wait_ge(slot_free[(s + c) % 2], lin((s + c) // 2 + 1, 3, g))
                    dve.wait_ge(co_ok, lin(c, 4, g))
                    ci = m_s["ci"][c % 2]
                    one(dve.tensor_scalar(ca[:, :], ci[:, 0:CO], m_s["gw"][:, 0, c:c + 1], None, ALU.mult))
                    for k in range(1, TAPS):
                        ins = dve.scalar_tensor_tensor(ca[:, :], ci[:, k:k + CO], m_s["gw"][:, k, c:c + 1], ca[:, :], ALU.mult, ALU.add)
                        if k < TAPS - 1:
                            one(ins)
                    ins.then_inc(conv_ok, 1)
                prev = m_s["prev"]
                for n, (d, c) in enumerate(S_UPD):
                    up = aux[2 + n % 2][:, 0:2 * P]
                    if c >= META or (d == 1 and c in (CP - 1, NC - 1)):
                        dst = prev[d][:, 0 if c == META else CP if c > META else c - 1, :]
                        dve.wait_ge(up_mm, lin(n + 1, U, g))
                        dve.tensor_copy(dst, up).then_inc(up_ok, 1)
                    else:
                        dst = prev[d][:, c + 1 if d == 0 else c - 1, :]
                        dve.wait_ge(up_ok, lin(n, U, g))
                        dve.wait_ge(up_mm, lin(n, U, g))
                        one(dve.tensor_tensor(heads4(dst), heads4(prev[d][:, c, :]), wide(m_s["gcd"][:, c, d, :]), ALU.mult))
                        dve.wait_ge(up_mm, lin(n + 1, U, g))
                        dve.tensor_tensor(dst, dst, up, ALU.add).then_inc(up_ok, 1)

                def decays(c):
                    for d in range(2):
                        if c >= 1:
                            dve.wait_ge(seg_mm, lin(4 * (c - 1) + 2 * d + 2, 4 * NC, g))
                        dve.tensor_tensor(m_s["rh"][d][:, :, :], incl[d][:, :].unsqueeze(1).broadcast_to([P, HPG, P]),
                                          m_s["gah"][:, c, d, :].unsqueeze(2).broadcast_to([P, HPG, P]), ALU.mult).then_inc(rh_ok, 1)

                def y_out(c):
                    dve.wait_ge(y_mm, lin(c + 1, NC, g))
                    for q in range(2):
                        dve.scalar_tensor_tensor(ys[q][:, P * c:P * (c + 1)], m_s["co"][q][:, CO_CHUNK[c]:CO_CHUNK[c] + P],
                                                 m_s["gd"][:, q:q + 1], aux[3][:, P * q:P * (q + 1)], ALU.mult, ALU.add).then_inc(y_ok, 1)

                decays(0)
                for c in range(NC):
                    b = c % 2
                    if c + 1 < NC:
                        decays(c + 1)
                    if c >= 2:
                        dve.wait_ge(y_mm, lin(c - 1, NC, g))
                    for d in range(2):
                        dve.tensor_tensor(heads4(m_s["xdt"][b][d][:, :]), heads4(m_s["xbt"][:, c + 2, 0:2 * P]), wide(m_s["gdt"][:, c, d, :]),
                                          ALU.mult).then_inc(xdt_ok, 1)
                    dve.wait_ge(cb_mm, lin(c + 1, NC, g))
                    for d in range(2):
                        dve.tensor_tensor(m_s["cb"][b][d][:, :], aux[2][:, 0:P], incl[d][:, :], ALU.mult).then_inc(cbm_ok, 1)
                    for d in range(2):
                        dve.wait_ge(exp_ok, lin(4 * c + 2 * d + 1, 4 * NC, g))
                        dve.wait_ge(cbm_ok, lin(2 * c + d + 1, 2 * NC, g))
                        v = m_s["e"][b][d][:, :, :]
                        dve.tensor_tensor(v, v, m_s["cb"][b][d][:, :].unsqueeze(1).broadcast_to([P, HPG, P]), ALU.mult).then_inc(wy_ok, 1)
                    if c >= 1:
                        y_out(c - 1)
                y_out(NC - 1)
                dve.wait_ge(y_ok, lin(2 * NC, 2 * NC, g))
                for q in range(2):
                    dve.wait_ge(slot_free[(s + 4 + q) % 2], lin((s + 4 + q) // 2 + 1, 3, g))
                    dve.tensor_tensor(ys[q], ys[q], zs[q], ALU.mult).then_inc(yz_ok, 1)
                for q in range(2):
                    dve.wait_ge(yz_ok, lin(q + 1, 2, g))
                    one(dve.tensor_tensor(ca[:, 0:NX], ys[q], ys[q], ALU.mult))
                    dve.wait_ge(acc_ok, lin(9 * 2 + 1 + q, 2, g))
                    dve.tensor_tensor(acc[:, N_META:], acc[:, N_META:], ca[:, 0:NX], ALU.add).then_inc(acc_ok, 1)
                    dve.wait_ge(acc_ok, lin(9 * 2 + 2 + q, 2, g))
                    dve.tensor_scalar(m_s["ya"][:, bass.ds(g * 2 + q, 1), :], ys[q], m_s["gd"][:, 2 + q:3 + q], None, ALU.mult).then_inc(ya_ok, 1)
                own.leave(GROUPS)

            def low_parts(m, src, base):
                for t in range(KT):
                    dve.wait_ge(pa_hi, base + t + 1)
                    dve.tensor_tensor(m["lo"][:, t, :], src[:, t, :], m["hi"][:, t, :].bitcast(F32), ALU.subtract).then_inc(pa_lo, 1)

            low_parts(m_a, m_s["ya"], 0)
            dve.wait_ge(rs_ok, 3)
            with dve.Fori(0, KT // 2) as i:
                own.enter(i, 2)
                for c in range(2):
                    j = J_PA + 2 * c
                    dve.wait_ge(slot_free[j % 2], lin(j // 2 + 1, 2, i))
                    one(dve.tensor_tensor(gate[c], gate[c], rs[:, N_META:], ALU.mult))
                    dve.wait_ge(dense_done, lin(j + 2, 4, i))
                    dve.wait_ge(pm_out[c], lin(0, 16, i))
                    dve.tensor_tensor(prod[c], gate[c], slot[(j + 1) % 2][:, PC + N_META:], ALU.mult).then_inc(slot_free[(j + 1) % 2], 1)
                own.leave(KT // 2)

            q_, k_, b_, s_ = m_h["q"], m_h["k"], m_h["b"], m_h["s"]
            main = lambda v: v[:, N_META:N_META + NX].rearrange("p (c t) -> p c t", t=64)
            dve.wait_ge(dense_done, J_HG)
            for v in (m_h["reset"][:, :],):
                one(dve.memset(v, 1.0))
            own.add(dve.memset(m_h["reset"][:, 0:1], 0.0))
            one(dve.memset(m_h["reset"][:, N_META::64], 0.0))
            for v in m_h["am"]:
                for d in range(2):
                    own.add(dve.memset(v[d][:, :], 0.0))
            own.wait()

            def of(j, i):
                return slice(j, j + 1) if i is None else bass.ds(i * 2 + j, 1)

            def hg_gates(j, d, i=None):
                jj, f, c0 = J_HG + 5 * j + d, s_[j % 2][d], N_META * d
                if j or d:
                    dve.wait_ge(k_ok, lin(2 * (2 * j + d), 8, i))
                own.add(dve.tensor_copy(m_h["lo"][:, d, 0:1], oml[:, d, of(j, i)]))
                own.add(dve.tensor_copy(m_h["lo"][:, d, 1:2], lb[:, d, of(j, i)]))
                own.wait()
                dve.wait_ge(slot_free[jj % 2], lin(jj // 2 + 1, 5, i))
                one(dve.tensor_scalar(f[:, c0:], f[:, c0:], m_h["lo"][:, d, 0:1], m_h["lo"][:, d, 1:2], ALU.mult, ALU.add))
                dve.tensor_scalar(k_[:, c0:], f[:, c0:], -1.0, 1.0, ALU.mult, ALU.add).then_inc(f_ok, 1)

            def hg_sums(j, d, i=None):
                w = lambda sem_, v, n: dve.wait_ge(sem_, lin(v, 2 * n, i))
                f = s_[j % 2][d]
                w(ln_ok, 2 * j + d + 1, 2)
                if d == 0:
                    o, r, l = b_[:, :], m_h["reset"][:, 0:NT], f[:, :]
                else:
                    o, r, l = b_[:, N_META:][:, ::-1], m_h["reset"][:, N_META + 1:][:, ::-1], f[:, N_META:][:, ::-1]
                dve.tensor_tensor_scan(o, r, l, 0.0, ALU.mult, ALU.add).then_inc(bc_ok, 1)
                w(bc_ok, 2 * j + d + 1, 2)
                if j or d:
                    w(e_ok, 4 * (2 * j + d) - 1, 8)
                mid, end = (32, 63) if d == 0 else (31, 0)
                dve.tensor_tensor(main(dif), main(b_), main(b_)[:, :, mid:mid + 1].broadcast_to([P, 2 * NC, 64]),
                                  ALU.subtract).then_inc(d_ok, 1)
                if d == 0:
                    own.add(dve.tensor_tensor(f[:, 0:N_META], b_[:, N_META - 1:N_META].broadcast_to([P, N_META]), b_[:, 0:N_META],
                                              ALU.subtract))
                dve.tensor_tensor(main(f), main(b_)[:, :, end:end + 1].broadcast_to([P, 2 * NC, 64]), main(b_),
                                  ALU.subtract).then_inc(d_ok, 1)

            def hg_keys(j, d, i=None):
                w = lambda sem_, v, n: dve.wait_ge(sem_, lin(v, 2 * n, i))
                c0, end = N_META * d, 63 if d == 0 else 0
                w(e_ok, 4 * (2 * j + d) + 1, 8)
                if j:
                    w(kv_ok, len(H_UPD) * j, len(H_UPD))
                dve.tensor_copy(m_h["dec"][d][:, :], main(q_[d][0])[:, :, end]).then_inc(dec_ok, 1)
                w(e_ok, 4 * (2 * j + d) + 3, 8)
                w(f_ok, 2 * j + d + 1, 2)
                dve.tensor_tensor(q_[d][2][:, N_META:], q_[d][2][:, N_META:], k_[:, N_META:], ALU.mult).then_inc(k_ok, 1)
                w(e_ok, 4 * (2 * j + d) + 4, 8)
                dve.tensor_tensor(q_[d][3][:, c0:], q_[d][3][:, c0:], k_[:, c0:], ALU.mult).then_inc(k_ok, 1)

            def hg_states(j, first, last, i=None):
                w = lambda sem_, v, n: dve.wait_ge(sem_, lin(v, 2 * n, i))
                U, prev, dec = len(H_UPD), m_h["prev"], m_h["dec"]
                w(dec_ok, 2 * (j + 1), 2)
                if j:
                    w(o_mm, NC * j, NC)
                for u, q, (d, c) in ((u, q, v) for u in range(first, last) for q, v in enumerate(H_BANKS[u])):
                    up = aux[u % 4][:, P * q:P * (q + 1)]
                    w(kv_mm, len(H_BANKS) * j + u + 1, len(H_BANKS))
                    if c < 0:
                        own.add(dve.tensor_copy(prev[0][:, 0, :], up))
                        ins = dve.tensor_copy(prev[0][:, 2 * CP, :], up)
                    elif d == 1 and c in (2 * CP - 1, 2 * NC - 1):
                        ins = dve.tensor_copy(prev[1][:, c - 1, :], up)
                    else:
                        before = (0, -1) if d == 0 and c in (0, 2 * CP) else (d, c - 1 if d == 0 else c + 1)
                        w(kv_ok, U * j + H_UPD.index(before) + 1, U)
                        ins = dve.scalar_tensor_tensor(prev[d][:, c + 1 if d == 0 else c - 1, :], prev[d][:, c, :], dec[d][:, c:c + 1], up,
                                                       ALU.mult, ALU.add)
                    ins.then_inc(kv_ok, 1)

            def hg_masks(j, i=None):
                w = lambda sem_, v, n: dve.wait_ge(sem_, lin(v, 2 * n, i))
                own.wait()
                for p in range(NC):
                    w(a_mm, NC * j + p + 1, NC)
                    if p >= 2:
                        w(o_mm, NC * j + p - 1, NC)
                    own.add(dve.tensor_copy(m_h["turn"][:, p:p + 1], ones[:, 0:1]))
                    for d in range(2):
                        dve.copy_predicated(m_h["am"][p % 2][d][:, :], incl64[d][:, :].bitcast(I32),
                                            aux[1 - p % 2][:, P * d:P * (d + 1)]).then_inc(am_ok, 1)

            def hg_out(j, i=None):
                if j:
                    dve.wait_ge(yb_ok, lin(j, 2, i))
                own.add(dve.tensor_copy(m_h["nw"][:, :], norm_w["hg"][:, of(j, i)]))
                own.wait()
                dve.wait_ge(ors_ok, lin(j + 1, 2, i))
                yj = m_h["yb"][:, j, :] if i is None else m_h["yb"][:, bass.ds(i * 2 + j, 1), :]
                one(dve.scalar_tensor_tensor(yj, aux2[1][:, PC + N_META:], m_h["nw"][:, 0:1], osq, ALU.mult, ALU.mult))
                jj = J_HG + 5 * j + 4
                dve.wait_ge(slot_free[jj % 2], lin(jj // 2 + 1, 5, i))
                dve.tensor_tensor(yj, yj, hg[j % 2], ALU.mult).then_inc(yb_ok, 1)

            def hg_step(j, i=None, scan=True):
                hg_gates(j + 1, 0, i)
                hg_sums(j + 1, 0, i)
                if scan:
                    hg_states(j, 0, len(H_BANKS), i)
                    hg_masks(j, i)
                hg_keys(j + 1, 0, i)
                hg_gates(j + 1, 1, i)
                if scan:
                    hg_out(j, i)
                hg_sums(j + 1, 1, i)
                hg_keys(j + 1, 1, i)

            hg_step(-1, scan=False)
            with dve.Fori(0, HH // 2 - 1) as i:
                own.enter(i, 2 * (4 + 2 + 1 + 3 + NC))
                hg_step(0, i)
                hg_step(1, i)
                own.leave(HH // 2 - 1)
            hg_step(HH - 2)
            hg_states(HH - 1, 0, len(H_BANKS))
            hg_masks(HH - 1)
            hg_out(HH - 1)

            low_parts(m_b, m_h["yb"], KT)
            with dve.Fori(0, KT // 2) as i:
                for c in range(2):
                    j = J_PB + 2 * c
                    dve.wait_ge(slot_free[j % 2], lin(j // 2 + 1, 2, i))
                    dve.wait_ge(dense_done, lin(j + 2, 4, i))
                    dve.wait_ge(ml_ok, lin(c, 2, i))
                    dve.tensor_tensor(prod[c], gate[c], slot[(j + 1) % 2][:, PC + N_META:], ALU.mult).then_inc(slot_free[(j + 1) % 2], 1)
                    dve.wait_ge(slot_free[(j + 1) % 2], lin((j + 1) // 2 + 1, 2, i))
                    dve.wait_ge(m_in[c], lin(16, 16, i))
                    dve.tensor_tensor(prod[c], prod[c], back[c], ALU.add).then_inc(mg_ok, 1)
                    dve.wait_ge(mg_ok, lin(c + 1, 2, i))
                    dve.wait_ge(mh_ok, lin(c + 1, 2, i))
                    t = bass.ds(i * 2 + c, 1)
                    dve.tensor_tensor(m_b["ml"][:, t, :], prod[c], m_b["mh"][:, t, :].bitcast(F32), ALU.subtract).then_inc(ml_ok, 1)
            clear_sum(3, (mg_ok, KT))
            dve.wait_ge(spill_in, 16)
            down(f2, N_META, J_WO, 3, True, 1.0)
            normed(f2["h"], "ffn2", 3, 2, N_META)
            ffn(J_FF2, f2, N_META, 4, D_FF // P)
            dve.wait_ge(rs_ok, 5)
            for t in range(KT):
                h = f2["h"][:, t, N_META:]
                dve.scalar_tensor_tensor(h, h, norm_w["final"][:, t:t + 1], rs[:, N_META:], ALU.mult, ALU.mult).then_inc(tmp_ok, 1)
            for c in range(0, NC, 2):
                dve.wait_ge(out_mm, c + 1)
                dve.wait_ge(out_ok, c)
                if c >= 2:
                    dve.wait_ge(out_done[c % 2], 16 * (c // 2))
                dve.tensor_copy(f2["io"][c % 2][:, :], slot[c % 2][:, :]).then_inc(out_ok, 1)

        @block.gpsimd
        def _(pool):
            own = Tally(pool, pool_step)

            def low(s, n=0, i=None):
                pool.wait_ge(w_hi, lin(s + 1, n, i))
                pool.tensor_tensor(wlo[s % 2][:, :, :], raw[s % 2][:, :, :], whi[s % 2][:, :, :].bitcast(F32), ALU.subtract).then_inc(w_lo, 1)

            pool.memset(ident[:, :], 0.0)
            pool.memset(ones[:, :], 1.0)
            pool.memset(ones_r[:, :].bitcast(F32), 1.0)
            pool.memset(eps[:, :], EPS)
            own.add(pool.memset(incl[0][:, :], 1.0))
            own.wait()
            sel = lambda out, fill, op, mult, step, base: own.add(pool.affine_select(
                out=out, in_=out, compare_op=op, fill=fill, base=base, pattern=[[step, P]], channel_multiplier=mult))
            own.wait()
            sel(ident[:, :], 1.0, ALU.not_equal, 1, -1, 0)
            for d in range(2):
                sg = 1 - 2 * d
                src = ones[:, :]
                own.add(pool.affine_select(out=strict[d][:, :], in_=src, compare_op=ALU.is_gt, fill=0.0, base=0,
                                           pattern=[[-sg, P]], channel_multiplier=sg))
                own.add(pool.affine_select(out=incl[d][:, :], in_=src, compare_op=ALU.is_ge, fill=0.0, base=0,
                                           pattern=[[sg, P]], channel_multiplier=-sg))
                own.add(pool.affine_select(out=incl64[d][:, :], in_=src, compare_op=ALU.is_ge, fill=0.0, base=0,
                                           pattern=[[sg, P]], channel_multiplier=-sg))
            own.wait()
            own.add(pool.memset(incl64[0][0:64, 64:P], 0.0))
            own.add(pool.memset(incl64[1][64:P, 0:64], 0.0))
            own.wait()
            pool.memset(eps[:, :], EPS).then_inc(const_ok, 1)

            def lows(s, count):
                with pool.Fori(0, count // 2) as i:
                    low(s, 2, i)
                    low(s + 1, 2, i)
                if count % 2:
                    low(s + count - 1)

            def normed(q, c0):
                for t in range(KT):
                    pool.wait_ge(xh_ok, KT * q + t + 1)
                    pool.tensor_tensor(xl[:, t, c0:], tmp[t % 2][:, c0:], xh[:, t, c0:].bitcast(F32), ALU.subtract).then_inc(xn_ok, 1)

            low(0)
            normed(0, 0)
            lows(1, J_DT)
            for b in range(2):
                pool.wait_ge(slot_free[(J_DT - 1 - b) % 2], (J_DT - 1 - b) // 2 + 1)
            pool.dma_start(h_spill, f1["h"][:, :, N_META:]).then_inc(spill_out, 16)
            normed(1, 0)
            low(J_DT + 1)

            U = len(S_UPD)

            def ssd_scan(g):
                pool.wait_ge(gat_ok, lin(2, 2, g))
                for n, (d, c) in enumerate(S_UPD):
                    q, k, m = (c - META, N_META, META) if c >= META else (c + 2, P, c)
                    pool.wait_ge(tr_ok, lin(NC + 2 if n else 2, NC + 2, g))
                    if n >= 2:
                        pool.wait_ge(up_mm, lin(n - 1, U, g))
                    h4 = lambda v: v.rearrange("p (h q) -> p h q", h=HPG)
                    pool.tensor_tensor(h4(m_s["xw"][n % 2][0:k, :]), h4(m_s["xbt"][0:k, q, 0:2 * P]),
                                       m_s["gw_t"][0:k, m, d, :].unsqueeze(2).broadcast_to([k, HPG, PD]), ALU.mult).then_inc(xw_ok, 1)

                def decays(c):
                    for d in range(2):
                        if c >= 1:
                            pool.wait_ge(seg_mm, lin(4 * (c - 1) + 2 * d + 2, 4 * NC, g))
                        pool.tensor_tensor(m_s["rl"][d][:, :, :], incl[d][:, :].unsqueeze(1).broadcast_to([P, HPG, P]),
                                           m_s["gal"][:, c, d, :].unsqueeze(2).broadcast_to([P, HPG, P]), ALU.mult).then_inc(rl_ok, 1)

                decays(0)
                for c in range(NC):
                    if c + 1 < NC:
                        decays(c + 1)
                    for d in range(2):
                        pool.wait_ge(exp_ok, lin(4 * c + 2 * d + 2, 4 * NC, g))
                        v = m_s["ea"][c % 2][d][:, :, :]
                        pool.tensor_tensor(v, v, m_s["co"][3][:, CO_CHUNK[c]:CO_CHUNK[c] + P].unsqueeze(1).broadcast_to([P, HPG, P]),
                                           ALU.mult).then_inc(ch_ok, 1)

            for c in range(6):
                low(J_SSD + c + 1)
            with pool.Fori(0, GROUPS - 1) as g:
                ssd_scan(g)
                for c in range(6):
                    low(J_SSD + 7 + c, 6, g)
            ssd_scan(GROUPS - 1)

            with pool.Fori(0, KT // 2) as i:
                for c in range(2):
                    j = J_PA + 2 * c
                    low(j + 1, 4, i)
                    low(j + 2, 4, i)
                    pool.wait_ge(slot_free[(j + 1) % 2], lin((j + 1) // 2 + 1, 2, i))
                    pool.dma_start(m_spill[bass.ds(i * 2 + c, 1)].rearrange("a p n -> p (a n)"), prod[c]).then_inc(pm_out[c], 16)

            def hg_queries(j, d, i=None):
                a = j % 2
                w = lambda sem_, v, n: pool.wait_ge(sem_, lin(v, 2 * n, i))
                w(dec_ok, 2 * j + d + 1, 2)
                w(e_ok, 4 * (2 * j + d) + 2, 8)
                jj = J_HG + 5 * j + 3
                pool.wait_ge(slot_free[jj % 2], lin(jj // 2 + 1, 5, i))
                for c in range(2):
                    v = m_h["q"][d][c][:, N_META:]
                    pool.tensor_tensor(v, v, hq[a], ALU.mult).then_inc(q_ok, 1)

            def hg_step(j, i=None):
                for c in range(4):
                    low(J_HG + 5 * (j + 1) + c + 1, 10, i)
                hg_queries(j + 1, 0, i)
                low(J_HG + 5 * (j + 2), 10, i)
                hg_queries(j + 1, 1, i)

            hg_step(-1)
            with pool.Fori(0, HH // 2 - 1) as i:
                hg_step(0, i)
                hg_step(1, i)
            hg_step(HH - 2)

            pool.wait_ge(yb_ok, HH)
            with pool.Fori(0, KT // 2) as i:
                for c in range(2):
                    j = J_PB + 2 * c
                    if c == 0:
                        pool.wait_ge(mg_ok, lin(0, 2, i))
                        for b in range(2):
                            pool.dma_start(back[b], m_spill[bass.ds(i * 2 + b, 1)].rearrange("a p n -> p (a n)")).then_inc(m_in[b], 16)
                    low(j + 1, 4, i)
                    low(j + 2, 4, i)
            pool.wait_ge(dense_done, J_WO)
            pool.dma_start(f2["h"][:, :, N_META:], h_spill).then_inc(spill_in, 16)
            lows(J_WO + 1, KT)
            normed(2, N_META)
            lows(J_FF2 + 1, FFN_JOBS - 1)


_INS = ["x_prompt", "x_sample", "meta_tokens", "ffn1_norm", "ffn1_w_gate_up", "ffn1_w_down", "mix_norm", "w_in",
        "ssd_conv_w", "ssd_conv_b", "ssd_dt_bias", "ssd_a_log", "ssd_d", "ssd_norm", "ssd_w_proj", "hg_lb_table",
        "hg_norm", "hg_w_proj", "w_out", "ffn2_norm", "ffn2_w_gate_up", "ffn2_w_down", "final_norm"]
_OUTS = [(1, 256, 1024), (1, 512, 1024)]


def kernel(**inputs):
    import numpy as _np
    import concourse.bacc as _bacc
    from concourse import mybir as _mybir
    from concourse.bass_utils import run_bass_kernel_spmd as _run

    nc = _bacc.Bacc("TRN2", target_bir_lowering=False, num_devices=1)
    arrays, args = {}, []
    for name in _INS:
        a = _np.ascontiguousarray(inputs[name])
        arrays[f"in_{name}"] = a
        args.append(nc.dram_tensor(f"in_{name}", a.shape, _mybir.dt.from_np(a.dtype), kind="ExternalInput").ap())
    for n, shape in enumerate(_OUTS):
        args.append(nc.dram_tensor(f"out_{n}", shape, _mybir.dt.float32, kind="ExternalOutput").ap())
    build(nc, *args)
    r = _run(nc, [arrays], core_ids=[0])
    return tuple(_np.asarray(r.results[0][f"out_{n}"]) for n in range(len(_OUTS)))
```

```python
from contextlib import ExitStack

import concourse.bass as bass
from concourse import mybir

P = 128
F32 = mybir.dt.float32
F32R = mybir.dt.float32r
I32 = mybir.dt.int32
ALU = mybir.AluOpType
ACT = mybir.ActivationFunctionType

D = 1024
KT = D // P
D_FF = 2816
N_META, N_P, N_S = 16, 256, 512
NT = N_META + N_P + N_S
NX = N_P + N_S
HEADS, GROUPS, HPG, STATE, PD = 16, 4, 4, 128, 64
TAPS = 5
HH = 8
EPS = 1e-6
BANK = 512
PC = 2 * BANK - NT
SPLIT = NT - BANK
Z0, X0, B0, C0, DT0 = 0, D, 2 * D, 2 * D + 512, 3 * D
HQ0 = DT0 + 2 * HEADS
HF0, HI0, HG0, GA0 = HQ0 + D, HQ0 + 3 * D, HQ0 + 4 * D, HQ0 + 5 * D
FF_GROUPS = [(0, 8), (8, 7), (15, 7)]
assert FF_GROUPS[-1][0] + FF_GROUPS[-1][1] == D_FF // P
CI = 2 + N_META + N_P + 2 + N_META + N_S + 2
CO = CI - (TAPS - 1)
CO_META = [0, N_META + N_P + 2]
NC = NX // P
CP = N_P // P
CO_CHUNK = [N_META + P * c + (0 if c < CP else 2 + N_META) for c in range(NC)]
META = NC

FFN_JOBS = sum(2 * n + KT for _, n in FF_GROUPS)
J_DT = FFN_JOBS
J_SSD = J_DT + 1
J_PA = J_SSD + 6 * GROUPS
J_HG = J_PA + 2 * KT
J_PB = J_HG + 5 * HH
J_WO = J_PB + 2 * KT
J_FF2 = J_WO + KT
JOBS = J_FF2 + FFN_JOBS


def lin(s, n=0, i=None):
    return s if i is None else i * n + s


def halves(c0):
    return ((c0, SPLIT), (SPLIT, NT))


class Tally:

    def __init__(self, eng, sem):
        self.eng, self.sem, self.n, self.stride, self.i, self.start = eng, sem, 0, 0, None, 0

    def add(self, ins):
        ins.then_inc(self.sem, 1)
        self.n += 1

    def wait(self, back=0):
        self.eng.wait_ge(self.sem, lin(self.n - back, self.stride, self.i))

    def enter(self, i, stride):
        self.i, self.stride, self.start = i, stride, self.n

    def leave(self, trips):
        assert self.n - self.start == self.stride, (self.n - self.start, self.stride)
        self.n = self.start + self.stride * trips
        self.i, self.stride = None, 0


def build(nc, x_prompt, x_sample, meta_tokens, ffn1_norm, ffn1_w_gate_up, ffn1_w_down, mix_norm, w_in,
          ssd_conv_w, ssd_conv_b, ssd_dt_bias, ssd_a_log, ssd_d, ssd_norm, ssd_w_proj, hg_lb_table,
          hg_norm, hg_w_proj, w_out, ffn2_norm, ffn2_w_gate_up, ffn2_w_down, final_norm, y_prompt, y_sample):
    ctx = ExitStack()
    with ctx:
        def sb(name, shape, dt=F32, where=ctx):
            return where.enter_context(nc.sbuf_tensor(name, shape, dt))

        def sem(name):
            return ctx.enter_context(nc.semaphore(name))

        xh = sb("xh", [P, KT, NT], F32R)
        xl = sb("xl", [P, KT, NT], F32R)
        raw = [sb(f"raw{s}", [P, KT, P]) for s in range(2)]
        whi = [sb(f"whi{s}", [P, KT, P], F32R) for s in range(2)]
        wlo = [sb(f"wlo{s}", [P, KT, P], F32R) for s in range(2)]
        vec_a = sb("vec_a", [P, P])
        vec_b = sb("vec_b", [P, 6 * KT])
        ident = sb("ident", [P, P])
        ones = sb("ones", [P, P])
        strict = [sb(f"strict{d}", [P, P], F32R) for d in range(2)]
        incl = [sb(f"incl{d}", [P, P]) for d in range(2)]
        incl64 = [sb(f"incl64{d}", [P, P]) for d in range(2)]
        eps = sb("eps", [P, 1])
        lb = sb("lb", [P, 2, KT])
        oml = sb("oml", [P, 2, KT])
        lbs = sb("lbs", [P, 4, 2, KT])
        dtb = sb("dtb", [2 * HEADS, 1])
        alog = sb("alog", [2 * HEADS, 1])
        aneg = sb("aneg", [2 * HEADS, 1])
        dt_t = sb("dt_t", [P, NC + 1, 2, HEADS])
        da_t = sb("da_t", [P, NC + 1, 2, HEADS])
        da_hi = sb("da_hi", [P, NC, 2, HEADS], F32R)
        da_lo = sb("da_lo", [P, NC, 2, HEADS], F32R)
        w_t = sb("w_t", [P, NC + 1, 2, HEADS])
        cd_t = sb("cd_t", [P, NC, 2, HEADS])
        ec_t = sb("ec_t", [P, NC, 2, HEADS])
        drow = sb("drow", [P, HEADS])
        acc = sb("acc", [P, NT])
        sq = [sb(f"sq{s}", [P, NT]) for s in range(2)]
        rs = sb("rs", [P, NT])
        tmp = [sb(f"tmp{s}", [P, NT]) for s in range(2)]

        cw = vec_a[:, 0:(TAPS + 1) * 16].rearrange("p (k t) -> p k t", t=16)
        lbt = vec_a[:, 96:128].rearrange("p (d l t) -> p d l t", d=2, l=2)
        norm_w = {n: vec_b[:, KT * k:KT * (k + 1)] for k, n in enumerate(["ffn1", "mix", "ssd", "hg", "ffn2", "final"])}

        def scope(make):
            with ExitStack() as s:
                return make(lambda name, shape, dt=F32: sb(name, shape, dt, s))

        def ffn_mem(new, t):
            return dict(h=new(f"h{t}", [P, KT, NT]), t=new(f"gate{t}", [P, NT]), p=new(f"prod{t}", [P, NT]),
                        ah=new(f"ah{t}", [P, 8, NT], F32R), al=new(f"al{t}", [P, 8, NT], F32R),
                        io=[new(f"io{t}_{s}", [P, D]) for s in range(2)],
                        xs=new(f"xs{t}", [P, 2, D]), va=new(f"va{t}", [P, P]), vb=new(f"vb{t}", [6 * KT, P]))

        f1 = scope(lambda new: ffn_mem(new, 1))
        f2 = scope(lambda new: ffn_mem(new, 2))
        m_dt = scope(lambda new: [new(f"dtw{k}", [2 * HEADS, NT]) for k in range(7)])
        m_s = scope(lambda new: dict(
            ya=new("ya", [P, KT, NX]), _pad=new("pad_s", [P, KT * N_META]),
            ci=[new(f"ci{s}", [P, CI]) for s in range(2)], ca=new("ca", [P, CO]),
            co=[new(f"co{s}", [P, CO]) for s in range(4)], gw=new("gw", [P, TAPS + 1, 4]), gn=new("gn", [P, 2]),
            gd=new("gd", [P, HPG]), gdt=new("gdt", [P, NC, 2, HPG]), gw_t=new("gw_t", [P, NC + 1, 2, HPG]),
            gcd=new("gcd", [P, NC, 2, HPG]), gec=new("gec", [P, NC, 2, HPG]),
            gah=new("gah", [P, NC, 2, HPG]), gal=new("gal", [P, NC, 2, HPG]),
            xbt=new("xbt", [P, NC + 2, 3 * P]), xw=new("xw", [P, 4, 2 * P]),
            xdt=[[new(f"xdt{s}{d}", [P, 2 * P]) for d in range(2)] for s in range(2)],
            prev=[new(f"prev{d}", [P, NC, 2 * P]) for d in range(2)],
            rh=[new(f"rh{u}", [P, HPG, P], F32R) for u in range(3)],
            rl=[new(f"rl{u}", [P, HPG, P], F32R) for u in range(3)],
            e=[new(f"e{u}", [P, HPG, P]) for u in range(4)]))
        m_a = scope(lambda new: dict(lo=new("ya_lo", [P, KT, NX], F32R), _pad=new("pad_a", [P, KT * N_META]),
                                     hi=new("ya_hi", [P, KT, NX], F32R)))
        m_h = scope(lambda new: dict(
            yb=new("yb", [P, KT, NX]), _pad=new("pad_h", [P, KT * N_META]),
            s=[[new(f"s{a}{d}", [P, NT]) for d in range(2)] for a in range(2)],
            v=[new(f"v{a}", [P, NT]) for a in range(2)], k=new("k", [P, NT]), b=new("b", [P, NT]),
            q=[[new(f"q{c}{d}", [P, NT]) for c in range(4)] for d in range(2)],
            reset=new("reset", [P, NT + 1]), dec=[new(f"dec{d}", [P, 2 * NC]) for d in range(2)],
            lo=new("hlo", [P, 2, 2]), nw=new("hnw", [P, 1]), turn=new("turn", [P, NC]),
            vt=new("vt", [P, NC + 1, P]), kt=[new(f"kt{d}", [P, NC + 1, P]) for d in range(2)],
            prev=[new(f"hprev{d}", [P, 2 * NC, P]) for d in range(2)],
            am=[[new(f"am{s}{d}", [P, P]) for d in range(2)] for s in range(2)]))
        m_b = scope(lambda new: dict(lo=new("yb_lo", [P, KT, NX], F32R), _pad=new("pad_b", [P, KT * N_META]),
                                     hi=new("yb_hi", [P, KT, NX], F32R), mh=new("mh", [P, KT, NX], F32R),
                                     ml=new("ml", [P, KT, NX], F32R)))
        x_sq = f1["xs"].rearrange("p s (t k) -> p s t k", k=P)
        nb = tmp + sq
        xws = [m_s["xw"][:, n, :] for n in range(4)] + [m_s["co"][n // 3][:, 2 * P * (n % 3):2 * P * (n % 3 + 1)] for n in range(6)]
        cbm = m_s["prev"][1].rearrange("p c (d t) -> p d c t", d=2)
        yoff = m_s["prev"][0]
        zs, ys = [v[:, 0:NX] for v in sq], [v[:, 0:NX] for v in tmp]
        gate, prod = zs, ys
        back = [v[:, 0:NX] for v in (rs, acc)]
        hg, hq = zs, ys
        dif, osq = rs, acc[:, 0:NX]

        slot = [ctx.enter_context(nc.psum_tensor(f"slot{s}", [P, 2 * BANK], F32)) for s in range(2)]
        aux2 = [ctx.enter_context(nc.psum_tensor(f"aux{s}", [P, 2 * BANK], F32)) for s in range(2)]
        out_ps = slot + aux2
        aux = [aux2[b // 2][:, BANK * (b % 2):BANK * (b % 2 + 1)] for b in range(4)]

        h_spill = nc.dram_tensor("h_spill", (P, KT, NX), F32, kind="Internal").ap()
        m_spill = nc.dram_tensor("m_spill", (KT, P, NX), F32, kind="Internal").ap()

        vec_in = sem("vec_in")
        const_ok = sem("const_ok")
        vec_mm = sem("vec_mm")
        lb_sub, lb_exp, dec_ok = sem("lb_sub"), sem("lb_exp"), sem("dec_ok")
        vec_ok = sem("vec_ok")
        x_in = [sem(f"x_in{s}") for s in range(2)]
        x_mm = sem("x_mm")
        x_ok = sem("x_ok")
        raw_in = [sem(f"raw_in{s}") for s in range(2)]
        w_hi, w_lo = sem("w_hi"), sem("w_lo")
        dense_done = sem("dense_done")
        slot_free = [sem(f"slot_free{s}") for s in range(2)]
        a_hi_ok, a_ok = sem("a_hi_ok"), sem("a_ok")
        sq_ok, acc_ok = sem("sq_ok"), sem("acc_ok")
        norm_mm, rs_ln, rs_ok = sem("norm_mm"), sem("rs_ln"), sem("rs_ok")
        tmp_ok, xh_ok = sem("tmp_ok"), sem("xh_ok")
        xn_ok = [sem("xn_even"), sem("xn_odd")]
        spill_out, spill_in = sem("spill_out"), sem("spill_in")
        dve_step, act_step, pool_step = sem("dve_step"), sem("act_step"), sem("pool_step")
        dt_exp, dt_ok, dt_mm, dt_tok, dt_sum, dt_dec, dt_all = (
            sem(n) for n in ("dt_exp", "dt_ok", "dt_mm", "dt_tok", "dt_sum", "dt_dec", "dt_all"))
        z_ok, conv_ok, co_ok, tr_mm, tr_ok = (sem(n) for n in ("z_ok", "conv_ok", "co_ok", "tr_mm", "tr_ok"))
        gat_ok, xw_ok, up_mm, up_ok = sem("gat_ok"), sem("xw_ok"), sem("up_mm"), sem("up_ok")
        off_mm, off_ok, yoff_ok = sem("off_mm"), sem("off_ok"), sem("yoff_ok")
        rh_ok, rl_ok, seg_mm, exp_ok = sem("rh_ok"), sem("rl_ok"), sem("seg_mm"), sem("exp_ok")
        cb_mm, cbm_ok, wy_ok = sem("cb_mm"), sem("cbm_ok"), sem("wy_ok")
        xdt_ok, y_mm, yz_ok, ya_ok = sem("xdt_ok"), sem("y_mm"), sem("yz_ok"), sem("ya_ok")
        pa_hi, pa_lo = sem("pa_hi"), sem("pa_lo")
        pm_out, m_in = [sem("pm_out0"), sem("pm_out1")], [sem("m_in0"), sem("m_in1")]
        f_ok, ln_ok, bc_ok, d_ok, e_ok, k_ok, q_ok = (sem(n) for n in ("f_ok", "ln_ok", "bc_ok", "d_ok", "e_ok", "k_ok", "q_ok"))
        ht_mm, ht_ok, kv_mm, kv_ok, a_mm, am_ok, o_mm = (
            sem(n) for n in ("ht_mm", "ht_ok", "kv_mm", "kv_ok", "a_mm", "am_ok", "o_mm"))
        osq_ok, os_mm, ors_ln, ors_ok, yb_ok = (sem(n) for n in ("osq_ok", "os_mm", "ors_ln", "ors_ok", "yb_ok"))
        mg_ok, mh_ok, ml_ok = sem("mg_ok"), sem("mh_ok"), sem("ml_ok")
        out_mm, out_ok = sem("out_mm"), [sem("out_ok0"), sem("out_ok1")]
        out_done = [sem("out_done0"), sem("out_done1")]

        S_UPD = [(0, META), (0, META + 1), (1, 1), (1, 5), (0, 0), (1, 4), (0, 2), (1, 3), (0, 3), (0, 4)]
        UP_BANK = [2, 3, 0, 1, 2]
        S_UNITS = [(c, d) for c in range(NC) for d in range(2)]
        S_STEPS = [((0, 1, 2), ()), ((3, 4, 5), (0,)), ((6, 7, 8), (1, 2)), ((9, 10, 11), (3,)), ((), (4, 5))]
        Y_STEP = [1, 2, 2, 3, 4, 4]

        def wait(eng, sem_, n, v, G):
            if G[1] is not None or v + n * G[0] > 0:
                eng.wait_ge(sem_, lin(v + n * G[0], n, G[1]))

        H_BANKS = [[(0, -1)], [(1, 3), (1, 11)], [(0, 0), (0, 4), (1, 2), (1, 10)], [(0, 1), (0, 5), (1, 1), (1, 9)],
                   [(0, 2), (0, 6), (1, 8)], [(0, 7), (1, 7)], [(0, 8), (1, 6)], [(0, 9), (1, 5)], [(0, 10)]]
        H_UPD = [v for b in H_BANKS for v in b]
        H_END = [sum(map(len, H_BANKS[:u + 1])) for u in range(len(H_BANKS))]
        X_TILES = [(meta_tokens, 0, N_META, 0)] + [(x_prompt[0], P * c, P, N_META + P * c) for c in range(CP)] + \
            [(x_sample[0], P * c, P, N_META + N_P + P * c) for c in range(NC - CP)]

        FFNS = [(0, f1, 0, ffn1_w_gate_up[0], ffn1_w_down[0]), (J_FF2, f2, N_META, ffn2_w_gate_up[0], ffn2_w_down[0])]

        def ffn_groups(j0):
            out = []
            for n, (f, k) in enumerate(FF_GROUPS):
                out.append((n, f, k, j0, j0 + 2 * k))
                j0 += 2 * k + KT
            return out

        block = ctx.enter_context(nc.Block())

        @block.sync
        def _(sp):
            def load(src, k, s, n=0, i=None):
                if s >= 2:
                    sp.wait_ge(w_lo, lin(s - 1, n, i))
                sp.dma_start(raw[s % 2][:, 0:k, :], src.rearrange("(k p) m -> p k m", p=P)).then_inc(raw_in[s % 2], 16)

            def at(i, step, base):
                return bass.ds(i * step + base if base else (i + 1) * step - step, P)

            rows = lambda v: v.rearrange("a (t p) -> (a t) p", p=P)
            for k in range(TAPS):
                sp.dma_start(f1["va"][16 * k:16 * (k + 1), :], ssd_conv_w[0, k].rearrange("(t p) -> t p", p=P)).then_inc(vec_in, 16)
            sp.dma_start(f1["va"][80:96, :], rows(ssd_conv_b)).then_inc(vec_in, 16)
            sp.dma_start(f1["va"][96:128, :], hg_lb_table.rearrange("d l (t p) -> (d l t) p", p=P)).then_inc(vec_in, 16)
            for k, v in enumerate((ffn1_norm, mix_norm, ssd_norm, hg_norm, ffn2_norm)):
                sp.dma_start(f1["vb"][KT * k:KT * (k + 1), :], rows(v)).then_inc(vec_in, 16)
            sp.dma_start(f1["vb"][5 * KT:6 * KT, :], final_norm.rearrange("(t p) -> t p", p=P)).then_inc(vec_in, 16)
            sp.dma_start(dtb[:, :], ssd_dt_bias.rearrange("a d h -> (d h) a")).then_inc(vec_in, 16)
            sp.dma_start(alog[:, :], ssd_a_log.rearrange("a d h -> (d h) a")).then_inc(vec_in, 16)
            sp.dma_start(drow[:, :], ssd_d.broadcast_to([P, HEADS])).then_inc(vec_in, 16)
            for n, (src, r, k, _) in enumerate(X_TILES):
                if n >= 2:
                    sp.wait_ge(x_mm, n - 1)
                sp.dma_start(f1["io"][n % 2][0:k, :], src[r:r + k, :]).then_inc(x_in[n % 2], 16)
                if n < 2:
                    load(FFNS[0][3][:, D_FF * n:D_FF * n + P], KT, n)

            def ffn(j0, _m, _c0, w_gu, w_down):
                for n, f, k, jg, jd in ffn_groups(j0):
                    first = 1 if jg == 0 else 0
                    with sp.Fori(first, k) as i:
                        load(w_gu[:, at(i, P, f * P)], KT, jg if jg >= 2 else 2, 2, i if jg >= 2 else i - 1)
                        load(w_gu[:, at(i, P, f * P + D_FF)], KT, jg + 1 if jg >= 2 else 3, 2, i if jg >= 2 else i - 1)
                    with sp.Fori(0, KT // 2) as i:
                        for c in range(2):
                            load(w_down[P * f:P * (f + k), at(i, 2 * P, c * P)], k, jd + c, 2, i)

            ffn(*FFNS[0])
            W = w_in[0]
            load(W[:, DT0:DT0 + P], KT, J_DT)
            with sp.Fori(0, GROUPS) as g:
                for c, (off, step) in enumerate(((X0, 2 * P), (X0 + P, 2 * P), (B0, P), (C0, P), (Z0, 2 * P), (Z0 + P, 2 * P))):
                    load(W[:, at(g, step, off)], KT, J_SSD + c, 6, g)
            with sp.Fori(0, KT // 2) as i:
                for c in range(2):
                    load(W[:, at(i, 2 * P, GA0 + c * P)], KT, J_PA + c, 4, i)
                for c in range(2):
                    load(ssd_w_proj[0][:, at(i, 2 * P, c * P)], KT, J_PA + 2 + c, 4, i)
            with sp.Fori(0, HH // 2) as i:
                for a in range(2):
                    for c, off in enumerate((HF0, HF0 + D, HI0, HQ0, HG0)):
                        load(W[:, at(i, 2 * P, off + a * P)], KT, J_HG + 5 * a + c, 10, i)
            with sp.Fori(0, KT // 2) as i:
                for c in range(2):
                    load(W[:, at(i, 2 * P, GA0 + D + c * P)], KT, J_PB + c, 4, i)
                for c in range(2):
                    load(hg_w_proj[0][:, at(i, 2 * P, c * P)], KT, J_PB + 2 + c, 4, i)
            with sp.Fori(0, KT // 2) as i:
                for c in range(2):
                    load(w_out[0][:, at(i, 2 * P, c * P)], KT, J_WO + c, 2, i)
            ffn(*FFNS[1])
            for c in range(NC):
                dst = y_prompt[0] if c < CP else y_sample[0]
                r = P * c if c < CP else P * (c - CP)
                sp.wait_ge(out_ok[c % 2], c // 2 + 1)
                sp.dma_start(dst[r:r + P, :], f2["io"][c % 2][:, :]).then_inc(out_done[c % 2], 16)
            for s in range(2):
                sp.wait_ge(out_done[s], 16 * (NC // 2))

        @block.tensor
        def _(pe):
            def job(k, hi, lo, c0, off, s, n=0, i=None, ready=None, late=False):
                b = s % 2
                pe.wait_ge(w_lo, lin(s + 1, n, i))
                pe.wait_ge(slot_free[b], lin(s // 2, n // 2, i))
                order = (((whi, hi), (wlo, hi)), ((whi, lo),)) if late else (((whi, hi), (whi, lo), (wlo, hi)),)
                for q, products in enumerate(order):
                    for t in range(k):
                        if ready:
                            if q == 0:
                                pe.wait_ge(ready[0], ready[2] + t)
                            if q == len(order) - 1:
                                low = ready[1]
                                if isinstance(low, list):
                                    pe.wait_ge(low[t % 2], (ready[2] - 1) // 2 + t // 2 + 1)
                                else:
                                    pe.wait_ge(low, ready[2] + t)
                        for p, (w, x) in enumerate(products):
                            for u, v in halves(c0):
                                mm = pe.matmul(slot[b][:, PC + u:PC + v], w[b][:, t, :], x[:, t, u + off:v + off],
                                               start=(t == 0 and p == 0 and q == 0),
                                               stop=(t == k - 1 and q == len(order) - 1 and p == len(products) - 1))
                mm.then_inc(dense_done, 1)

            def norm_sum(n, c0):
                pe.wait_ge(acc_ok, 9 * (n + 1))
                for u, v in halves(c0):
                    mm = pe.matmul(aux2[0][:, PC + u:PC + v], ones[:, :], acc[:, u:v], start=True, stop=True)
                mm.then_inc(norm_mm, 1)

            def ffn(j0, m, c0, r, nf):
                for n, f, k, jg, jd in ffn_groups(j0):
                    if n == 0:
                        for c in range(2):
                            job(KT, xh, xl, c0, 0, jg + c, ready=(xh_ok, xn_ok, KT * r + 1), late=(c == 0))
                    with pe.Fori(1 if n == 0 else 0, k) as i:
                        for c in range(2):
                            job(KT, xh, xl, c0, 0, jg + c, 2, i)
                    with pe.Fori(0, KT // 2) as i:
                        for c in range(2):
                            job(k, m["ah"], m["al"], c0, 0, jd + c, 2, i, (a_hi_ok, a_ok, nf + f + 1))

            pe.wait_ge(vec_in, 16 * 16)
            pe.wait_ge(const_ok, 1)
            pe.transpose(aux[0][:, 0:P], f1["va"][:, :], ident[:, :])
            pe.transpose(aux[0][:, P:P + 6 * KT], f1["vb"][:, :], ident[0:6 * KT, 0:6 * KT]).then_inc(vec_mm, 1)
            for n, (_, _, k, _) in enumerate(X_TILES):
                pe.wait_ge(x_in[n % 2], 16 * (n // 2 + 1))
                if n >= 2:
                    pe.wait_ge(x_ok, n - 1)
                for t in range(KT):
                    mm = pe.transpose(slot[n % 2][:, P * t:P * t + k], f1["io"][n % 2][0:k, P * t:P * (t + 1)], ident[0:k, 0:k])
                mm.then_inc(x_mm, 1)
            pe.wait_ge(vec_ok, 1)
            norm_sum(0, 0)
            pe.wait_ge(x_ok, len(X_TILES))
            ffn(0, f1, 0, 0, 0)
            norm_sum(1, 0)

            job(KT, xh, xl, 0, 0, J_DT, ready=(xh_ok, xn_ok, KT + 1), late=True)
            dtf, daf = m_dt[5], m_dt[6]

            def dt_part():
                pe.wait_ge(rs_ln, 2)
                pe.wait_ge(dt_ok, 2)
                for c in range(NC + 1):
                    k, t = (P, N_META + P * c) if c < NC else (N_META, 0)
                    for q, v in enumerate((dtf, daf)):
                        mm = pe.transpose(aux[0][0:k, 64 * c + 32 * q:64 * c + 32 * (q + 1)], v[:, t:t + k], ident[0:32, 0:32])
                mm.then_inc(dt_mm, 1)
                pe.wait_ge(dt_tok, 4)
                for d in range(2):
                    pe.matmul(aux[1][:, 0:32 * NC].rearrange("p (c d h) -> p c d h", d=2, h=HEADS)[:, :, d, :],
                              strict[d][:, :].bitcast(F32), da_t[:, 0:NC, d, :], start=True, stop=True, skip_group_check=True)
                pe.matmul(aux[1][:, 192:384], ones[:, :], da_t[:, 0:NC, :, :], start=True, stop=True, skip_group_check=True)
                for d in range(2):
                    pe.matmul(aux[2][:, 0:32 * NC].rearrange("p (c d h) -> p c d h", d=2, h=HEADS)[:, :, d, :],
                              incl[d][:, :], da_t[:, 0:NC, d, :], start=True, stop=True, skip_group_check=True)
                pe.matmul(aux[1][0:N_META, 384:400], strict[0][0:N_META, 0:N_META].bitcast(F32), da_t[0:N_META, META, 0, :],
                          start=True, stop=True, skip_group_check=True).then_inc(dt_sum, 1)

            def ssd_turn(G):
                wait(pe, co_ok, 4, 3, G)
                wait(pe, exp_ok, 2 * NC, 0, G)
                for n in range(NC + 2):
                    k, t = (N_META, CO_META[n]) if n < 2 else (P, CO_CHUNK[n - 2])
                    if n >= 2:
                        wait(pe, tr_ok, NC + 2, n - 1, G)
                    for q in range(3):
                        mm = pe.transpose(aux[n % 2][0:k, P * q:P * (q + 1)], m_s["co"][q][:, t:t + k], ident[:, :])
                    mm.then_inc(tr_mm, 1)

            def ssd_states(G):
                wait(pe, yz_ok, 2 * NC, 0, G)
                wait(pe, tr_ok, NC + 2, NC + 2, G)
                for n, (d, c) in enumerate(S_UPD):
                    q, k = (c - META, N_META) if c >= META else (c + 2, P)
                    wait(pe, xw_ok, len(S_UPD), n + 1, G)
                    if n == 8:
                        wait(pe, up_ok, len(S_UPD), 2, G)
                    h = 2 * P * (n % 2)
                    mm = pe.matmul(aux[UP_BANK[n // 2]][:, h:h + 2 * P], m_s["xbt"][0:k, q, 2 * P:3 * P], xws[n][0:k, :],
                                   start=True, stop=True)
                    if n % 2:
                        mm.then_inc(up_mm, 1)
                wait(pe, up_ok, len(S_UPD), len(S_UPD), G)
                wait(pe, co_ok, 4, 4, G)
                wait(pe, tr_ok, NC + 2, NC + 2, G)
                for c in range(NC):
                    t = CO_CHUNK[c]
                    mm = pe.matmul(aux[2 + c // 4][:, P * (c % 4):P * (c % 4 + 1)], m_s["co"][2][:, t:t + P], m_s["co"][3][:, t:t + P],
                                   start=True, stop=True)
                mm.then_inc(cb_mm, 1)
                for c in range(NC):
                    if c >= 2:
                        wait(pe, off_ok, NC, c - 1, G)
                    t = CO_CHUNK[c]
                    for d in range(2):
                        if not (d == 1 and c in (CP - 1, NC - 1)):
                            mm = pe.matmul(aux[c % 2][:, 2 * P * d:2 * P * (d + 1)], m_s["co"][3][:, t:t + P], m_s["prev"][d][:, c, :],
                                           start=True, stop=True)
                    mm.then_inc(off_mm, 1)

            def ssd_step(k, G):
                units, outs = S_STEPS[k]
                if k == 0:
                    wait(pe, off_ok, NC, NC, G)
                    wait(pe, cbm_ok, 4, 4, G)
                for u in units:
                    c, d = S_UNITS[u]
                    wait(pe, rh_ok, 2 * NC, u + 1, G)
                    wait(pe, rl_ok, 2 * NC, u + 1, G)
                    if u >= 3:
                        wait(pe, exp_ok, 2 * NC, u - 2, G)
                    for p, v in enumerate((m_s["rh"], m_s["rl"])):
                        mm = pe.matmul(aux[u % 3][:, :], strict[d][:, :], v[u % 3][:, :, :], start=(p == 0), stop=(p == 1))
                    mm.then_inc(seg_mm, 1)
                for c in outs:
                    wait(pe, wy_ok, 2 * NC, 2 * c + 2, G)
                    wait(pe, xdt_ok, 2 * NC, 2 * c + 2, G)
                    wait(pe, yz_ok, 2 * NC, 2 * outs[0], G)
                    wait(pe, yoff_ok, 1, 1, G)
                    for q in range(2):
                        h = 2 * P * (c % 2) + P * q
                        pe.matmul(aux[3][:, h:h + P], yoff[:, c, P * q:P * (q + 1)], ident[:, :], start=True, stop=False,
                                  skip_group_check=True)
                        for hh in (2 * q, 2 * q + 1):
                            for d in range(2):
                                mm = pe.matmul(aux[3][PD * (hh % 2):PD * (hh % 2 + 1), h:h + P], m_s["xdt"][c % 2][d][:, PD * hh:PD * (hh + 1)],
                                               m_s["e"][(2 * c + d) % 4][:, hh, :], start=False, stop=(d == 1), skip_group_check=True)
                if outs:
                    mm.then_inc(y_mm, 1)

            def ssd_job(c, G):
                job(KT, xh, xl, 0 if c < 4 else N_META, 0, J_SSD + 6 * G[0] + c, 6, G[1])

            first = (0, None)
            for c in range(5):
                ssd_job(c, first)
                if c == 2:
                    dt_part()
            pe.wait_ge(dt_all, 1)
            ssd_turn(first)
            ssd_job(5, first)
            ssd_states(first)
            with pe.Fori(0, GROUPS - 1) as g:
                G, N = (0, g), (1, g)
                for k in range(5):
                    ssd_job(k, N)
                    ssd_step(k, G)
                ssd_turn(N)
                ssd_job(5, N)
                ssd_states(N)

            def gated(s, hi, lo, ready, i):
                for c in range(2):
                    job(KT, xh, xl, N_META, 0, s + c, 4, i)
                for c in range(2, 4):
                    job(KT, hi, lo, N_META, -N_META, s + c, 4, i, ready)

            last = (GROUPS - 1, None)
            job(KT, xh, xl, N_META, 0, J_PA)
            ssd_step(0, last)
            ssd_step(1, last)
            job(KT, xh, xl, N_META, 0, J_PA + 1)
            for k in range(2, 5):
                ssd_step(k, last)
            norm_sum(2, N_META)
            for c in range(2, 4):
                job(KT, m_a["hi"], m_a["lo"], N_META, -N_META, J_PA + c, ready=(pa_hi, pa_lo, 1), late=(c == 2))
            with pe.Fori(1, KT // 2) as i:
                gated(J_PA, m_a["hi"], m_a["lo"], (pa_hi, pa_lo, 1), i)

            def hg_job(j, c, i=None):
                job(KT, xh, xl, 0 if c < 3 else N_META, 0, J_HG + 5 * j + c, 10, i)

            def hg_turn(j, i=None):
                s = j % 2
                pe.wait_ge(k_ok, lin(4 * (j + 1), 8, i))
                pe.wait_ge(ors_ln, lin(j, 2, i))
                pe.wait_ge(yb_ok, lin(j, 2, i))
                for n, (v, blocks) in enumerate(((m_h["v"][s], (0, 1, 2, 3)), (m_h["v"][s], (4, 5, META)),
                                                 (m_h["q"][0][3], (0, 1, 2, 3)), (m_h["q"][0][3], (4, 5, META)),
                                                 (m_h["q"][1][3], (0, 1, 2, 3)), (m_h["q"][1][3], (4, 5)))):
                    if n >= 4:
                        pe.wait_ge(ht_ok, lin(6 * j + n - 3, 12, i))
                    for q, c in enumerate(blocks):
                        k, t = (N_META, 0) if c == META else (P, N_META + P * c)
                        mm = pe.transpose(aux[n % 4][0:k, P * q:P * (q + 1)], v[:, t:t + k], ident[:, :])
                    mm.then_inc(ht_mm, 1)

            def hg_states(j, first, last, i=None):
                pe.wait_ge(ht_ok, lin(6 * j + 6, 12, i))
                for u in range(first, last):
                    if u >= 4:
                        pe.wait_ge(kv_ok, lin(len(H_UPD) * j + H_END[u - 4], 2 * len(H_UPD), i))
                    for q, (d, c) in enumerate(H_BANKS[u]):
                        r0, r1, p = (0, N_META, META) if c < 0 else (64 * (c % 2), 64 * (c % 2) + 64, c // 2)
                        mm = pe.matmul(aux[u % 4][:, P * q:P * (q + 1)], m_h["kt"][d][r0:r1, p, :], m_h["vt"][r0:r1, p, :],
                                       start=True, stop=True)
                    mm.then_inc(kv_mm, 1)

            def hg_outputs(j, i=None):
                def within(p):
                    if p < 2:
                        pe.wait_ge(kv_ok, lin(len(H_UPD) * j + H_END[(5, 8)[p]], 2 * len(H_UPD), i))
                    else:
                        pe.wait_ge(am_ok, lin(12 * j + 2 * (p - 1), 24, i))
                    t = N_META + P * p
                    for d in range(2):
                        mm = pe.matmul(aux[1 - p % 2][:, P * d:P * (d + 1)], m_h["q"][d][2][:, t:t + P], m_h["q"][d][1][:, t:t + P],
                                       start=True, stop=True)
                    mm.then_inc(a_mm, 1)

                pe.wait_ge(q_ok, lin(4 * (j + 1), 8, i))
                within(0)
                for p in range(NC):
                    if p + 1 < NC:
                        within(p + 1)
                    pe.wait_ge(am_ok, lin(12 * j + 2 * p + 2, 24, i))
                    out = aux2[1][:, 2 * P + P * p:2 * P + P * (p + 1)]
                    for d in range(2):
                        pe.matmul(out, m_h["vt"][:, p, :], m_h["am"][p % 2][d][:, :], start=(d == 0), stop=False,
                                  skip_group_check=True)
                    for u in range(2):
                        c, t = 2 * p + u, N_META + P * p + 64 * u
                        for d in range(2):
                            if d == 1 and c in (2 * CP - 1, 2 * NC - 1):
                                continue
                            mm = pe.matmul(out[:, 64 * u:64 * u + 64], m_h["prev"][d][:, c, :], m_h["q"][d][0][:, t:t + 64],
                                           start=False, stop=True, skip_group_check=True)
                    mm.then_inc(o_mm, 1)

            def hg_sums(j, i=None):
                pe.wait_ge(osq_ok, lin(j + 1, 2, i))
                for u, v in halves(N_META):
                    mm = pe.matmul(aux2[0][:, PC + u:PC + v], ones[:, :], osq[:, u - N_META:v - N_META], start=True, stop=True)
                mm.then_inc(os_mm, 1)

            def hg_step(j, i=None):
                hg_job(j + 1, 0, i)
                hg_turn(j, i)
                hg_job(j + 1, 1, i)
                hg_states(j, 0, 4, i)
                hg_job(j + 1, 2, i)
                hg_states(j, 4, len(H_BANKS), i)
                hg_outputs(j, i)
                hg_job(j + 1, 3, i)
                hg_sums(j, i)
                hg_job(j + 1, 4, i)

            for c in range(5):
                hg_job(0, c)
            with pe.Fori(0, HH // 2 - 1) as i:
                hg_step(0, i)
                hg_step(1, i)
            hg_step(HH - 2)
            job(KT, xh, xl, N_META, 0, J_PB)
            hg_turn(HH - 1)
            hg_states(HH - 1, 0, len(H_BANKS))
            hg_outputs(HH - 1)
            job(KT, xh, xl, N_META, 0, J_PB + 1)
            hg_sums(HH - 1)

            for c in range(2, 4):
                job(KT, m_b["hi"], m_b["lo"], N_META, -N_META, J_PB + c, ready=(pa_hi, pa_lo, KT + 1), late=(c == 2))
            with pe.Fori(1, KT // 2) as i:
                gated(J_PB, m_b["hi"], m_b["lo"], (pa_hi, pa_lo, KT + 1), i)
            with pe.Fori(0, KT // 2) as i:
                for c in range(2):
                    job(KT, m_b["mh"], m_b["ml"], N_META, -N_META, J_WO + c, 2, i, (mh_ok, ml_ok, 1))
            norm_sum(3, N_META)
            ffn(J_FF2, f2, N_META, 2, D_FF // P)
            norm_sum(4, N_META)

            for t in range(KT):
                pe.wait_ge(tmp_ok, 3 * KT + t + 1)
                for c in range(4):
                    u = N_META + P * c
                    mm = pe.transpose(out_ps[c][:, P * t:P * (t + 1)], f2["h"][:, t, u:u + P], ident[:, :])
                    if t == KT - 1:
                        mm.then_inc(out_mm, 1)
            for c in range(4, NC):
                pe.wait_ge(out_ok[c % 2], (c - 4) // 2 + 1)
                for t in range(KT):
                    u = N_META + P * c
                    mm = pe.transpose(out_ps[c % 4][:, P * t:P * (t + 1)], f2["h"][:, t, u:u + P], ident[:, :])
                mm.then_inc(out_mm, 1)

        @block.scalar
        def _(act):
            own = Tally(act, act_step)

            def split(s, n=0, i=None):
                act.wait_ge(raw_in[s % 2], lin(16 * (s // 2 + 1), 8 * n, i))
                if s >= 1:
                    act.wait_ge(dense_done, lin(s - 1, n, i))
                act.activation(whi[s % 2][:, :, :], raw[s % 2][:, :, :], ACT.Copy).then_inc(w_hi, 1)

            def read_out(s, n=0, i=None, dst=None, func=ACT.Copy, c0=0):
                act.wait_ge(dense_done, lin(s + 1, n, i))
                act.activation(dst, slot[s % 2][:, PC + c0:], func).then_inc(slot_free[s % 2], 1)

            def rms(r, c0):
                act.preload_act_table_set("natural_log")
                act.wait_ge(norm_mm, r + 1)
                act.activation(rs[:, c0:], aux2[0][:, PC + c0:], ACT.Ln, bias=eps[:, 0:1], scale=1.0 / D).then_inc(rs_ln, 1)
                act.wait_ge(rs_ln, r + 1)
                act.activation(rs[:, c0:], rs[:, c0:], ACT.Exp, scale=-0.5).then_inc(rs_ok, 1)

            def normed(r, c0):
                for t in range(KT):
                    act.wait_ge(tmp_ok, KT * r + t + 1)
                    act.activation(xh[:, t, c0:], nb[t % 4][:, c0:], ACT.Copy).then_inc(xh_ok, 1)

            def square(src, b, r, c0, t, n=0, i=None):
                act.wait_ge(acc_ok, lin(9 * r + t, n, i))
                act.activation(sq[b][:, c0:], src, ACT.Square).then_inc(sq_ok, 1)

            def down(m, c0, s, r, last):
                def pair(s, i, end=False):
                    for c in range(2):
                        if not (end and c == 1):
                            split(s + c + 1, 2, i)
                        if last:
                            act.wait_ge(slot_free[(s + c) % 2], lin((s + c) // 2 + 1, 1, i))
                            t = c if i is not None else KT - 2 + c
                            square(m["h"][:, t, c0:] if i is None else m["h"][:, bass.ds(i * 2 + c, 1), c0:],
                                   c, r, c0, t, 2, i)
                if s + KT == JOBS:
                    with act.Fori(0, KT // 2 - 1) as i:
                        pair(s, i)
                    pair(s + KT - 2, None, True)
                else:
                    with act.Fori(0, KT // 2) as i:
                        pair(s, i)

            def ffn(j0, m, c0, r):
                for n, f, k, jg, jd in ffn_groups(j0):
                    with act.Fori(0, k) as i:
                        split(jg + 1, 2, i)
                        act.wait_ge(slot_free[(jg + 1) % 2], lin((jg + 1) // 2, 1, i))
                        read_out(jg, 2, i, m["t"][:, c0:], ACT.Silu, c0)
                        split(jg + 2, 2, i)
                        act.wait_ge(slot_free[(jg + 1) % 2], lin((jg + 1) // 2 + 1, 1, i))
                        act.activation(m["ah"][:, bass.ds(i, 1), c0:], m["p"][:, c0:], ACT.Copy).then_inc(a_hi_ok, 1)
                    down(m, c0, jd, r, n == len(FF_GROUPS) - 1)

            act.wait_ge(lb_sub, 1)
            act.activation(lbs[:, 1:3, :, :], lbs[:, 1:3, :, :], ACT.Exp).then_inc(lb_exp, 1)
            act.activation(aneg[:, :], alog[:, :], ACT.Exp).then_inc(lb_exp, 1)
            for n, (_, _, k, t) in enumerate(X_TILES):
                if n == 0:
                    split(0)
                act.wait_ge(x_ok, n + 1)
                if n >= 2:
                    act.wait_ge(acc_ok, n)
                act.activation(x_sq[:, n % 2, :, 0:k], f1["h"][:, :, t:t + k],
                               ACT.Square).then_inc(sq_ok, 1 + (n == len(X_TILES) - 1))
            rms(0, 0)
            normed(0, 0)
            ffn(0, f1, 0, 1)
            rms(1, 0)
            normed(1, 0)

            split(J_DT + 1)
            e = m_dt[1]
            act.wait_ge(slot_free[J_DT % 2], J_DT // 2 + 1)
            own.add(act.activation(e[:, :], m_dt[0][:, :], ACT.Abs))
            own.wait()
            act.activation(e[:, :], e[:, :], ACT.Exp, scale=-1.0).then_inc(dt_exp, 1)

            def dt_decays():
                act.wait_ge(dt_sum, 1)
                act.activation(w_t[:, 0:NC, :, :], aux[1][:, 0:192].rearrange("p (c d h) -> p c d h", d=2, h=HEADS), ACT.Exp).then_inc(dt_dec, 1)
                act.activation(cd_t[:, :, :, :], aux[1][:, 192:384].rearrange("p (c d h) -> p c d h", d=2, h=HEADS), ACT.Exp).then_inc(dt_dec, 1)
                act.activation(w_t[0:N_META, META, 0, :], aux[1][0:N_META, 384:400], ACT.Exp).then_inc(dt_dec, 1)
                act.activation(ec_t[:, :, :, :], aux[2][:, 0:192].rearrange("p (c d h) -> p c d h", d=2, h=HEADS), ACT.Exp).then_inc(dt_dec, 1)

            def convolved(c, G):
                wait(act, conv_ok, 4, c + 1, G)
                act.activation(m_s["co"][c][:, :], m_s["ca"][:, :], ACT.Silu, bias=m_s["gw"][:, TAPS, c:c + 1]).then_inc(co_ok, 1)

            def ssd_split(c, G):
                split(J_SSD + 6 * G[0] + c + 1, 6, G[1])

            def ssd_read(c, G):
                s = J_SSD + 6 * G[0] + c
                if c >= 4:
                    wait(act, yz_ok, 2 * NC, 0, G)
                    read_out(s, 6, G[1], zs[c - 4], ACT.Silu, N_META)
                    return
                wait(act, conv_ok, 4, c - 1, G)
                act.wait_ge(z_ok, 2)
                act.wait_ge(dense_done, lin(s + 1, 6, G[1]))
                b, p = m_s["ci"][c % 2], slot[s % 2][:, PC:]
                own.add(act.activation(b[:, 2:2 + SPLIT], p[:, 0:SPLIT], ACT.Copy))
                own.add(act.activation(b[:, 4 + SPLIT:4 + SPLIT + N_META], p[:, 0:N_META], ACT.Copy))
                act.activation(b[:, 4 + SPLIT + N_META:4 + SPLIT + N_META + N_S], p[:, SPLIT:], ACT.Copy).then_inc(slot_free[s % 2], 1)

            def ssd_turn(G):
                wait(act, xdt_ok, 2 * NC, 0, G)
                for n in range(NC + 2):
                    k = N_META if n < 2 else P
                    wait(act, tr_mm, NC + 2, n + 1, G)
                    act.activation(m_s["xbt"][0:k, n, :], aux[n % 2][0:k, 0:3 * P], ACT.Copy).then_inc(tr_ok, 1)

            def ssd_step(k, G):
                for u in S_STEPS[k][0]:
                    wait(act, seg_mm, 2 * NC, u + 1, G)
                    wait(act, y_mm, 4, Y_STEP[(u - 4) // 2] if u >= 4 else 0, G)
                    act.activation(m_s["e"][u % 4][:, :, :], aux[u % 3].rearrange("p (h t) -> p h t", h=HPG), ACT.Exp).then_inc(exp_ok, 1)

            first = (0, None)
            for c in range(4):
                ssd_split(c, first)
                if c == 2:
                    dt_decays()
                if c >= 2:
                    convolved(c - 2, first)
                ssd_read(c, first)
            convolved(2, first)
            ssd_split(4, first)
            convolved(3, first)
            ssd_turn(first)
            ssd_read(4, first)
            ssd_split(5, first)
            ssd_read(5, first)
            with act.Fori(0, GROUPS - 1) as g:
                G, N = (0, g), (1, g)
                for k in range(4):
                    ssd_split(k, N)
                    if k:
                        convolved(k - 1, N)
                    ssd_read(k, N)
                    ssd_step(k, G)
                ssd_split(4, N)
                convolved(3, N)
                ssd_turn(N)
                ssd_read(4, N)
                ssd_split(5, N)
                ssd_read(5, N)
            def parts(hi, src, ready):
                act.wait_ge(ready, KT)
                for t in range(KT):
                    act.activation(hi[:, t, :], src[:, t, :], ACT.Copy).then_inc(pa_hi, 1)

            def sigmoid(s, c, i=None):
                read_out(s + c, 4, i, gate[c], ACT.Sigmoid, N_META)

            last = (GROUPS - 1, None)
            split(J_PA + 1)
            ssd_step(0, last)
            ssd_step(1, last)
            split(J_PA + 2)
            ssd_step(2, last)
            ssd_step(3, last)
            act.wait_ge(yz_ok, 2 * NC * GROUPS)
            sigmoid(J_PA, 0)
            sigmoid(J_PA, 1)
            split(J_PA + 3)
            parts(m_a["hi"], m_s["ya"], ya_ok)
            rms(2, N_META)
            split(J_PA + 4)
            with act.Fori(1, KT // 2) as i:
                split(J_PA + 1, 4, i)
                sigmoid(J_PA, 0, i)
                split(J_PA + 2, 4, i)
                sigmoid(J_PA, 1, i)
                split(J_PA + 3, 4, i)
                split(J_PA + 4, 4, i)

            def hg_log(j, d, i=None):
                f = m_h["s"][j % 2][d]
                act.preload_act_table_set("natural_log")
                act.wait_ge(f_ok, lin(2 * j + d + 1, 4, i))
                act.activation(f[:, N_META * d:], f[:, N_META * d:], ACT.Ln).then_inc(ln_ok, 1)

            def hg_exps(j, d, i=None):
                q, b = m_h["q"][d], m_h["b"]
                act.wait_ge(bc_ok, lin(2 * j + d + 1, 4, i))
                act.wait_ge(o_mm, lin(NC * j, 2 * NC, i))
                act.activation(q[0][:, N_META:], b[:, N_META:], ACT.Exp).then_inc(e_ok, 1)
                act.wait_ge(d_ok, lin(2 * (2 * j + d) + 1, 8, i))
                act.activation(q[1][:, N_META:], dif[:, N_META:], ACT.Exp).then_inc(e_ok, 1)
                act.activation(q[2][:, N_META:], dif[:, N_META:], ACT.Exp, scale=-1.0).then_inc(e_ok, 1)

            def hg_end_exp(j, d, i=None):
                f = m_h["s"][j % 2][d]
                act.wait_ge(d_ok, lin(2 * (2 * j + d) + 2, 8, i))
                act.activation(m_h["q"][d][3][:, N_META * d:], f[:, N_META * d:], ACT.Exp).then_inc(e_ok, 1)

            def hg_read(j, c, i=None):
                a = j % 2
                if c == 4 and j >= 1:
                    act.wait_ge(yb_ok, lin(j - 1, 2, i))
                if c == 3 and j >= 1:
                    act.wait_ge(q_ok, lin(4 * (j - 1), 8, i))
                dst, func = ((m_h["s"][a][0][:, :], ACT.Sigmoid), (m_h["s"][a][1][:, :], ACT.Sigmoid),
                             (m_h["v"][a][:, :], ACT.Copy), (hq[a], ACT.Silu), (hg[a], ACT.Silu))[c]
                read_out(J_HG + 5 * j + c, 10, i, dst, func, 0 if c < 3 else N_META)

            def hg_turn(j, i=None):
                vt, kt = m_h["vt"], m_h["kt"]
                for n, (dst, c, m) in enumerate(((vt, 0, 0), (vt, 4, 1), (kt[0], 0, 0), (kt[0], 4, 1), (kt[1], 0, 0), (kt[1], 4, 0))):
                    act.wait_ge(ht_mm, lin(6 * j + n + 1, 12, i))
                    k = 4 if c == 0 else 2
                    ins = act.activation(dst[:, c:c + k, :], aux[n % 4][:, 0:P * k].rearrange("p (c k) -> p c k", k=P), ACT.Copy)
                    if m:
                        ins = act.activation(dst[0:N_META, META, :], aux[n % 4][0:N_META, 2 * P:3 * P], ACT.Copy)
                    ins.then_inc(ht_ok, 1)

            def hg_squares(j, i=None):
                act.wait_ge(o_mm, lin(NC * (j + 1), 2 * NC, i))
                act.wait_ge(yb_ok, lin(j, 2, i))
                act.activation(osq, aux2[1][:, PC + N_META:], ACT.Square).then_inc(osq_ok, 1)

            def hg_rms(j, i=None):
                act.preload_act_table_set("natural_log")
                act.wait_ge(os_mm, lin(j + 1, 2, i))
                act.activation(osq, aux2[0][:, PC + N_META:], ACT.Ln, bias=eps[:, 0:1], scale=1.0 / P).then_inc(ors_ln, 1)
                act.wait_ge(ors_ln, lin(j + 1, 2, i))
                act.activation(osq, osq, ACT.Exp, scale=-0.5).then_inc(ors_ok, 1)

            def hg_step(j, i=None, scan=True):
                n, s = j + 1, J_HG + 5 * (j + 1)
                split(s + 1, 10, i)
                hg_read(n, 0, i)
                if scan:
                    hg_turn(j, i)
                hg_log(n, 0, i)
                split(s + 2, 10, i)
                hg_read(n, 1, i)
                split(s + 3, 10, i)
                hg_read(n, 2, i)
                if scan:
                    hg_squares(j, i)
                hg_exps(n, 0, i)
                hg_end_exp(n, 0, i)
                split(s + 4, 10, i)
                hg_read(n, 3, i)
                if scan:
                    hg_rms(j, i)
                hg_log(n, 1, i)
                split(s + 5, 10, i)
                hg_exps(n, 1, i)
                hg_read(n, 4, i)
                hg_end_exp(n, 1, i)

            act.wait_ge(pm_out[0], 16 * (KT // 2))
            act.wait_ge(pm_out[1], 16 * (KT // 2))
            hg_step(-1, scan=False)
            with act.Fori(0, HH // 2 - 1) as i:
                hg_step(0, i)
                hg_step(1, i)
            hg_step(HH - 2)
            split(J_PB + 1)
            hg_turn(HH - 1)
            act.wait_ge(yb_ok, HH - 1)
            sigmoid(J_PB, 0)
            hg_squares(HH - 1)
            split(J_PB + 2)
            hg_rms(HH - 1)
            act.wait_ge(yb_ok, HH)
            sigmoid(J_PB, 1)
            split(J_PB + 3)

            def merged(c, i):
                act.wait_ge(mg_ok, lin(c + 1, 2, i))
                act.activation(m_b["mh"][:, c:c + 1, :] if i is None else m_b["mh"][:, bass.ds(i * 2 + c, 1), :], prod[c], ACT.Copy).then_inc(mh_ok, 1)

            parts(m_b["hi"], m_h["yb"], yb_ok)
            split(J_PB + 4)
            merged(0, None)
            merged(1, None)
            with act.Fori(1, KT // 2) as i:
                split(J_PB + 1, 4, i)
                sigmoid(J_PB, 0, i)
                split(J_PB + 2, 4, i)
                sigmoid(J_PB, 1, i)
                split(J_PB + 3, 4, i)
                split(J_PB + 4, 4, i)
                merged(0, i)
                merged(1, i)
            down(f2, N_META, J_WO, 3, True)
            rms(3, N_META)
            normed(2, N_META)
            ffn(J_FF2, f2, N_META, 4)
            rms(4, N_META)
            for c in range(1, NC, 2):
                act.wait_ge(out_mm, c + 1)
                if c >= 2:
                    act.wait_ge(out_done[c % 2], 16 * (c // 2))
                act.activation(f2["io"][c % 2][:, :], out_ps[c % 4][:, :], ACT.Copy).then_inc(out_ok[1], 1)

        @block.vector
        def _(dve):
            own = Tally(dve, dve_step)

            def one(ins):
                own.add(ins)
                own.wait()

            def squares_sum(r, c0, b, t, n=0, i=None):
                dve.wait_ge(sq_ok, lin(KT * (r if r < 2 else r - 1) + t + 1, n, i))
                dve.wait_ge(acc_ok, lin(9 * r + 1 + t, n, i))
                dve.tensor_tensor(acc[:, c0:], acc[:, c0:], sq[b][:, c0:], ALU.add).then_inc(acc_ok, 1)

            def clear_sum(r, used):
                dve.wait_ge(*used)
                dve.memset(acc[:, :], 0.0).then_inc(acc_ok, 1)

            def normed(h, w, r, q, c0):
                dve.wait_ge(rs_ok, r + 1)
                def low(t):
                    dve.wait_ge(xh_ok, KT * q + t + 1)
                    dve.tensor_tensor(xl[:, t, c0:], nb[t % 4][:, c0:], xh[:, t, c0:].bitcast(F32), ALU.subtract).then_inc(xn_ok[1], 1)

                for t in range(KT):
                    if t >= 4:
                        dve.wait_ge(xn_ok[t % 2], KT // 2 * q + t // 2 - 1)
                    dve.scalar_tensor_tensor(nb[t % 4][:, c0:], h[:, t, c0:], norm_w[w][:, t:t + 1], rs[:, c0:],
                                             ALU.mult, ALU.mult).then_inc(tmp_ok, 1)
                    if t in (2, 4, 6):
                        low(t - 1)
                low(KT - 1)

            def down(m, c0, s, r, last, scale):
                with dve.Fori(0, KT // 2) as i:
                    for c in range(2):
                        j = s + c
                        hm = m["h"][:, bass.ds(i * 2 + c, 1), c0:]
                        dve.wait_ge(dense_done, lin(j + 1, 2, i))
                        dve.scalar_tensor_tensor(hm, slot[j % 2][:, PC + c0:], scale, hm, ALU.mult, ALU.add).then_inc(slot_free[j % 2], 1)
                        if last:
                            squares_sum(r, c0, c, c, 2, i)

            def ffn(j0, m, c0, r, nf):
                for n, f, k, jg, jd in ffn_groups(j0):
                    with dve.Fori(0, k) as i:
                        b = (jg + 1) % 2
                        dve.wait_ge(slot_free[jg % 2], lin(jg // 2 + 1, 1, i))
                        dve.wait_ge(dense_done, lin(jg + 2, 2, i))
                        dve.wait_ge(a_ok, lin(nf + f, 1, i))
                        dve.tensor_tensor(m["p"][:, c0:], m["t"][:, c0:], slot[b][:, PC + c0:], ALU.mult).then_inc(slot_free[b], 1)
                        dve.wait_ge(slot_free[b], lin((jg + 1) // 2 + 1, 1, i))
                        dve.wait_ge(a_hi_ok, lin(nf + f + 1, 1, i))
                        dve.tensor_tensor(m["al"][:, bass.ds(i, 1), c0:], m["p"][:, c0:], m["ah"][:, bass.ds(i, 1), c0:].bitcast(F32),
                                          ALU.subtract).then_inc(a_ok, 1)
                    last = n == len(FF_GROUPS) - 1
                    if last:
                        clear_sum(r, (norm_mm, r))
                    down(m, c0, jd, r, last, 0.5)

            dve.memset(acc[:, :], 0.0).then_inc(acc_ok, 1)
            dve.wait_ge(vec_mm, 1)
            own.add(dve.tensor_copy(vec_a[:, :], aux[0][:, 0:P]))
            one(dve.tensor_copy(vec_b[:, :], aux[0][:, P:P + 6 * KT]))
            one(dve.tensor_tensor(lbs[:, 0], lbt[:, :, 0, :], lbt[:, :, 1, :], ALU.max))
            for q in range(2):
                ins = dve.tensor_tensor(lbs[:, 1 + q], lbt[:, :, q, :], lbs[:, 0], ALU.subtract)
                if q == 0:
                    own.add(ins)
            ins.then_inc(lb_sub, 1)
            dve.wait_ge(lb_exp, 2)
            own.add(dve.tensor_scalar(aneg[:, :], aneg[:, :], -1.0, None, ALU.mult))
            one(dve.tensor_tensor(lbs[:, 3], lbs[:, 1], lbs[:, 2], ALU.add))
            one(dve.reciprocal(lbs[:, 3], lbs[:, 3]))
            one(dve.tensor_tensor(lb[:, :, :], lbs[:, 1], lbs[:, 3], ALU.mult))
            dve.tensor_scalar(oml[:, :, :], lb[:, :, :], -1.0, 1.0, ALU.mult, ALU.add).then_inc(vec_ok, 1)
            dve.wait_ge(vec_ok, 1)
            def square_sum(n):
                _, _, k, t = X_TILES[n]
                last = n == len(X_TILES) - 1
                dve.wait_ge(sq_ok, n + 1 + last)
                dve.tensor_reduce(acc[:, t:t + k], x_sq[:, n % 2, :, 0:k].rearrange("p t k -> p k t"), mybir.AxisListType.X,
                                  ALU.add).then_inc(acc_ok, 1 + last)

            for n, (_, _, k, t) in enumerate(X_TILES):
                dve.wait_ge(x_mm, n + 1)
                dve.tensor_copy(f1["h"][:, :, t:t + k], slot[n % 2][:, :].rearrange("p (t k) -> p t k", k=P)[:, :, 0:k]).then_inc(x_ok, 1)
                if n == 0:
                    dve.wait_ge(acc_ok, 1)
                else:
                    square_sum(n - 1)
            square_sum(len(X_TILES) - 1)
            dve.wait_ge(x_ok, len(X_TILES))
            normed(f1["h"], "ffn1", 0, 0, 0)
            ffn(0, f1, 0, 1, 0)
            normed(f1["h"], "mix", 1, 1, 0)

            dx, e, s, s2, poly, dtf, daf = m_dt
            dve.wait_ge(spill_out, 16)
            dve.wait_ge(tmp_ok, 2 * KT)
            dve.wait_ge(dense_done, J_DT + 1)
            dve.tensor_scalar(dx[:, :], slot[J_DT % 2][0:32, PC:], dtb[:, 0:1], None, ALU.add).then_inc(slot_free[J_DT % 2], 1)
            clear_sum(2, (norm_mm, 2))
            for b in range(2):
                dve.memset(m_s["ci"][b][:, :], 0.0).then_inc(z_ok, 1)
            dve.wait_ge(dt_exp, 1)
            one(dve.tensor_scalar(s2[:, :], e[:, :], 2.0, None, ALU.add))
            one(dve.reciprocal(s[:, :], s2[:, :]))
            one(dve.tensor_tensor(s[:, :], e[:, :], s[:, :], ALU.mult))
            one(dve.tensor_tensor(s2[:, :], s[:, :], s[:, :], ALU.mult))
            one(dve.tensor_scalar(poly[:, :], s2[:, :], 1.0 / 15, None, ALU.mult))
            for k in range(13, 1, -2):
                one(dve.scalar_tensor_tensor(poly[:, :], poly[:, :], 1.0 / k, s2[:, :], ALU.add, ALU.mult))
            one(dve.scalar_tensor_tensor(poly[:, :], poly[:, :], 1.0, s[:, :], ALU.add, ALU.mult))
            one(dve.tensor_scalar(dx[:, :], dx[:, :], 0.0, None, ALU.max))
            dve.scalar_tensor_tensor(dtf[:, :], poly[:, :], 2.0, dx[:, :], ALU.mult, ALU.add).then_inc(dt_ok, 1)
            dve.wait_ge(dt_ok, 1)
            dve.tensor_scalar(daf[:, :], dtf[:, :], aneg[:, 0:1], None, ALU.mult).then_inc(dt_ok, 1)
            dve.wait_ge(dt_mm, 1)
            both = aux[0][:, 0:64 * NC].rearrange("p (c q h) -> p c q h", q=2, h=2 * HEADS)
            flat = lambda v: v.rearrange("p c d h -> p c (d h)")
            dve.tensor_copy(flat(da_t[:, 0:NC]), both[:, :, 1, :]).then_inc(dt_tok, 1)
            dve.tensor_copy(flat(da_t[0:N_META, NC:NC + 1]), aux[0][0:N_META, 64 * NC + 32:64 * NC + 64]).then_inc(dt_tok, 1)
            dve.tensor_copy(flat(dt_t[:, 0:NC]), both[:, :, 0, :]).then_inc(dt_tok, 1)
            dve.tensor_copy(flat(dt_t[0:N_META, NC:NC + 1]), aux[0][0:N_META, 64 * NC:64 * NC + 32]).then_inc(dt_tok, 1)
            dve.wait_ge(dt_tok, 4)
            one(dve.tensor_copy(da_hi[:, :, :, :], da_t[:, 0:NC]))
            own.add(dve.tensor_tensor(da_lo[:, :, :, :], da_t[:, 0:NC], da_hi[:, :, :, :].bitcast(F32), ALU.subtract))
            dve.wait_ge(dt_dec, 4)
            own.add(dve.tensor_tensor(w_t[0:N_META, META, 0, :], w_t[0:N_META, META, 0, :], dt_t[0:N_META, META, 0, :], ALU.mult))
            own.wait()
            dve.tensor_tensor(w_t[:, 0:NC], w_t[:, 0:NC], dt_t[:, 0:NC], ALU.mult).then_inc(dt_all, 1)
            dve.wait_ge(dt_all, 1)

            def wide(v):
                return v.unsqueeze(2).broadcast_to([P, HPG, PD])

            heads4 = lambda v: v.rearrange("p (h q) -> p h q", h=HPG)
            U = len(S_UPD)
            ca, prev = m_s["ca"], m_s["prev"]

            def some(v, step, n, G, off=0):
                a = step * G[0] + off
                return v[..., a:a + n] if G[1] is None else v[..., bass.ds(G[1] * step + a if a else (G[1] + 1) * step - step, n)]

            def conv_vectors(G):
                wait(dve, co_ok, 4, 0, G)
                for c, (step, n, off) in ((0, (2, 2, 0)), (2, (1, 1, 8)), (3, (1, 1, 12))):
                    own.add(dve.tensor_copy(m_s["gw"][:, :, c:c + n], some(cw, step, n, G, off)))
                own.wait()

            def convolve(c, G):
                s = J_SSD + 6 * G[0] + c
                dve.wait_ge(slot_free[s % 2], lin(s // 2 + 1, 3, G[1]))
                wait(dve, co_ok, 4, c, G)
                ci = m_s["ci"][c % 2]
                one(dve.tensor_scalar(ca[:, :], ci[:, 0:CO], m_s["gw"][:, 0, c:c + 1], None, ALU.mult))
                for k in range(1, TAPS):
                    ins = dve.scalar_tensor_tensor(ca[:, :], ci[:, k:k + CO], m_s["gw"][:, k, c:c + 1], ca[:, :], ALU.mult, ALU.add)
                    if k < TAPS - 1:
                        one(ins)
                ins.then_inc(conv_ok, 1)

            def scan_vectors(G):
                wait(dve, rl_ok, 2 * NC, 0, G)
                wait(dve, xw_ok, U, 0, G)
                wait(dve, xdt_ok, 2 * NC, 0, G)
                for dst, src in (("gd", drow), ("gdt", dt_t[:, 0:NC]), ("gcd", cd_t), ("gec", ec_t),
                                 ("gah", da_hi[:, :, :, :].bitcast(F32)), ("gal", da_lo[:, :, :, :].bitcast(F32))):
                    own.add(dve.tensor_copy(m_s[dst][...], some(src, HPG, HPG, G)))
                dve.tensor_copy(m_s["gw_t"][:, 0:NC, :, :], some(w_t[:, 0:NC], HPG, HPG, G)).then_inc(gat_ok, 1)
                dve.tensor_copy(m_s["gw_t"][0:N_META, META, 0, :], some(w_t[0:N_META, META, 0, :], HPG, HPG, G)).then_inc(gat_ok, 1)
                own.wait()

            def ssd_states(G):
                for n, (d, c) in enumerate(S_UPD):
                    up = aux[UP_BANK[n // 2]][:, 2 * P * (n % 2):2 * P * (n % 2 + 1)]
                    if c >= META or (d == 1 and c in (CP - 1, NC - 1)):
                        dst = prev[d][:, 0 if c == META else CP if c > META else c - 1, :]
                        wait(dve, up_mm, U // 2, n // 2 + 1, G)
                        dve.tensor_copy(dst, up).then_inc(up_ok, 1)
                    else:
                        dst = prev[d][:, c + 1 if d == 0 else c - 1, :]
                        wait(dve, up_ok, U, n, G)
                        one(dve.tensor_tensor(heads4(dst), heads4(prev[d][:, c, :]), wide(m_s["gcd"][:, c, d, :]), ALU.mult))
                        wait(dve, up_mm, U // 2, n // 2 + 1, G)
                        dve.tensor_tensor(dst, dst, up, ALU.add).then_inc(up_ok, 1)
                for c in range(NC):
                    wait(dve, off_mm, NC, c + 1, G)
                    two = c not in (CP - 1, NC - 1)
                    for d in range(1 + two):
                        ins = dve.tensor_tensor(heads4(prev[d][:, c, :]), heads4(aux[c % 2][:, 2 * P * d:2 * P * (d + 1)]),
                                                wide(m_s["gec"][:, c, d, :]), ALU.mult)
                        if d < two:
                            own.add(ins)
                    ins.then_inc(off_ok, 1)
                wait(dve, off_ok, NC, NC, G)
                for u, v in ((0, CP - 1), (CP, NC - 1)):
                    own.add(dve.tensor_tensor(yoff[:, u:v, :], yoff[:, u:v, :], prev[1][:, u:v, :], ALU.add))
                own.wait()
                one(dve.tensor_tensor(prev[1].rearrange("p c (h q) -> p c h q", h=HPG),
                                      m_s["xbt"][:, 2:NC + 2, 0:2 * P].rearrange("p c (h q) -> p c h q", h=HPG),
                                      m_s["gd"][:, :].unsqueeze(1).unsqueeze(3).broadcast_to([P, NC, HPG, PD]), ALU.mult))
                dve.tensor_tensor(yoff[:, :, :], yoff[:, :, :], prev[1][:, :, :], ALU.add).then_inc(yoff_ok, 1)
                wait(dve, yoff_ok, 1, 1, G)
                wait(dve, cb_mm, 1, 1, G)
                for d in range(2):
                    for u, v in ((0, 4), (4, NC)):
                        dve.tensor_tensor(cbm[:, d, u:v, :], aux[2 + u // 4][:, 0:P * (v - u)].rearrange("p (c t) -> p c t", t=P),
                                          incl[d][:, :].unsqueeze(1).broadcast_to([P, v - u, P]), ALU.mult).then_inc(cbm_ok, 1)

            def decays(k, G):
                for u in S_STEPS[k][0]:
                    c, d = S_UNITS[u]
                    wait(dve, seg_mm, 2 * NC, max(u - 2, 0), G)
                    dve.tensor_tensor(m_s["rh"][u % 3][:, :, :], incl[d][:, :].unsqueeze(1).broadcast_to([P, HPG, P]),
                                      m_s["gah"][:, c, d, :].unsqueeze(2).broadcast_to([P, HPG, P]), ALU.mult).then_inc(rh_ok, 1)

            def gates(chunks, G):
                for c in chunks:
                    wait(dve, y_mm, 4, Y_STEP[c], G)
                    for q in range(2):
                        s = J_SSD + 6 * G[0] + 4 + q
                        dve.wait_ge(slot_free[s % 2], lin(s // 2 + 1, 3, G[1]))
                        h = 2 * P * (c % 2) + P * q
                        dve.tensor_tensor(ys[q][:, P * c:P * (c + 1)], aux[3][:, h:h + P], zs[q][:, P * c:P * (c + 1)], ALU.mult).then_inc(yz_ok, 1)

            def masked(k, G):
                units = S_STEPS[k][0]
                wait(dve, cbm_ok, 4, 4, G)
                for u in units:
                    c, d = S_UNITS[u]
                    wait(dve, exp_ok, 2 * NC, u + 1, G)
                    v = m_s["e"][u % 4][:, :, :]
                    dve.tensor_tensor(v, v, cbm[:, d, c, :].unsqueeze(1).broadcast_to([P, HPG, P]), ALU.mult).then_inc(wy_ok, 1)

            def weighted(G):
                wait(dve, ya_ok, 2, 0, G)
                one(dve.tensor_copy(m_s["gn"][:, :], some(norm_w["ssd"], 2, 2, G)))
                wait(dve, yz_ok, 2 * NC, 2 * NC, G)
                for q in range(2):
                    one(dve.tensor_tensor(rs[:, N_META:], ys[q], ys[q], ALU.mult))
                    wait(dve, acc_ok, 2, 9 * 2 + 1 + q, G)
                    dve.tensor_tensor(acc[:, N_META:], acc[:, N_META:], rs[:, N_META:], ALU.add).then_inc(acc_ok, 1)
                    wait(dve, acc_ok, 2, 9 * 2 + 2 + q, G)
                    ya = some(m_s["ya"].rearrange("p t n -> p n t"), 2, 1, G, q).rearrange("p n t -> p t n")
                    dve.tensor_scalar(ya, ys[q], m_s["gn"][:, q:q + 1], None, ALU.mult).then_inc(ya_ok, 1)

            first, last = (0, None), (GROUPS - 1, None)
            conv_vectors(first)
            scan_vectors(first)
            for c in range(4):
                convolve(c, first)
            ssd_states(first)
            with dve.Fori(0, GROUPS - 1) as g:
                G, N = (0, g), (1, g)
                own.enter(g, 3 + 4 * (TAPS - 1) + 2 + 7 + 6 + 4 + 3)
                conv_vectors(N)
                for k in range(4):
                    decays(k, G)
                    gates(S_STEPS[k][1], G)
                    convolve(k, N)
                    masked(k, G)
                scan_vectors(N)
                gates(S_STEPS[4][1], G)
                weighted(G)
                ssd_states(N)
                own.leave(GROUPS - 1)
            for k in range(5):
                decays(k, last)
                gates(S_STEPS[k][1], last)
                masked(k, last)
            weighted(last)

            def low_parts(m, src, base):
                for t in range(KT):
                    dve.wait_ge(pa_hi, base + t + 1)
                    dve.tensor_tensor(m["lo"][:, t, :], src[:, t, :], m["hi"][:, t, :].bitcast(F32), ALU.subtract).then_inc(pa_lo, 1)

            low_parts(m_a, m_s["ya"], 0)
            dve.wait_ge(rs_ok, 3)
            with dve.Fori(0, KT // 2) as i:
                own.enter(i, 2)
                for c in range(2):
                    j = J_PA + 2 + c
                    dve.wait_ge(slot_free[j % 2], lin(j // 2, 2, i))
                    one(dve.tensor_tensor(gate[c], gate[c], rs[:, N_META:], ALU.mult))
                    dve.wait_ge(dense_done, lin(j + 1, 4, i))
                    dve.wait_ge(pm_out[c], lin(0, 16, i))
                    dve.tensor_tensor(prod[c], gate[c], slot[j % 2][:, PC + N_META:], ALU.mult).then_inc(slot_free[j % 2], 1)
                own.leave(KT // 2)

            q_, k_, b_, s_ = m_h["q"], m_h["k"], m_h["b"], m_h["s"]
            main = lambda v: v[:, N_META:N_META + NX].rearrange("p (c t) -> p c t", t=64)
            dve.wait_ge(dense_done, J_HG)
            for v in (m_h["reset"][:, :],):
                one(dve.memset(v, 1.0))
            own.add(dve.memset(m_h["reset"][:, 0:1], 0.0))
            one(dve.memset(m_h["reset"][:, N_META::64], 0.0))
            for v in m_h["am"]:
                for d in range(2):
                    own.add(dve.memset(v[d][:, :], 0.0))
            own.wait()

            def of(j, i):
                return slice(j, j + 1) if i is None else bass.ds(i * 2 + j, 1)

            def hg_gates(j, d, i=None):
                jj, f, c0 = J_HG + 5 * j + d, s_[j % 2][d], N_META * d
                if j or d:
                    dve.wait_ge(k_ok, lin(2 * (2 * j + d), 8, i))
                own.add(dve.tensor_copy(m_h["lo"][:, d, 0:1], oml[:, d, of(j, i)]))
                own.add(dve.tensor_copy(m_h["lo"][:, d, 1:2], lb[:, d, of(j, i)]))
                own.wait()
                dve.wait_ge(slot_free[jj % 2], lin(jj // 2 + 1, 5, i))
                one(dve.tensor_scalar(f[:, c0:], f[:, c0:], m_h["lo"][:, d, 0:1], m_h["lo"][:, d, 1:2], ALU.mult, ALU.add))
                dve.tensor_scalar(k_[:, c0:], f[:, c0:], -1.0, 1.0, ALU.mult, ALU.add).then_inc(f_ok, 1)

            def hg_sums(j, d, i=None):
                w = lambda sem_, v, n: dve.wait_ge(sem_, lin(v, 2 * n, i))
                f = s_[j % 2][d]
                w(ln_ok, 2 * j + d + 1, 2)
                if d == 0:
                    o, r, l = b_[:, :], m_h["reset"][:, 0:NT], f[:, :]
                else:
                    o, r, l = b_[:, N_META:][:, ::-1], m_h["reset"][:, N_META + 1:][:, ::-1], f[:, N_META:][:, ::-1]
                dve.tensor_tensor_scan(o, r, l, 0.0, ALU.mult, ALU.add).then_inc(bc_ok, 1)
                w(bc_ok, 2 * j + d + 1, 2)
                if j or d:
                    w(e_ok, 4 * (2 * j + d) - 1, 8)
                mid, end = (32, 63) if d == 0 else (31, 0)
                dve.tensor_tensor(main(dif), main(b_), main(b_)[:, :, mid:mid + 1].broadcast_to([P, 2 * NC, 64]),
                                  ALU.subtract).then_inc(d_ok, 1)
                if d == 0:
                    own.add(dve.tensor_tensor(f[:, 0:N_META], b_[:, N_META - 1:N_META].broadcast_to([P, N_META]), b_[:, 0:N_META],
                                              ALU.subtract))
                dve.tensor_tensor(main(f), main(b_)[:, :, end:end + 1].broadcast_to([P, 2 * NC, 64]), main(b_),
                                  ALU.subtract).then_inc(d_ok, 1)

            def hg_keys(j, d, i=None):
                w = lambda sem_, v, n: dve.wait_ge(sem_, lin(v, 2 * n, i))
                c0, end = N_META * d, 63 if d == 0 else 0
                w(e_ok, 4 * (2 * j + d) + 1, 8)
                if j:
                    w(kv_ok, len(H_UPD) * j, len(H_UPD))
                dve.tensor_copy(m_h["dec"][d][:, :], main(q_[d][0])[:, :, end]).then_inc(dec_ok, 1)
                w(e_ok, 4 * (2 * j + d) + 3, 8)
                w(f_ok, 2 * j + d + 1, 2)
                dve.tensor_tensor(q_[d][2][:, N_META:], q_[d][2][:, N_META:], k_[:, N_META:], ALU.mult).then_inc(k_ok, 1)
                w(e_ok, 4 * (2 * j + d) + 4, 8)
                dve.tensor_tensor(q_[d][3][:, c0:], q_[d][3][:, c0:], k_[:, c0:], ALU.mult).then_inc(k_ok, 1)

            def hg_states(j, first, last, i=None):
                w = lambda sem_, v, n: dve.wait_ge(sem_, lin(v, 2 * n, i))
                U, prev, dec = len(H_UPD), m_h["prev"], m_h["dec"]
                w(dec_ok, 2 * (j + 1), 2)
                if j:
                    w(o_mm, NC * j, NC)
                for u, q, (d, c) in ((u, q, v) for u in range(first, last) for q, v in enumerate(H_BANKS[u])):
                    up = aux[u % 4][:, P * q:P * (q + 1)]
                    w(kv_mm, len(H_BANKS) * j + u + 1, len(H_BANKS))
                    if c < 0:
                        own.add(dve.tensor_copy(prev[0][:, 0, :], up))
                        ins = dve.tensor_copy(prev[0][:, 2 * CP, :], up)
                    elif d == 1 and c in (2 * CP - 1, 2 * NC - 1):
                        ins = dve.tensor_copy(prev[1][:, c - 1, :], up)
                    else:
                        before = (0, -1) if d == 0 and c in (0, 2 * CP) else (d, c - 1 if d == 0 else c + 1)
                        w(kv_ok, U * j + H_UPD.index(before) + 1, U)
                        ins = dve.scalar_tensor_tensor(prev[d][:, c + 1 if d == 0 else c - 1, :], prev[d][:, c, :], dec[d][:, c:c + 1], up,
                                                       ALU.mult, ALU.add)
                    ins.then_inc(kv_ok, 1)

            def hg_masks(j, i=None):
                w = lambda sem_, v, n: dve.wait_ge(sem_, lin(v, 2 * n, i))
                own.wait()
                for p in range(NC):
                    w(a_mm, NC * j + p + 1, NC)
                    if p >= 2:
                        w(o_mm, NC * j + p - 1, NC)
                    own.add(dve.tensor_copy(m_h["turn"][:, p:p + 1], ones[:, 0:1]))
                    for d in range(2):
                        dve.copy_predicated(m_h["am"][p % 2][d][:, :], incl64[d][:, :].bitcast(I32),
                                            aux[1 - p % 2][:, P * d:P * (d + 1)]).then_inc(am_ok, 1)

            def hg_out(j, i=None):
                if j:
                    dve.wait_ge(yb_ok, lin(j, 2, i))
                own.add(dve.tensor_copy(m_h["nw"][:, :], norm_w["hg"][:, of(j, i)]))
                own.wait()
                dve.wait_ge(ors_ok, lin(j + 1, 2, i))
                yj = m_h["yb"][:, j, :] if i is None else m_h["yb"][:, bass.ds(i * 2 + j, 1), :]
                one(dve.scalar_tensor_tensor(yj, aux2[1][:, PC + N_META:], m_h["nw"][:, 0:1], osq, ALU.mult, ALU.mult))
                jj = J_HG + 5 * j + 4
                dve.wait_ge(slot_free[jj % 2], lin(jj // 2 + 1, 5, i))
                dve.tensor_tensor(yj, yj, hg[j % 2], ALU.mult).then_inc(yb_ok, 1)

            def hg_step(j, i=None, scan=True):
                hg_gates(j + 1, 0, i)
                hg_sums(j + 1, 0, i)
                if scan:
                    hg_states(j, 0, len(H_BANKS), i)
                    hg_masks(j, i)
                hg_keys(j + 1, 0, i)
                hg_gates(j + 1, 1, i)
                if scan:
                    hg_out(j, i)
                hg_sums(j + 1, 1, i)
                hg_keys(j + 1, 1, i)

            hg_step(-1, scan=False)
            with dve.Fori(0, HH // 2 - 1) as i:
                own.enter(i, 2 * (4 + 2 + 1 + 3 + NC))
                hg_step(0, i)
                hg_step(1, i)
                own.leave(HH // 2 - 1)
            hg_step(HH - 2)
            hg_states(HH - 1, 0, len(H_BANKS))
            hg_masks(HH - 1)
            hg_out(HH - 1)

            low_parts(m_b, m_h["yb"], KT)
            with dve.Fori(0, KT // 2) as i:
                for c in range(2):
                    j = J_PB + 2 + c
                    dve.wait_ge(slot_free[j % 2], lin(j // 2, 2, i))
                    dve.wait_ge(dense_done, lin(j + 1, 4, i))
                    dve.wait_ge(ml_ok, lin(c, 2, i))
                    dve.tensor_tensor(prod[c], gate[c], slot[j % 2][:, PC + N_META:], ALU.mult).then_inc(slot_free[j % 2], 1)
                    dve.wait_ge(slot_free[j % 2], lin(j // 2 + 1, 2, i))
                    dve.wait_ge(m_in[c], lin(16, 16, i))
                    dve.tensor_tensor(prod[c], prod[c], back[c], ALU.add).then_inc(mg_ok, 1)
                    dve.wait_ge(mg_ok, lin(c + 1, 2, i))
                    dve.wait_ge(mh_ok, lin(c + 1, 2, i))
                    t = bass.ds(i * 2 + c, 1)
                    dve.tensor_tensor(m_b["ml"][:, t, :], prod[c], m_b["mh"][:, t, :].bitcast(F32), ALU.subtract).then_inc(ml_ok, 1)
            clear_sum(3, (mg_ok, KT))
            dve.wait_ge(spill_in, 16)
            down(f2, N_META, J_WO, 3, True, 1.0)
            normed(f2["h"], "ffn2", 3, 2, N_META)
            ffn(J_FF2, f2, N_META, 4, D_FF // P)
            dve.wait_ge(rs_ok, 5)
            for t in range(KT):
                h = f2["h"][:, t, N_META:]
                dve.scalar_tensor_tensor(h, h, norm_w["final"][:, t:t + 1], rs[:, N_META:], ALU.mult, ALU.mult).then_inc(tmp_ok, 1)
            for c in range(0, NC, 2):
                dve.wait_ge(out_mm, c + 1)
                if c >= 2:
                    dve.wait_ge(out_done[c % 2], 16 * (c // 2))
                dve.tensor_copy(f2["io"][c % 2][:, :], out_ps[c % 4][:, :]).then_inc(out_ok[0], 1)

        @block.gpsimd
        def _(pool):
            own = Tally(pool, pool_step)

            def low(s, n=0, i=None):
                pool.wait_ge(w_hi, lin(s + 1, n, i))
                pool.tensor_tensor(wlo[s % 2][:, :, :], raw[s % 2][:, :, :], whi[s % 2][:, :, :].bitcast(F32), ALU.subtract).then_inc(w_lo, 1)

            pool.memset(ident[:, :], 0.0)
            pool.memset(ones[:, :], 1.0)
            pool.memset(eps[:, :], EPS)
            own.add(pool.memset(incl[0][:, :], 1.0))
            own.wait()
            sel = lambda out, fill, op, mult, step, base: own.add(pool.affine_select(
                out=out, in_=out, compare_op=op, fill=fill, base=base, pattern=[[step, P]], channel_multiplier=mult))
            own.wait()
            sel(ident[:, :], 1.0, ALU.not_equal, 1, -1, 0)
            for d in range(2):
                sg = 1 - 2 * d
                src = ones[:, :]
                own.add(pool.affine_select(out=strict[d][:, :], in_=src, compare_op=ALU.is_gt, fill=0.0, base=0,
                                           pattern=[[-sg, P]], channel_multiplier=sg))
                own.add(pool.affine_select(out=incl[d][:, :], in_=src, compare_op=ALU.is_ge, fill=0.0, base=0,
                                           pattern=[[sg, P]], channel_multiplier=-sg))
                own.add(pool.affine_select(out=incl64[d][:, :], in_=src, compare_op=ALU.is_ge, fill=0.0, base=0,
                                           pattern=[[sg, P]], channel_multiplier=-sg))
            own.wait()
            own.add(pool.memset(incl64[0][0:64, 64:P], 0.0))
            own.add(pool.memset(incl64[1][64:P, 0:64], 0.0))
            own.wait()
            pool.memset(eps[:, :], EPS).then_inc(const_ok, 1)

            def lows(s, count):
                with pool.Fori(0, count // 2) as i:
                    low(s, 2, i)
                    low(s + 1, 2, i)
                if count % 2:
                    low(s + count - 1)

            def normed(q, c0):
                for t in range(0, KT, 2):
                    pool.wait_ge(xh_ok, KT * q + t + 1)
                    pool.tensor_tensor(xl[:, t, c0:], nb[t % 4][:, c0:], xh[:, t, c0:].bitcast(F32), ALU.subtract).then_inc(xn_ok[0], 1)

            low(0)
            normed(0, 0)
            lows(1, J_DT)
            for b in range(2):
                pool.wait_ge(slot_free[(J_DT - 1 - b) % 2], (J_DT - 1 - b) // 2 + 1)
            pool.dma_start(h_spill, f1["h"][:, :, N_META:]).then_inc(spill_out, 16)
            normed(1, 0)
            low(J_DT + 1)

            h4 = lambda v: v.rearrange("p (h q) -> p h q", h=HPG)

            def ssd_weighted(G):
                wait(pool, gat_ok, 2, 2, G)
                wait(pool, up_mm, len(S_UPD) // 2, 0, G)
                for n, (d, c) in enumerate(S_UPD):
                    q, k, m = (c - META, N_META, META) if c >= META else (c + 2, P, c)
                    wait(pool, tr_ok, NC + 2, NC + 2 if n >= 4 else q + 1, G)
                    pool.tensor_tensor(h4(xws[n][0:k, :]), h4(m_s["xbt"][0:k, q, 0:2 * P]),
                                       m_s["gw_t"][0:k, m, d, :].unsqueeze(2).broadcast_to([k, HPG, PD]), ALU.mult).then_inc(xw_ok, 1)

            def decays(k, G):
                for u in S_STEPS[k][0]:
                    c, d = S_UNITS[u]
                    wait(pool, gat_ok, 2, 2, G)
                    wait(pool, seg_mm, 2 * NC, max(u - 2, 0), G)
                    pool.tensor_tensor(m_s["rl"][u % 3][:, :, :], incl[d][:, :].unsqueeze(1).broadcast_to([P, HPG, P]),
                                       m_s["gal"][:, c, d, :].unsqueeze(2).broadcast_to([P, HPG, P]), ALU.mult).then_inc(rl_ok, 1)

            def steps(k, G):
                for u in S_STEPS[k][0]:
                    c, d = S_UNITS[u]
                    wait(pool, y_mm, 4, Y_STEP[c - 2] if c >= 2 else 0, G)
                    pool.tensor_tensor(h4(m_s["xdt"][c % 2][d][:, :]), h4(m_s["xbt"][:, c + 2, 0:2 * P]),
                                       m_s["gdt"][:, c, d, :].unsqueeze(2).broadcast_to([P, HPG, PD]), ALU.mult).then_inc(xdt_ok, 1)

            def ssd_low(c, G):
                low(J_SSD + 6 * G[0] + c + 1, 6, G[1])

            for c in range(5):
                ssd_low(c, (0, None))
            ssd_weighted((0, None))
            ssd_low(5, (0, None))
            with pool.Fori(0, GROUPS - 1) as g:
                G, N = (0, g), (1, g)
                decays(0, G)
                for k in range(4):
                    ssd_low(k, N)
                    steps(k, G)
                    if k < 3:
                        decays(k + 1, G)
                ssd_low(4, N)
                ssd_weighted(N)
                ssd_low(5, N)
            last = (GROUPS - 1, None)
            for k in range(4):
                decays(k, last)
                if k == 1:
                    low(J_PA + 1)
                steps(k, last)
            low(J_PA + 2)

            def store_pair(i=None):
                low(J_PA + 3, 4, i)
                low(J_PA + 4, 4, i)
                for c in range(2):
                    j = J_PA + 2 + c
                    pool.wait_ge(slot_free[j % 2], lin(j // 2 + 1, 2, i))
                    dst = m_spill[c:c + 1] if i is None else m_spill[bass.ds(i * 2 + c, 1)]
                    pool.dma_start(dst.rearrange("a p n -> p (a n)"), prod[c]).then_inc(pm_out[c], 16)

            store_pair()
            with pool.Fori(1, KT // 2) as i:
                low(J_PA + 1, 4, i)
                low(J_PA + 2, 4, i)
                store_pair(i)

            def hg_queries(j, d, i=None):
                a = j % 2
                w = lambda sem_, v, n: pool.wait_ge(sem_, lin(v, 2 * n, i))
                w(dec_ok, 2 * j + d + 1, 2)
                w(e_ok, 4 * (2 * j + d) + 2, 8)
                jj = J_HG + 5 * j + 3
                pool.wait_ge(slot_free[jj % 2], lin(jj // 2 + 1, 5, i))
                for c in range(2):
                    v = m_h["q"][d][c][:, N_META:]
                    pool.tensor_tensor(v, v, hq[a], ALU.mult).then_inc(q_ok, 1)

            def hg_step(j, i=None):
                for c in range(4):
                    low(J_HG + 5 * (j + 1) + c + 1, 10, i)
                hg_queries(j + 1, 0, i)
                low(J_HG + 5 * (j + 2), 10, i)
                hg_queries(j + 1, 1, i)

            hg_step(-1)
            with pool.Fori(0, HH // 2 - 1) as i:
                hg_step(0, i)
                hg_step(1, i)
            hg_step(HH - 2)

            with pool.Fori(0, KT // 2) as i:
                low(J_PB + 1, 4, i)
                low(J_PB + 2, 4, i)
                pool.wait_ge(mg_ok, lin(0, 2, i))
                pool.wait_ge(yb_ok, HH)
                for b in range(2):
                    pool.dma_start(back[b], m_spill[bass.ds(i * 2 + b, 1)].rearrange("a p n -> p (a n)")).then_inc(m_in[b], 16)
                low(J_PB + 3, 4, i)
                low(J_PB + 4, 4, i)
            pool.wait_ge(dense_done, J_WO)
            pool.dma_start(f2["h"][:, :, N_META:], h_spill).then_inc(spill_in, 16)
            lows(J_WO + 1, KT)
            normed(2, N_META)
            lows(J_FF2 + 1, FFN_JOBS - 1)


_INS = ["x_prompt", "x_sample", "meta_tokens", "ffn1_norm", "ffn1_w_gate_up", "ffn1_w_down", "mix_norm", "w_in",
        "ssd_conv_w", "ssd_conv_b", "ssd_dt_bias", "ssd_a_log", "ssd_d", "ssd_norm", "ssd_w_proj", "hg_lb_table",
        "hg_norm", "hg_w_proj", "w_out", "ffn2_norm", "ffn2_w_gate_up", "ffn2_w_down", "final_norm"]
_OUTS = [(1, 256, 1024), (1, 512, 1024)]


def kernel(**inputs):
    import numpy as _np
    import concourse.bacc as _bacc
    from concourse import mybir as _mybir
    from concourse.bass_utils import run_bass_kernel_spmd as _run

    nc = _bacc.Bacc("TRN2", target_bir_lowering=False, num_devices=1)
    arrays, args = {}, []
    for name in _INS:
        a = _np.ascontiguousarray(inputs[name])
        arrays[f"in_{name}"] = a
        args.append(nc.dram_tensor(f"in_{name}", a.shape, _mybir.dt.from_np(a.dtype), kind="ExternalInput").ap())
    for n, shape in enumerate(_OUTS):
        args.append(nc.dram_tensor(f"out_{n}", shape, _mybir.dt.float32, kind="ExternalOutput").ap())
    build(nc, *args)
    r = _run(nc, [arrays], core_ids=[0])
    return tuple(_np.asarray(r.results[0][f"out_{n}"]) for n in range(len(_OUTS)))
```
